# Optimizing a Trainium2 kernel written in Bass

```python
import jax, jax.numpy as jnp
from jax import lax
import numpy as np

D_MODEL = 1024
BATCH = 1
SEQ = 512
DEPTH = 1

N_HEADS = 8
N_KV_HEADS = 2
HEAD_DIM = 64
GQA_GROUP = N_HEADS // N_KV_HEADS
ATTN_DIM = N_HEADS * HEAD_DIM
KV_DIM = N_KV_HEADS * HEAD_DIM
WINDOW = 128
ATTN_BLOCK = 128
ROT_DIM = HEAD_DIM // 4
ROPE_THETA = 500000.0
CONV_DIM = D_MODEL // 2
CONV_WIDTH = 3
SPLIT_SIZES = (ATTN_DIM, KV_DIM, KV_DIM, CONV_DIM, CONV_DIM, CONV_DIM, D_MODEL, D_MODEL)
PROJ_WIDTH = sum(SPLIT_SIZES)
SPLIT_POINTS = tuple(int(v) for v in np.cumsum(SPLIT_SIZES)[:-1])
N_GROUPS = 4
EXPERTS_PER_GROUP = 8
N_EXPERTS = N_GROUPS * EXPERTS_PER_GROUP
TOP_K = 2
D_FF_EXPERT = D_MODEL // 4
MOE_BLOCK = 128
NORM_EPS = 1e-6
MASK_VALUE = -1e30


def rmsnorm(x, g):
    xf = x.astype(jnp.float32)
    xf = xf * lax.rsqrt(jnp.mean(xf * xf, axis=-1, keepdims=True) + NORM_EPS)
    return xf.astype(x.dtype) * g

def rope_tables(seq_len):
    inv_freq = ROPE_THETA ** (-jnp.arange(0, ROT_DIM, 2, dtype=jnp.float32) / ROT_DIM)
    ang = jnp.arange(seq_len, dtype=jnp.float32)[:, None] * inv_freq[None, :]
    return jnp.cos(ang), jnp.sin(ang)

def partial_rope(x, cos, sin):
    half = ROT_DIM // 2
    c = cos[None, :, None, :].astype(x.dtype)
    s = sin[None, :, None, :].astype(x.dtype)
    x1 = x[..., :half]
    x2 = x[..., half:ROT_DIM]
    return jnp.concatenate([x1 * c - x2 * s, x2 * c + x1 * s, x[..., ROT_DIM:]], axis=-1)

def band_keys(t):
    b, s, hk, hd = t.shape
    nb = s // ATTN_BLOCK
    tp = jnp.pad(t, ((0, 0), (WINDOW, WINDOW), (0, 0), (0, 0))).reshape(b, nb + 2, ATTN_BLOCK, hk, hd)
    return jnp.concatenate([tp[:, :-2], tp[:, 1:-1], tp[:, 2:]], axis=2)

def windowed_gqa(q, k, v, sink):
    b, s, _, hd = q.shape
    nb = s // ATTN_BLOCK
    qb = q.reshape(b, nb, ATTN_BLOCK, N_KV_HEADS, GQA_GROUP, hd)
    kw = band_keys(k)
    vw = band_keys(v)
    scores = jnp.einsum('bnqhgd,bnkhd->bnhgqk', qb, kw,
                        preferred_element_type=jnp.float32) * (HEAD_DIM ** -0.5)
    blk = jnp.arange(nb)[:, None, None] * ATTN_BLOCK
    qpos = blk + jnp.arange(ATTN_BLOCK)[None, :, None]
    kpos = blk - WINDOW + jnp.arange(3 * ATTN_BLOCK)[None, None, :]
    valid = (jnp.abs(qpos - kpos) <= WINDOW) & (kpos >= 0) & (kpos < s)
    scores = jnp.where(valid[None, :, None, None], scores, MASK_VALUE)
    sink_b = sink.astype(jnp.float32).reshape(1, 1, N_KV_HEADS, GQA_GROUP, 1, 1)
    m = jnp.maximum(jnp.max(scores, axis=-1, keepdims=True), sink_b)
    e = jnp.exp(scores - m)
    p = e / (jnp.sum(e, axis=-1, keepdims=True) + jnp.exp(sink_b - m))
    o = jnp.einsum('bnhgqk,bnkhd->bnqhgd', p.astype(v.dtype), vw)
    return o.reshape(b, s, N_HEADS * hd)

def short_gated_conv(gate_b, gate_c, xc, conv_w, conv_b):
    u = gate_c * xc
    up = jnp.pad(u, ((0, 0), (1, 1), (0, 0)))
    conv = up[:, :-2] * conv_w[0] + up[:, 1:-1] * conv_w[1] + up[:, 2:] * conv_w[2] + conv_b
    return gate_b * conv

def hierarchical_moe(h, w_rg, b_rg, w_re, b_re, w_gate, w_up, w_down):
    b, s, d = h.shape
    t = b * s
    hf = h.reshape(t, d)
    hf32 = hf.astype(jnp.float32)
    g_logits = hf32 @ w_rg.astype(jnp.float32) + b_rg.astype(jnp.float32)
    grp = jnp.argmax(g_logits, axis=-1)
    p_grp = jnp.take_along_axis(jax.nn.softmax(g_logits, axis=-1), grp[:, None], axis=-1)
    e_logits = (hf32 @ w_re.astype(jnp.float32) + b_re.astype(jnp.float32)).reshape(t, N_GROUPS, EXPERTS_PER_GROUP)
    e_in = jnp.take_along_axis(e_logits, grp[:, None, None], axis=1)[:, 0]
    top_p, top_i = lax.top_k(jax.nn.softmax(e_in, axis=-1), TOP_K)
    top_p = top_p / jnp.sum(top_p, axis=-1, keepdims=True)
    gates = (p_grp * top_p).reshape(t * TOP_K)
    expert = (grp[:, None] * EXPERTS_PER_GROUP + top_i).reshape(t * TOP_K)
    n_assign = t * TOP_K
    order = jnp.argsort(expert)
    e_sorted = expert[order]
    tok = order // TOP_K
    counts = jnp.bincount(expert, length=N_EXPERTS)
    starts = jnp.cumsum(counts) - counts
    padded = ((counts + MOE_BLOCK - 1) // MOE_BLOCK) * MOE_BLOCK
    pad_ends = jnp.cumsum(padded)
    pad_starts = pad_ends - padded
    dest = pad_starts[e_sorted] + (jnp.arange(n_assign) - starts[e_sorted])
    n_rows = n_assign + N_EXPERTS * MOE_BLOCK
    n_blocks = n_rows // MOE_BLOCK
    x_pad = jnp.zeros((n_rows, d), h.dtype).at[dest].set(hf[tok])
    block_e = jnp.minimum(jnp.searchsorted(pad_ends, jnp.arange(n_blocks) * MOE_BLOCK, side='right'),
                          N_EXPERTS - 1)

    def expert_block(args):
        xb, e = args
        hid = jax.nn.silu(xb @ w_gate[e]) * (xb @ w_up[e])
        return hid @ w_down[e]

    y_pad = lax.map(expert_block, (x_pad.reshape(n_blocks, MOE_BLOCK, d), block_e)).reshape(n_rows, d)
    y = y_pad[dest] * gates[order][:, None].astype(h.dtype)
    out = jnp.zeros((t, d), h.dtype).at[tok].add(y)
    return out.reshape(b, s, d)

def first_inputs(seed: int = 0) -> dict:
    key = jax.random.key(seed)
    ks = jax.random.split(key, 20)
    f32 = jnp.float32

    def nrm(k, shape, fan_in):
        return jax.random.normal(k, shape, f32) * (fan_in ** -0.5)

    def gain(k, shape):
        return 1.0 + 0.02 * jax.random.normal(k, shape, f32)

    return {
        "x": jax.random.normal(ks[0], (BATCH, SEQ, D_MODEL), f32),
        "norm1_g": gain(ks[1], (DEPTH, D_MODEL)),
        "w_in": nrm(ks[2], (DEPTH, D_MODEL, PROJ_WIDTH), D_MODEL),
        "q_norm_g": gain(ks[3], (DEPTH, HEAD_DIM)),
        "k_norm_g": gain(ks[4], (DEPTH, HEAD_DIM)),
        "attn_sink": 0.5 * jax.random.normal(ks[5], (DEPTH, N_HEADS), f32),
        "conv_w": nrm(ks[6], (DEPTH, CONV_WIDTH, CONV_DIM), CONV_WIDTH),
        "conv_b": 0.02 * jax.random.normal(ks[7], (DEPTH, CONV_DIM), f32),
        "w_attn_proj": nrm(ks[8], (DEPTH, ATTN_DIM, D_MODEL), ATTN_DIM),
        "w_conv_proj": nrm(ks[9], (DEPTH, CONV_DIM, D_MODEL), CONV_DIM),
        "w_out": nrm(ks[10], (DEPTH, D_MODEL, D_MODEL), D_MODEL),
        "norm2_g": gain(ks[11], (DEPTH, D_MODEL)),
        "w_router_group": nrm(ks[12], (DEPTH, D_MODEL, N_GROUPS), D_MODEL),
        "b_router_group": 0.01 * jax.random.normal(ks[13], (DEPTH, N_GROUPS), f32),
        "w_router_expert": nrm(ks[14], (DEPTH, D_MODEL, N_EXPERTS), D_MODEL),
        "b_router_expert": 0.01 * jax.random.normal(ks[15], (DEPTH, N_EXPERTS), f32),
        "w_gate_e": nrm(ks[16], (DEPTH, N_EXPERTS, D_MODEL, D_FF_EXPERT), D_MODEL),
        "w_up_e": nrm(ks[17], (DEPTH, N_EXPERTS, D_MODEL, D_FF_EXPERT), D_MODEL),
        "w_down_e": nrm(ks[18], (DEPTH, N_EXPERTS, D_FF_EXPERT, D_MODEL), D_FF_EXPERT),
    }

def first_block(x, norm1_g, w_in, q_norm_g, k_norm_g, attn_sink, conv_w, conv_b,
              w_attn_proj, w_conv_proj, w_out, norm2_g, w_router_group, b_router_group,
              w_router_expert, b_router_expert, w_gate_e, w_up_e, w_down_e):
    b, s, _ = x.shape
    cos, sin = rope_tables(s)
    for l in range(DEPTH):
        h = rmsnorm(x, norm1_g[l])
        proj = h @ w_in[l]
        q, k, v, cb, cc, cx, g_attn, g_conv = jnp.split(proj, SPLIT_POINTS, axis=-1)
        q = rmsnorm(q.reshape(b, s, N_HEADS, HEAD_DIM), q_norm_g[l])
        k = rmsnorm(k.reshape(b, s, N_KV_HEADS, HEAD_DIM), k_norm_g[l])
        v = v.reshape(b, s, N_KV_HEADS, HEAD_DIM)
        q = partial_rope(q, cos, sin)
        k = partial_rope(k, cos, sin)
        attn = windowed_gqa(q, k, v, attn_sink[l])
        conv = short_gated_conv(cb, cc, cx, conv_w[l], conv_b[l])
        merged = (jax.nn.sigmoid(g_attn) * (attn @ w_attn_proj[l])
                  + jax.nn.sigmoid(g_conv) * (conv @ w_conv_proj[l]))
        x = x + merged @ w_out[l]
        h2 = rmsnorm(x, norm2_g[l])
        x = x + hierarchical_moe(h2, w_router_group[l], b_router_group[l],
                                 w_router_expert[l], b_router_expert[l],
                                 w_gate_e[l], w_up_e[l], w_down_e[l])
    return x


DEPTH_2 = 2

ROPE_DIM = HEAD_DIM // 4
Q_BLOCK = 128
D_FF = 4 * D_MODEL

A_HEADS = 8
A_NOPE = HEAD_DIM - ROPE_DIM
A_KV_RANK = 256
IDX_HEADS = 8
IDX_DIM = 64
TOPK_MAX = 256
B_HEADS = 8
C_HEADS = 16
C_KV_GROUPS = 2
C_HPG = C_HEADS // C_KV_GROUPS
CMP_LEN = 32
CMP_STRIDE = 16
CMP_HIDDEN = 2 * HEAD_DIM
SEL_LEN = 64
SEL_N_MAX = 16
WINDOW_2 = 512
N_BRANCH = 3
FORCE_SCORE = 1e4

AB_WIDTHS = (A_HEADS * HEAD_DIM, A_KV_RANK, ROPE_DIM, IDX_HEADS * IDX_DIM, IDX_DIM, IDX_HEADS,
             B_HEADS * HEAD_DIM, B_HEADS * HEAD_DIM, B_HEADS * HEAD_DIM, B_HEADS)
AB_IN = sum(AB_WIDTHS)
C_WIDTHS = (C_HEADS * HEAD_DIM,) + (C_KV_GROUPS * HEAD_DIM,) * 6 + (C_HEADS * N_BRANCH,)
C_IN = sum(C_WIDTHS)
MIX_WIDTH_AB = (A_HEADS + B_HEADS) * HEAD_DIM
MIX_WIDTH_C = C_HEADS * HEAD_DIM
N_EVEN = (DEPTH_2 + 1) // 2
N_ODD = DEPTH_2 // 2


def rms_norm(x, g):
    xf = x.astype(jnp.float32)
    y = xf * lax.rsqrt(jnp.mean(xf * xf, axis=-1, keepdims=True) + NORM_EPS)
    return (y * g.astype(jnp.float32)).astype(x.dtype)

def rope_tables_2(seq):
    pos = jnp.arange(seq, dtype=jnp.float32)
    inv = ROPE_THETA ** (-jnp.arange(0, ROPE_DIM, 2, dtype=jnp.float32) / ROPE_DIM)
    ang = pos[:, None] * inv[None, :]
    return jnp.cos(ang), jnp.sin(ang)

def partial_rope_2(x, cos, sin):
    half = ROPE_DIM // 2
    shp = (1, x.shape[1]) + (1,) * (x.ndim - 3) + (half,)
    c = cos.reshape(shp).astype(x.dtype)
    s = sin.reshape(shp).astype(x.dtype)
    x1, x2, rest = x[..., :half], x[..., half:ROPE_DIM], x[..., ROPE_DIM:]
    return jnp.concatenate([x1 * c - x2 * s, x2 * c + x1 * s, rest], axis=-1)

def masked_softmax(s, mask):
    s = jnp.where(mask, s.astype(jnp.float32), -jnp.inf)
    m = jnp.max(s, axis=-1, keepdims=True)
    m = jnp.where(jnp.isfinite(m), m, 0.0)
    e = jnp.where(mask, jnp.exp(s - m), 0.0)
    return e / jnp.maximum(jnp.sum(e, axis=-1, keepdims=True), 1e-30)

def split_cols(y, widths):
    points, acc = [], 0
    for w in widths[:-1]:
        acc += w
        points.append(acc)
    return jnp.split(y, points, axis=-1)

def to_blocks(a):
    b, s = a.shape[:2]
    return jnp.moveaxis(a.reshape((b, s // Q_BLOCK, Q_BLOCK) + a.shape[2:]), 1, 0)

def from_blocks(a):
    n, b, q = a.shape[:3]
    return jnp.moveaxis(a, 0, 1).reshape((b, n * q) + a.shape[3:])

def dsa_mixer(q, ckv, k_rope, q_idx, k_idx, w_idx, w_uk, w_uv):
    b, s = ckv.shape[:2]
    n_keep = min(TOPK_MAX, s // 4)
    scale = HEAD_DIM ** -0.5
    q_abs = jnp.einsum('bshe,rhe->bshr', q[..., ROPE_DIM:], w_uk)
    q_rot = q[..., :ROPE_DIM]
    w_idx = w_idx * (IDX_HEADS ** -0.5 * IDX_DIM ** -0.5)
    gather = jax.vmap(lambda table, ix: table[ix])
    key_pos = jnp.arange(s)

    def block(args):
        i, qa, qr, qi, wi = args
        t = i * Q_BLOCK + jnp.arange(Q_BLOCK)
        causal = key_pos[None, :] <= t[:, None]
        rel = jax.nn.relu(jnp.einsum('bqhd,bsd->bqhs', qi, k_idx))
        score = jnp.einsum('bqhs,bqh->bqs', rel, wi).astype(jnp.float32)
        score = jnp.where(causal[None], score, -jnp.inf)
        _, idx = lax.top_k(score, n_keep)
        valid = idx <= t[None, :, None]
        c_sel = gather(ckv, idx)
        kr_sel = gather(k_rope, idx)
        logits = (jnp.einsum('bqhr,bqkr->bqhk', qa, c_sel)
                  + jnp.einsum('bqhe,bqke->bqhk', qr, kr_sel)) * scale
        p = masked_softmax(logits, valid[:, :, None, :]).astype(c_sel.dtype)
        return jnp.einsum('bqhk,bqkr->bqhr', p, c_sel)

    nblk = s // Q_BLOCK
    o_lat = from_blocks(lax.map(block, (jnp.arange(nblk), to_blocks(q_abs), to_blocks(q_rot),
                                        to_blocks(q_idx), to_blocks(w_idx))))
    return jnp.einsum('bshr,rhd->bshd', o_lat, w_uv)

def fox_mixer(q, k, v, f_logit):
    b, s = q.shape[:2]
    scale = HEAD_DIM ** -0.5
    cum = lax.cumsum(jax.nn.log_sigmoid(f_logit.astype(jnp.float32)), axis=1)
    cum_k = jnp.transpose(cum, (0, 2, 1))
    key_pos = jnp.arange(s)

    def block(args):
        i, qb, cq = args
        t = i * Q_BLOCK + jnp.arange(Q_BLOCK)
        causal = key_pos[None, :] <= t[:, None]
        logits = (jnp.einsum('bqhd,bshd->bhqs', qb, k).astype(jnp.float32) * scale
                  + jnp.transpose(cq, (0, 2, 1))[..., None] - cum_k[:, :, None, :])
        p = masked_softmax(logits, causal[None, None]).astype(v.dtype)
        return jnp.einsum('bhqs,bshd->bqhd', p, v)

    nblk = s // Q_BLOCK
    return from_blocks(lax.map(block, (jnp.arange(nblk), to_blocks(q), to_blocks(cum))))

def nsa_mixer(q, k_cmp, v_cmp, k_sel, v_sel, k_win, v_win, gate_logit,
              pe_k, pe_v, wk1, wk2, wv1, wv2):
    b, s = q.shape[:2]
    g, d = C_KV_GROUPS, HEAD_DIM
    scale = d ** -0.5
    n_cmp = (s - CMP_LEN) // CMP_STRIDE + 1
    n_selb = s // SEL_LEN
    n_keep = min(SEL_N_MAX, n_selb)
    tok = np.arange(n_cmp)[:, None] * CMP_STRIDE + np.arange(CMP_LEN)[None, :]

    def compress(x, pe, w1, w2):
        xb = x[:, tok] + pe[None, None, :, None, :]
        xb = jnp.transpose(xb, (0, 1, 3, 2, 4)).reshape(b, n_cmp, g, CMP_LEN * d)
        return jax.nn.gelu(xb @ w1) @ w2

    kc = compress(k_cmp, pe_k, wk1, wk2)
    vc = compress(v_cmp, pe_v, wv1, wv2)
    cmp_end = jnp.asarray(tok[:, -1])
    sel_start = np.arange(n_selb) * SEL_LEN
    overlap = ((tok[:, 0][None, :] <= sel_start[:, None] + SEL_LEN - 1)
               & (tok[:, -1][None, :] >= sel_start[:, None]))
    overlap = jnp.asarray(overlap, jnp.float32)
    ks_blk = jnp.transpose(k_sel.reshape(b, n_selb, SEL_LEN, g, d), (0, 3, 1, 2, 4))
    vs_blk = jnp.transpose(v_sel.reshape(b, n_selb, SEL_LEN, g, d), (0, 3, 1, 2, 4))
    kw_pad = jnp.pad(k_win, ((0, 0), (WINDOW_2, 0), (0, 0), (0, 0)))
    vw_pad = jnp.pad(v_win, ((0, 0), (WINDOW_2, 0), (0, 0), (0, 0)))
    gather2 = jax.vmap(jax.vmap(lambda table, ix: table[ix]))
    qg = q.reshape(b, s, g, C_HPG, d)
    gates = jax.nn.sigmoid(gate_logit.astype(jnp.float32)).reshape(b, s, g, C_HPG, N_BRANCH)
    blk_ids = jnp.arange(n_selb)

    def block(args):
        i, qb, gb = args
        t = i * Q_BLOCK + jnp.arange(Q_BLOCK)
        s_c = jnp.einsum('bqghd,bngd->bghqn', qb, kc) * scale
        p_c = masked_softmax(s_c, cmp_end[None, :] <= t[:, None])
        o_c = jnp.einsum('bghqn,bngd->bqghd', p_c.astype(vc.dtype), vc)
        imp = jnp.einsum('bghqn,jn->bgqj', p_c, overlap)
        cur = t // SEL_LEN
        forced = ((blk_ids[None, :] == 0) | (blk_ids[None, :] == cur[:, None])
                  | (blk_ids[None, :] == cur[:, None] - 1))
        imp = jnp.where(forced, FORCE_SCORE, imp)
        imp = jnp.where(blk_ids[None, :] * SEL_LEN <= t[:, None], imp, -jnp.inf)
        _, idx = lax.top_k(imp, n_keep)
        k_g = gather2(ks_blk, idx).reshape(b, g, Q_BLOCK, n_keep * SEL_LEN, d)
        v_g = gather2(vs_blk, idx).reshape(b, g, Q_BLOCK, n_keep * SEL_LEN, d)
        tok_pos = (idx[..., None] * SEL_LEN + jnp.arange(SEL_LEN)).reshape(b, g, Q_BLOCK, n_keep * SEL_LEN)
        valid_s = tok_pos <= t[None, None, :, None]
        s_s = jnp.einsum('bqghd,bgqkd->bghqk', qb, k_g) * scale
        p_s = masked_softmax(s_s, valid_s[:, :, None]).astype(v_g.dtype)
        o_s = jnp.einsum('bghqk,bgqkd->bqghd', p_s, v_g)
        start = i * Q_BLOCK
        kw = lax.dynamic_slice_in_dim(kw_pad, start, Q_BLOCK + WINDOW_2, axis=1)
        vw = lax.dynamic_slice_in_dim(vw_pad, start, Q_BLOCK + WINDOW_2, axis=1)
        pos = start - WINDOW_2 + jnp.arange(Q_BLOCK + WINDOW_2)
        valid_w = ((pos[None, :] >= 0) & (pos[None, :] <= t[:, None])
                   & (pos[None, :] > t[:, None] - WINDOW_2))
        s_w = jnp.einsum('bqghd,bkgd->bghqk', qb, kw) * scale
        p_w = masked_softmax(s_w, valid_w).astype(vw.dtype)
        o_w = jnp.einsum('bghqk,bkgd->bqghd', p_w, vw)
        out = gb[..., 0:1] * o_c + gb[..., 1:2] * o_s + gb[..., 2:3] * o_w
        return out.astype(qb.dtype)

    nblk = s // Q_BLOCK
    o = from_blocks(lax.map(block, (jnp.arange(nblk), to_blocks(qg), to_blocks(gates))))
    return o.reshape(b, s, C_HEADS * d)

def ab_layer(u, w_in, b_forget, kv_norm, w_uk, w_uv, kidx_norm, w_out, cos, sin):
    b, s, _ = u.shape
    aq, ackv, akr, aqi, aki, awi, bq, bk, bv, bf = split_cols(u @ w_in, AB_WIDTHS)
    aq = partial_rope_2(aq.reshape(b, s, A_HEADS, HEAD_DIM), cos, sin)
    ackv = rms_norm(ackv, kv_norm)
    akr = partial_rope_2(akr, cos, sin)
    aqi = partial_rope_2(aqi.reshape(b, s, IDX_HEADS, IDX_DIM), cos, sin)
    aki = partial_rope_2(rms_norm(aki, kidx_norm), cos, sin)
    o_a = dsa_mixer(aq, ackv, akr, aqi, aki, awi, w_uk, w_uv)
    o_b = fox_mixer(bq.reshape(b, s, B_HEADS, HEAD_DIM), bk.reshape(b, s, B_HEADS, HEAD_DIM),
                    bv.reshape(b, s, B_HEADS, HEAD_DIM), bf + b_forget)
    o = jnp.concatenate([o_a.reshape(b, s, -1), o_b.reshape(b, s, -1)], axis=-1)
    return o @ w_out

def c_layer(u, w_in, b_gate, pe_k, pe_v, wk1, wk2, wv1, wv2, w_out, cos, sin):
    b, s, _ = u.shape
    q, kc, vc, ks, vs, kw, vw, gl = split_cols(u @ w_in, C_WIDTHS)
    kv = lambda a: a.reshape(b, s, C_KV_GROUPS, HEAD_DIM)
    q = partial_rope_2(q.reshape(b, s, C_HEADS, HEAD_DIM), cos, sin)
    kc = partial_rope_2(kv(kc), cos, sin)
    ks = partial_rope_2(kv(ks), cos, sin)
    kw = partial_rope_2(kv(kw), cos, sin)
    o = nsa_mixer(q, kc, kv(vc), ks, kv(vs), kw, kv(vw), gl + b_gate, pe_k, pe_v, wk1, wk2, wv1, wv2)
    return o @ w_out

def sqrelu_mlp(u, w1, w2):
    return jnp.square(jax.nn.relu(u @ w1)) @ w2

def second_inputs(seed: int = 0) -> dict:
    key = jax.random.key(seed)
    ks = jax.random.split(key, 22)
    nrm = lambda k, shape, fan: jax.random.normal(k, shape, jnp.float32) * (fan ** -0.5)
    gain = lambda k, shape: 1.0 + 0.02 * jax.random.normal(k, shape, jnp.float32)
    return {
        "x": jax.random.normal(ks[0], (BATCH, SEQ, D_MODEL), jnp.float32),
        "attn_norm": gain(ks[1], (DEPTH_2, D_MODEL)),
        "mlp_norm": gain(ks[2], (DEPTH_2, D_MODEL)),
        "mlp_w1": nrm(ks[3], (DEPTH_2, D_MODEL, D_FF), D_MODEL),
        "mlp_w2": nrm(ks[4], (DEPTH_2, D_FF, D_MODEL), D_FF),
        "ab_w_in": nrm(ks[5], (N_EVEN, D_MODEL, AB_IN), D_MODEL),
        "ab_b_forget": jax.random.uniform(ks[6], (N_EVEN, B_HEADS), jnp.float32, 1.0, 6.0),
        "a_kv_norm": gain(ks[7], (N_EVEN, A_KV_RANK)),
        "a_w_uk": nrm(ks[8], (N_EVEN, A_KV_RANK, A_HEADS, A_NOPE), A_KV_RANK),
        "a_w_uv": nrm(ks[9], (N_EVEN, A_KV_RANK, A_HEADS, HEAD_DIM), A_KV_RANK),
        "a_kidx_norm": gain(ks[10], (N_EVEN, IDX_DIM)),
        "ab_w_out": nrm(ks[11], (N_EVEN, MIX_WIDTH_AB, D_MODEL), MIX_WIDTH_AB),
        "c_w_in": nrm(ks[12], (N_ODD, D_MODEL, C_IN), D_MODEL),
        "c_b_gate": 0.1 * jax.random.normal(ks[13], (N_ODD, C_HEADS * N_BRANCH), jnp.float32),
        "c_pe_k": 0.02 * jax.random.normal(ks[14], (N_ODD, CMP_LEN, HEAD_DIM), jnp.float32),
        "c_pe_v": 0.02 * jax.random.normal(ks[15], (N_ODD, CMP_LEN, HEAD_DIM), jnp.float32),
        "c_cmp_k_w1": nrm(ks[16], (N_ODD, CMP_LEN * HEAD_DIM, CMP_HIDDEN), CMP_LEN * HEAD_DIM),
        "c_cmp_k_w2": nrm(ks[17], (N_ODD, CMP_HIDDEN, HEAD_DIM), CMP_HIDDEN),
        "c_cmp_v_w1": nrm(ks[18], (N_ODD, CMP_LEN * HEAD_DIM, CMP_HIDDEN), CMP_LEN * HEAD_DIM),
        "c_cmp_v_w2": nrm(ks[19], (N_ODD, CMP_HIDDEN, HEAD_DIM), CMP_HIDDEN),
        "c_w_out": nrm(ks[20], (N_ODD, MIX_WIDTH_C, D_MODEL), MIX_WIDTH_C),
        "final_norm": gain(ks[21], (D_MODEL,)),
    }

def second_block(x, attn_norm, mlp_norm, mlp_w1, mlp_w2, ab_w_in, ab_b_forget, a_kv_norm, a_w_uk,
              a_w_uv, a_kidx_norm, ab_w_out, c_w_in, c_b_gate, c_pe_k, c_pe_v, c_cmp_k_w1,
              c_cmp_k_w2, c_cmp_v_w1, c_cmp_v_w2, c_w_out, final_norm):
    cos, sin = rope_tables_2(x.shape[1])
    h = x
    for layer in range(DEPTH_2):
        u = rms_norm(h, attn_norm[layer])
        if layer % 2 == 0:
            j = layer // 2
            h = h + ab_layer(u, ab_w_in[j], ab_b_forget[j], a_kv_norm[j], a_w_uk[j], a_w_uv[j],
                             a_kidx_norm[j], ab_w_out[j], cos, sin)
        else:
            j = layer // 2
            h = h + c_layer(u, c_w_in[j], c_b_gate[j], c_pe_k[j], c_pe_v[j], c_cmp_k_w1[j],
                            c_cmp_k_w2[j], c_cmp_v_w1[j], c_cmp_v_w2[j], c_w_out[j], cos, sin)
        h = h + sqrelu_mlp(rms_norm(h, mlp_norm[layer]), mlp_w1[layer], mlp_w2[layer])
    return rms_norm(h, final_norm)


def setup_inputs(seed=0):
    out = dict(first_inputs(seed))
    for name, value in second_inputs(seed + 1).items():
        if name != "x":
            out[name + "_2"] = value
    return out


def reference(
    x, norm1_g, w_in, q_norm_g, k_norm_g, attn_sink, conv_w, conv_b, w_attn_proj, w_conv_proj,
    w_out, norm2_g, w_router_group, b_router_group, w_router_expert, b_router_expert, w_gate_e,
    w_up_e, w_down_e, attn_norm_2, mlp_norm_2, mlp_w1_2, mlp_w2_2, ab_w_in_2, ab_b_forget_2,
    a_kv_norm_2, a_w_uk_2, a_w_uv_2, a_kidx_norm_2, ab_w_out_2, c_w_in_2, c_b_gate_2, c_pe_k_2,
    c_pe_v_2, c_cmp_k_w1_2, c_cmp_k_w2_2, c_cmp_v_w1_2, c_cmp_v_w2_2, c_w_out_2, final_norm_2,
):
    x = first_block(
        x, norm1_g, w_in, q_norm_g, k_norm_g, attn_sink, conv_w, conv_b, w_attn_proj,
        w_conv_proj, w_out, norm2_g, w_router_group, b_router_group, w_router_expert,
        b_router_expert, w_gate_e, w_up_e, w_down_e,
    )
    return second_block(
        x, attn_norm_2, mlp_norm_2, mlp_w1_2, mlp_w2_2, ab_w_in_2, ab_b_forget_2, a_kv_norm_2,
        a_w_uk_2, a_w_uv_2, a_kidx_norm_2, ab_w_out_2, c_w_in_2, c_b_gate_2, c_pe_k_2, c_pe_v_2,
        c_cmp_k_w1_2, c_cmp_k_w2_2, c_cmp_v_w1_2, c_cmp_v_w2_2, c_w_out_2, final_norm_2,
    )


_drawn_inputs = setup_inputs


def setup_inputs(seed=0):
    import zlib

    import numpy as np

    out = dict(_drawn_inputs(seed))
    spreads = {}
    factors = {'q_norm_g': 6.533,
     'k_norm_g': 6.849,
     'attn_sink': 8.0,
     'b_router_group': 7.468,
     'b_router_expert': 4.617,
     'attn_norm_2': 3.842,
     'a_kv_norm_2': 8.0,
     'a_kidx_norm_2': 6.146,
     'c_b_gate_2': 18.426,
     'c_pe_k_2': 134.875,
     'c_pe_v_2': 188.552,
     'final_norm_2': 22.824,
     'mlp_norm_2': 4.717}
    for name, (base, spread) in spreads.items():
        noise = np.random.default_rng([zlib.crc32(name.encode()), seed]).standard_normal(out[name].shape)
        drawn = base * np.exp(spread * noise) if base else spread * noise
        out[name] = __import__('jax').numpy.asarray(drawn.astype(out[name].dtype))
    for name, factor in factors.items():
        out[name] = (out[name] * factor).astype(out[name].dtype)
    return out
```

```python
import concourse.bass as bass
from concourse import mybir
from concourse.alu_op_type import AluOpType as ALU
from contextlib import ExitStack
import numpy as np

F32 = mybir.dt.float32
I32 = mybir.dt.int32
ACT = mybir.ActivationFunctionType
X = mybir.AxisListType.X

P = 128
T = 512
NT = T // P
D = 1024
KD = D // P
HD = 64
ROT = 8
EPS = 1e-6
NEG = -1e30
SCALE = HD ** -0.5
E = 32
G = 4
EG = E // G
F_E = 256
SPILL = 7
NB = E + SPILL
TABW = 40
F = 4096
NF = F // P
N_CMP = 31
CMP_LEN, CMP_STRIDE = 32, 16
KEEP = 128
RING = 3
BIG = 18000
SLOT = 4096
GELU_C = float((2 / np.pi) ** 0.5)
TAKEN = -3e38

CONST = {}
_at = 0
for _n, _w in (("ident", P), ("before", P), ("upto", T), ("band", 3 * P), ("causal", T), ("cmp", NT * 32),
               ("cmpok", NT), ("cos", NT * ROT), ("sin", NT * ROT), ("iota", E), ("token", NT)):
    CONST[_n] = (_at, _at + _w)
    _at += _w
NCONST = _at

GAINS = {"norm1_g": 0, "norm2_g": 8, "attn0": 16, "mlp0": 24, "attn1": 32, "mlp1": 40}
NORMS = tuple(GAINS)
CONVW, CONVB = 48, 60

PAR = {}
_at = 0
for _n, _w in (("qk_gain", 640), ("router_b", 36), ("final", D), ("sink", 8), ("forget_b", 8), ("ckv_gain", 256),
               ("kidx_gain", 64), ("gate_b", 48), ("router_w", KD * 36), ("cmp_w2", 2 * HD)):
    PAR[_n] = (_at, _at + _w)
    _at += _w
NPAR = _at


def constants():
    c = np.zeros((P, NCONST), np.float32)
    p, j = np.arange(P)[:, None], np.arange(P)[None, :]

    def put(name, a):
        c[:, CONST[name][0]:CONST[name][1]] = a

    put("ident", p == j)
    put("before", p < j)
    put("upto", np.concatenate([p <= j, np.ones((P, T - P), bool)], 1))
    band = np.zeros((P, 3 * P), np.float32)
    band[:, :P] = np.where(j >= p, 0, NEG)
    band[:, 2 * P:] = np.where(j <= p, 0, NEG)
    put("band", band)
    put("causal", np.concatenate([np.zeros((P, T - P)), np.where(j <= p, 0, NEG)], 1))
    t = (np.arange(NT)[None, :] * P + p)
    n = np.arange(32)
    ok = (n[None, None, :] * CMP_STRIDE + CMP_LEN - 1 <= t[:, :, None]) & (n < N_CMP)[None, None, :]
    put("cmp", np.where(ok, 0, NEG).reshape(P, -1))
    put("cmpok", t >= CMP_LEN - 1)
    inv = np.float32(500000.0) ** (-np.arange(0, 2 * ROT, 2, dtype=np.float32) / np.float32(2 * ROT))
    ang = t.astype(np.float32)[:, :, None] * inv.astype(np.float32)[None, None, :]
    put("cos", np.cos(ang).reshape(P, -1))
    put("sin", np.sin(ang).reshape(P, -1))
    put("iota", np.arange(E)[None, :] - 64.0 + 0 * p)
    put("token", t)
    return c


JOBS = {}
_at = 0
for _n, _w in (("vec", 1),
               ("norm0", KD), ("q", NT), ("kv", NT), ("cc", 4), ("cx", 4), ("cb", 4), ("ga", KD), ("gc", KD),
               ("turn_q", 5), ("turn_o0", 4), ("merge", 2 * KD), ("wo", 2 * NT),
               ("norm1", KD), ("logits", 1), ("ranks", 1), ("moe", 2 + 6 * (NB - 1) + 4),
               ("norm2", KD), ("ai", NT), ("ax", NT), ("aq", NT), ("bv", NT), ("turn_small", 4), ("turn_uk", 2),
               ("turn_qi", 4), ("forget", 1), ("index", 8 * (NT - 1)), ("bq", 4), ("bk", 4), ("turn_aq", 4),
               ("latent", 8 * 2 + 8 * NT), ("turn_o1", KD), ("ao", 2 * NT),
               ("norm3", KD), ("up0", NF),
               ("norm4", KD), ("nk", NT), ("nv", NT), ("nq", 2 * NT), ("turn_nq", 8), ("turn_nk", 4), ("cmp", 7),
               ("turn_o2", KD), ("no", 2 * NT),
               ("norm5", KD), ("up1", NF)):
    JOBS[_n] = _at
    _at += _w


def latent_order():
    order = []
    for r in range(-2, 8 * NT + 4):
        if r + 2 < 8 * NT and (r + 2) % NT == 0:
            order += [("up", (r + 2) // NT, 0), ("up", (r + 2) // NT, 1)]
        if r >= 4:
            order.append(("out", r - 4))
    return order


LATENT = {key: JOBS["latent"] + n for n, key in enumerate(latent_order())}


def moe_job(b, what):
    if what == "turn" and b == 0:
        return JOBS["moe"]
    after = 2 if b < NB - 1 else 0
    return JOBS["moe"] + 2 + 6 * b + {"turn": -5, "gate": 0, "hid": 1 + after, "down": 2 + after}[what]


def weight_plan(w):
    plan = []

    def kview(a):
        return a.rearrange("(k p) n -> p k n", p=P)

    def cols(name, a, c0, c1, last):
        plan.append((name, [(0, KD * (c1 - c0), c1 - c0, 0, c1 - c0, kview(a)[:, :, c0:c1])], last))

    def whole(name, src, last):
        plan.append((name, [(0, SLOT, SLOT // src.shape[1], 0, SLOT // src.shape[1], src)], last))

    w_in = w["w_in"][0]
    for name, c0, c1, last in (("q", 0, 512, "q+3"), ("kv", 512, 768, "kv+3"), ("cc", 1280, 1792, "cc+3"),
                               ("cx", 1792, 2304, "cx+3"), ("cb", 768, 1280, "cb+3"),
                               ("ga0", 2304, 2816, "ga+3"), ("ga1", 2816, 3328, "ga+7"),
                               ("gc0", 3328, 3840, "gc+3"), ("gc1", 3840, 4352, "gc+7")):
        cols(name, w_in, c0, c1, last)
    whole("ap", kview(w["w_attn_proj"][0]), "merge+14")
    whole("cp", kview(w["w_conv_proj"][0]), "merge+15")
    for c in range(2):
        cols(f"wo{c}", w["w_out"][0], c * 512, c * 512 + 512, f"wo+{4 * c + 3}")
    plan.append(("experts", None, None))
    ab = w["ab_w_in_2"][0]
    cols("ai", ab, 784, 1296, "ai+3")
    plan.append(("ax", [(0, KD * 352, 352, o, o + c1 - c0, kview(ab)[:, :, c0:c1])
                        for o, c0, c1 in ((0, 512, 784), (272, 1296, 1368), (344, 2904, 2912))], "ax+3"))
    cols("aq", ab, 0, 512, "aq+3")
    cols("bv", ab, 2392, 2904, "bv+3")
    cols("bq", ab, 1368, 1880, "bq+3")
    cols("bk", ab, 1880, 2392, "bk+3")
    for c in range(2):
        cols(f"ao{c}", w["ab_w_out_2"][0], c * 512, c * 512 + 512, f"ao+{4 * c + 3}")

    def mlp(l):
        for i in range(8):
            cols(f"up{l}{i}", w["mlp_w1_2"][l], i * 512, (i + 1) * 512, f"up{l}+{4 * i + 3}")
        down = kview(w["mlp_w2_2"][l])
        for c in range(2):
            for q in range(4):
                whole(f"down{l}{c}{q}", down[:, q * 8:(q + 1) * 8, c * 512:(c + 1) * 512], ("down", l, c, q))

    mlp(0)
    cw = w["c_w_in_2"][0]
    for name, c0, c1, last in (("nk", 1024, 1536, "nk+3"), ("nv", 1536, 1840, "nv+3"), ("nq0", 0, 512, "nq+3"),
                               ("nq1", 512, 1024, "nq+7")):
        cols(name, cw, c0, c1, last)
    for n, kind in enumerate("kv"):
        a = w[f"c_cmp_{kind}_w1_2"][0].rearrange("(o d) n -> d o n", d=HD)
        plan.append((f"w1{kind}", [("half", 0, a), ("half", HD, a)], f"cmp+{2 * n + 2}"))
    for c in range(2):
        cols(f"no{c}", w["c_w_out_2"][0], c * 512, c * 512 + 512, f"no+{4 * c + 3}")
    mlp(1)
    return plan


def build(nc, w, out):
    ctx = ExitStack()
    with ctx:
        def sb(name, shape, dt=F32):
            return ctx.enter_context(nc.sbuf_tensor(name, shape, dt))

        def sem(name):
            return ctx.enter_context(nc.semaphore(name))

        rows_dram = nc.dram_tensor("rows_dram", [T, D], F32, kind="Internal").ap()
        y_dram = nc.dram_tensor("y_dram", [NB * P, D], F32, kind="Internal").ap()
        tab_dram = nc.dram_tensor("tab_dram", [P * TABW, 1], I32, kind="Internal").ap()

        x = sb("x", [P, NT, D])
        hT = sb("hT", [P, KD, T])
        tok = sb("tok", [P, NT, D])
        ring = sb("ring", [P, RING, SLOT])
        big = sb("big", [P, BIG])
        scr = sb("scr", [P, 7, T])
        const = sb("const", [P, NCONST])
        par = sb("par", [P, NPAR])
        vec_rows = sb("vec_rows", [64, P])
        vec = sb("vec", [P, 64])
        pe_rows = sb("pe_rows", [32, P])
        stat = sb("stat", [P, 3, 256])
        small = sb("small", [P, 512])
        psA = [ctx.enter_context(nc.psum_tensor(f"psA{i}", [P, 512], F32)) for i in range(2)]
        psS = [ctx.enter_context(nc.psum_tensor(f"psS{i}", [P, 512], F32)) for i in range(2)]
        psT = [ctx.enter_context(nc.psum_tensor(f"psT{i}", [P, 512], F32)) for i in range(2)]
        psO = [ctx.enter_context(nc.psum_tensor(f"psO{i}", [P, 512], F32)) for i in range(2)]

        def cst(name):
            return const[:, CONST[name][0]:CONST[name][1]]

        def prm(name):
            return par[:, PAR[name][0]:PAR[name][1]]

        ident = cst("ident")
        upto = cst("upto")
        ones = upto[:, P:2 * P]
        before = cst("before")
        iota = cst("iota")
        cos4 = cst("cos").rearrange("p (t c) -> p t c", c=ROT)
        sin4 = cst("sin").rearrange("p (t c) -> p t c", c=ROT)
        negm, sums, fac = stat[:, 0, :], stat[:, 1, :], stat[:, 2, :]

        def carve(sizes):
            at, got = 0, {}
            for name, n in sizes:
                got[name] = big[:, at:at + n]
                at += n
            assert at <= BIG, at
            return got

        a1 = carve((("qk", 2560), ("v", 512), ("qT", 2048), ("kT", 512), ("u", 2056), ("conv", 2048),
                    ("ga", 4096), ("gc", 4096)))
        qk = a1["qk"].rearrange("p (t n) -> p t n", t=NT)
        v1 = a1["v"].rearrange("p (t n) -> p t n", t=NT)
        qT1 = a1["qT"].rearrange("p (j n) -> p j n", j=4)
        kT1 = a1["kT"]
        u = a1["u"].rearrange("p (m n) -> p m n", m=4)
        conv = a1["conv"].rearrange("p (m n) -> p m n", m=4)
        ga = a1["ga"].rearrange("p (m n) -> p m n", m=KD)
        gc = a1["gc"].rearrange("p (m n) -> p m n", m=KD)
        attnT = a1["qk"][:, 0:2048].rearrange("p (c n) -> p c n", c=4)
        a2 = carve((("logit", 144), ("w1", 512), ("w2", 512), ("w3", 512), ("oh1", 128), ("oh2", 128), ("asg", 128),
                    ("rank", 128), ("cnt", 32), ("spill", 32), ("incl", 32), ("obase", 32), ("s", 256), ("xg", 2048),
                    ("xT", 2048), ("sg", 512), ("hid", 512), ("hidT", 512), ("y", 2048), ("ya", 2048), ("yb", 2048)))
        a3 = carve((("bv", 2048), ("bqT", 2048), ("bkT", 2048), ("aqT", 2048), ("kiT", 512), ("krT", 512),
                    ("ckvT", 1024), ("ckv", 1024), ("wb", 64), ("sel", 1152), ("qabs", 2048), ("olat", 512),
                    ("wukT", 1024), ("wuv", 1024), ("ncum", 512), ("sp", 96)))
        a4 = carve((("qT", 4096), ("kv", 3072), ("kT4", 2048), ("gate", 192), ("kcT", 32), ("vcBD", 512),
                    ("hid", 512), ("peT", 32), ("cmpst", 512)))
        hid = big[:, 0:NF * T].rearrange("p (f n) -> p f n", f=NF)

        x_loaded = sem("x_loaded")
        const_loaded = sem("const_loaded")
        w_arrived = [sem(f"w_arrived{i}") for i in range(RING)]
        proj_ready = sem("proj_ready")
        proj_evacuated = [sem(f"proj_evacuated{i}") for i in range(2)]
        sumsq_ready = sem("sumsq_ready")
        mean_ready = sem("mean_ready")
        root_ready = sem("root_ready")
        rstd_ready = sem("rstd_ready")
        normed = sem("normed")
        head_mean = sem("head_mean")
        head_root = sem("head_root")
        heads_ready = sem("heads_ready")
        scores_ready = sem("scores_ready")
        masked = sem("masked")
        probs_ready = sem("probs_ready")
        turned = sem("turned")
        turned_copied = [sem(f"turned_copied{i}") for i in range(2)]
        values_ready = sem("values_ready")
        factor_ready = sem("factor_ready")
        out_taken = [sem(f"out_taken{i}") for i in range(2)]
        acc_ready = sem("acc_ready")
        acc_taken = sem("acc_taken")
        logits_shifted = sem("logits_shifted")
        logits_exp = sem("logits_exp")
        assigned = sem("assigned")
        slots_ready = sem("slots_ready")
        table_zeroed = sem("table_zeroed")
        zeros_made = sem("zeros_made")
        rows_stored = sem("rows_stored")
        scattered = sem("scattered")
        table_loaded = sem("table_loaded")
        gathered = [sem(f"gathered{i}") for i in range(2)]
        silu_ready = sem("silu_ready")
        y_written = [sem(f"y_written{i}") for i in range(2)]
        picked = [sem(f"picked{i}") for i in range(2)]
        combined = sem("combined")
        forget_z = sem("forget_z")
        forget_ln = sem("forget_ln")
        relu_used = sem("relu_used")
        gate_ready = sem("gate_ready")
        gelu_in = sem("gelu_in")
        gelu_sig = sem("gelu_sig")
        gelu_out = sem("gelu_out")
        final_ready = sem("final_ready")
        stored = sem("stored")
        down_used = sem("down_used")
        merged = sem("merged")
        gu_arrived = [sem(f"gu_arrived{i}") for i in range(2)]
        dn_arrived = [sem(f"dn_arrived{i}") for i in range(2)]
        hidden_part = sem("hidden_part")
        latent_zeroed = sem("latent_zeroed")
        latent_weights = sem("latent_weights")
        cmp_zeroed = sem("cmp_zeroed")
        dve_chain = sem("dve_chain")
        act_chain = sem("act_chain")

        block = ctx.enter_context(nc.Block())

        items = []

        band, causal = cst("band"), cst("causal")
        for j in range(4):
            for g in range(2):
                for t in range(NT):
                    lo, hi = max(0, t - 1), min(NT - 1, t + 1)
                    n = (hi - lo + 1) * P
                    items.append(dict(kind="band", head=4 * g + j, t=t, n=n, blocks=list(range(lo, hi + 1)),
                                      mask=band[:, (lo - t + 1) * P:(lo - t + 1) * P + n],
                                      scores=[(qT1[64 * g:64 * g + 64, j, t * P:(t + 1) * P],
                                               kT1[64 * g:64 * g + 64, lo * P:lo * P + n])],
                                      values=v1[:, :, 64 * g:64 * g + 64]))
        n_band = len(items)

        bv = a3["bv"].rearrange("p (t n) -> p t n", t=NT)
        bqT = a3["bqT"].rearrange("p (j n) -> p j n", j=4)
        bkT = a3["bkT"].rearrange("p (j n) -> p j n", j=4)
        aqT = a3["aqT"].rearrange("p (j n) -> p j n", j=4)
        qiT = bqT
        ckvT = a3["ckvT"].rearrange("p (m n) -> p m n", m=2)
        ckv = a3["ckv"].rearrange("p (t n) -> p t n", t=NT)
        qabs = a3["qabs"].rearrange("p (b m n) -> p b m n", b=2, m=2)
        olat = a3["olat"].rearrange("p (b n) -> p b n", b=2)
        wukT = a3["wukT"].rearrange("p (j n) -> p j n", j=4)
        wuv = a3["wuv"].rearrange("p (m n) -> p m n", m=2)
        ncum = a3["ncum"]
        wb = a3["wb"].rearrange("p (t n) -> p t n", t=NT)
        sel = {1: a3["sel"][:, 0:256], 2: a3["sel"][:, 256:640], 3: a3["sel"][:, 640:1152]}

        def cmask(t):
            return causal[:, T - (t + 1) * P:T]

        for h in range(8):
            for t in range(NT):
                r = 64 * (h % 2)
                n = (t + 1) * P
                items.append(dict(kind="fox", head=8 + h, t=t, n=n, blocks=list(range(t + 1)), mask=cmask(t),
                                  scores=[(bqT[r:r + 64, h // 2, t * P:(t + 1) * P], bkT[r:r + 64, h // 2, 0:n]),
                                          (ident[0:8, h:h + 1].broadcast_to([8, P]), ncum[0:8, 0:n])],
                                  values=bv[:, :, 64 * h:64 * h + 64]))

        for h in range(8):
            for t in range(NT):
                r = 64 * (h % 2)
                n = (t + 1) * P
                items.append(dict(kind="latent", head=h, t=t, n=n, blocks=list(range(t + 1)),
                                  mask=cmask(t) if t == 0 else sel[t],
                                  scores=[(qabs[:, h % 2, m, t * P:(t + 1) * P], ckvT[:, m, 0:n]) for m in range(2)]
                                  + [(aqT[r:r + 64, h // 2, t * P:(t + 1) * P], a3["krT"][r:r + 64, 0:n])]))
        first_fox, first_latent, first_nsa = n_band, n_band + 8 * NT, n_band + 16 * NT

        qT2 = a4["qT"].rearrange("p (j n) -> p j n", j=8)
        kv2 = a4["kv"].rearrange("p (t n) -> p t n", t=NT)
        kT4 = a4["kT4"].rearrange("p (s n) -> p s n", s=4)
        gate2 = a4["gate"].rearrange("p (t n) -> p t n", t=NT)
        kcT = a4["kcT"]
        vcBD = a4["vcBD"].rearrange("p (g n) -> p g n", g=2)
        chid = a4["hid"].rearrange("p (s n) -> p s n", s=8)
        cmpmask = cst("cmp").rearrange("p (t n) -> p t n", t=NT)
        cmpok = cst("cmpok")
        cmpst = a4["cmpst"].rearrange("p (i n) -> p i n", n=8)
        for g in range(2):
            for t in range(NT):
                items.append(dict(kind="cmp", g=g, t=t, n=256, blocks=[0, 1], index=len(items) - first_nsa))
        first_pair = len(items)
        for h in range(16):
            g, j = h // 8, h % 8
            for branch in range(2):
                for t in range(NT):
                    n = (t + 1) * P
                    items.append(dict(kind="pair", head=h, branch=branch, t=t, n=n, blocks=list(range(t + 1)), mask=cmask(t),
                                      gate=gate2[:, t, h * 3 + 1 + branch:h * 3 + 2 + branch],
                                      scores=[(qT2[64 * g:64 * g + 64, j, t * P:(t + 1) * P],
                                               kT4[64 * g:64 * g + 64, 2 + branch, 0:n])],
                                      values=kv2[:, :, 64 * g + (640 if branch else 384):64 * g + (704 if branch else 448)]))
        n_items = len(items)
        starts_head = range(first_latent - 2, first_nsa - 2, NT)
        kiT, krT = a3["kiT"], a3["krT"]
        S, PR, PT = ([scr[:, i, :] for i in at] for at in ((0, 1), (2, 3, 4), (5, 6)))

        yrow = small[:, 0:8].bitcast(I32)
        trow = small[:, 8:16].bitcast(I32)
        spill_expert = small[:, 16:24].bitcast(I32)
        token_id = small[:, 24:28].bitcast(I32)
        slot_token = small[:, 32:32 + TABW].bitcast(I32)
        zeros_i = small[:, 80:80 + TABW].bitcast(I32)
        g12 = small[:, 120:128].rearrange("p (k t) -> p k t", k=2)
        ss = small[:, 128:160]
        rstd = small[:, 160:192]
        qss = small[:, 192:232]
        negsink = small[:, 240:248]
        esink = small[:, 256:288]
        xg = a2["xg"].rearrange("p (b n) -> p b n", b=2)
        xT = a2["xT"].rearrange("p (b k n) -> p b k n", b=2, k=KD)
        sg = a2["sg"].rearrange("p (b n) -> p b n", b=2)
        ehid = a2["hid"].rearrange("p (b n) -> p b n", b=2)
        ehidT = a2["hidT"].rearrange("p (b n) -> p b n", b=2)
        ey = a2["y"].rearrange("p (b n) -> p b n", b=2)
        ya = a2["ya"].rearrange("p (b n) -> p b n", b=2)
        yb = a2["yb"].rearrange("p (b n) -> p b n", b=2)
        krd = scr[:, 2, :].rearrange("p (t n) -> p t n", t=NT)
        kid = scr[:, 3, :].rearrange("p (t n) -> p t n", t=NT)
        wuk = qabs.rearrange("p b m n -> p (b m n)")[:, 0:1024].rearrange("p (m h d) -> p m h d", m=2, h=8)
        peT = a4["peT"]
        asg = a2["asg"].rearrange("p (t n) -> p t n", t=NT)
        gexp, pexp = a2["w1"][:, 32:48], a2["s"][:, 24:28]
        sp_terms = a3["sp"][:, 64:96].rearrange("p (t n) -> p t n", t=NT)

        def sp_part(k):
            return a3["sp"][:, 32 * k:32 * k + 32]

        def cpart(k):
            return a4["hid"][:, 128 * k:128 * k + 128]

        def rows(a):
            return a.rearrange("(k p) -> k p", p=P)

        def everywhere(a):
            return a.partition_broadcast(P)

        def heads(a, n):
            return a.unsqueeze(0).unsqueeze(0).broadcast_to([P, n, HD])

        qk_gain = prm("qk_gain").rearrange("p (h d) -> p h d", d=HD)
        router_w3 = prm("router_w").rearrange("p (k n) -> p k n", k=KD)
        loads = [(const[:, :], w["constants"]),
                 (vec_rows[0:8, :], rows(w["norm1_g"][0])), (vec_rows[8:16, :], rows(w["norm2_g"][0])),
                 (vec_rows[16:24, :], rows(w["attn_norm_2"][0])), (vec_rows[24:32, :], rows(w["mlp_norm_2"][0])),
                 (vec_rows[32:40, :], rows(w["attn_norm_2"][1])), (vec_rows[40:48, :], rows(w["mlp_norm_2"][1])),
                 (vec_rows[CONVB:CONVB + 4, :], rows(w["conv_b"][0])),
                 (pe_rows[:, 0:HD], w["c_pe_k_2"][0]), (pe_rows[:, HD:P], w["c_pe_v_2"][0]),
                 (qk_gain[:, 0:8, :], heads(w["q_norm_g"][0], 8)), (qk_gain[:, 8:10, :], heads(w["k_norm_g"][0], 2)),
                 (prm("router_b")[:, 0:G], everywhere(w["b_router_group"][0])),
                 (prm("router_b")[:, G:G + E], everywhere(w["b_router_expert"][0])),
                 (prm("final"), everywhere(w["final_norm_2"])), (prm("sink"), everywhere(w["attn_sink"][0])),
                 (prm("forget_b"), everywhere(w["ab_b_forget_2"][0])),
                 (prm("ckv_gain"), everywhere(w["a_kv_norm_2"][0])),
                 (prm("kidx_gain"), everywhere(w["a_kidx_norm_2"][0])), (prm("gate_b"), everywhere(w["c_b_gate_2"][0])),
                 (router_w3[:, :, 0:G], w["w_router_group"][0].rearrange("(k p) n -> p k n", p=P)),
                 (router_w3[:, :, G:G + E], w["w_router_expert"][0].rearrange("(k p) n -> p k n", p=P)),
                 (prm("cmp_w2")[:, 0:HD], w["c_cmp_k_w2_2"][0]), (prm("cmp_w2")[:, HD:2 * HD], w["c_cmp_v_w2_2"][0])]
        for j in range(3):
            loads.append((vec_rows[CONVW + 4 * j:CONVW + 4 * j + 4, :], rows(w["conv_w"][0][j])))
        CONST_LOADS = len(loads)

        plan = weight_plan(w)
        names = [name for name, _, _ in plan]
        experts_at = names.index("experts")
        in_ring = [n for n in names if n != "experts"]
        slot_of = {n: i % RING for i, n in enumerate(in_ring)}
        gu_slot = [experts_at % RING, (experts_at + 1) % RING]
        dn_slot = (experts_at + 2) % RING
        arrived_at, total = {}, [0] * RING
        for name, pieces, _ in plan:
            if name != "experts":
                total[slot_of[name]] += 16 * len(pieces)
                arrived_at[name] = total[slot_of[name]]

        def slot(name):
            return ring[:, slot_of[name], :]

        gu = [ring[:, i, :].rearrange("p (k n) -> p k n", k=KD) for i in gu_slot]
        dn = [ring[:, dn_slot, p * 2048:(p + 1) * 2048].rearrange("p (k n) -> p k n", k=2) for p in range(2)]

        def last_use(last):
            if isinstance(last, str):
                name, n = last.split("+")
                return proj_ready, JOBS[name] + int(n) + 1
            _, l, c, q = last
            return (down_used, 3 * (2 * l + c) + q + 1) if q < 3 else (acc_ready, 4 * (2 * l + c) + 4)

        def product(eng, n, i=0):
            eng.wait_ge(proj_ready, i * 12 + (n + 1))

        def copied(eng, n, i=0):
            eng.wait_ge(proj_evacuated[n % 2], i * 6 + (n // 2 + 1))

        def copied_all(eng, name, count):
            for n in range(max(0, count - 2), count):
                copied(eng, JOBS[name] + n)

        def bank(n):
            return psA[n % 2]

        def moe_pairs(eng, expert_block):
            for p in range(2):
                expert_block(p, 0)
            with eng.Fori(1, (NB - 1) // 2) as i:
                for p in range(2):
                    expert_block(p, i)
            expert_block(0, (NB - 1) // 2, last=True)

        def moe_products(p, i, last=False):
            n = JOBS["moe"] + 2 + 6 * p
            turns = JOBS["moe"] if isinstance(i, int) and 2 * i + p == 0 else n - 5
            after = 0 if last else 2
            return turns, n, n + 1 + after, n + 2 + after

        def first(i):
            return isinstance(i, int) and i == 0

        @block.sync
        def _(sp):
            sp.dma_start(x[:, :, :], w["x"][0].rearrange("(t p) d -> p t d", p=P)).then_inc(x_loaded, 16)
            held = {}

            def load_block(p, e):
                for o, a in ((0, w["w_gate_e"]), (F_E, w["w_up_e"])):
                    src = a[0][bass.ds(e, 1)].rearrange("e (k p) n -> p (e k) n", p=P)
                    sp.dma_start(gu[p][:, :, o:o + F_E], src).then_inc(gu_arrived[p], 16)

            def load_down(p, e):
                src = w["w_down_e"][0][bass.ds(e, 1)].rearrange("e (k p) n -> p (e k) n", p=P)
                sp.dma_start(dn[p], src).then_inc(dn_arrived[p], 16)

            def experts():
                for p in range(2):
                    sp.wait_ge(*held[gu_slot[p]])
                    load_block(p, p)
                sp.wait_ge(*held[dn_slot])
                for p in range(2):
                    load_down(p, p)
                with sp.Fori(1, E // 2) as i:
                    for p in range(2):
                        product(sp, moe_products(p, i)[1] - 12, i)
                        load_block(p, i * 2 + p)
                        product(sp, moe_products(p, i)[3] + 1 - 12, i)
                        load_down(p, i * 2 + p)
                sp.wait_ge(slots_ready, 1)
                for b in range(E, NB):
                    e = sp.value_load(spill_expert[0:1, b - E:b - E + 1], min_val=0, max_val=E - 1)
                    product(sp, moe_job(b - 2, "gate"))
                    load_block(b % 2, e)
                    product(sp, moe_job(b - 2, "down") + 1)
                    load_down(b % 2, e)
                held[gu_slot[(NB - 1) % 2]] = (proj_ready, moe_job(NB - 1, "gate") + 1)
                held[gu_slot[NB % 2]] = (proj_ready, moe_job(NB - 2, "gate") + 1)
                held[dn_slot] = (proj_ready, moe_job(NB - 1, "down") + 2)

            for name, pieces, last in plan:
                if name == "experts":
                    experts()
                    continue
                s = slot_of[name]
                if s in held:
                    sp.wait_ge(*held[s])
                for piece in pieces:
                    if piece[0] == "half":
                        _, p0, src = piece
                        dst = ring[p0:p0 + HD, s, :].rearrange("p (o n) -> p o n", n=P)
                    else:
                        first, words, width, c0, c1, src = piece
                        dst = ring[:, s, first:first + words].rearrange("p (k n) -> p k n", n=width)[:, :, c0:c1]
                    sp.dma_start(dst, src).then_inc(w_arrived[s], 16)
                held[s] = last_use(last)
            sp.wait_ge(final_ready, NT)
            sp.dma_start(out[0].rearrange("(t p) d -> p t d", p=P), tok[:, :, :]).then_inc(stored, 16)
            sp.wait_ge(stored, 16)

        @block.gpsimd
        def _(pool):
            nc.gpsimd.memset(zeros_i.bitcast(F32), 0.0).then_inc(zeros_made, 1)
            pool.wait_ge(zeros_made, 1)
            pool.dma_start(tab_dram.rearrange("(p n) o -> p (n o)", p=P), zeros_i).then_inc(table_zeroed, 16)
            pool.wait_ge(table_zeroed, 16)
            pool.wait_ge(slots_ready, 1)
            for c in range(2 * NT):
                pool.indirect_dma_start(tab_dram[:, :], bass.IndirectOffsetOnAxis(ap=trow[:, c:c + 1], axis=0),
                                        token_id[:, c % NT:c % NT + 1], None).then_inc(scattered, 16)
            pool.wait_ge(scattered, 2 * NT * 16)
            pool.dma_start(slot_token, tab_dram.rearrange("(p n) o -> p (n o)", p=P)).then_inc(table_loaded, 16)
            pool.wait_ge(table_loaded, 16)
            pool.wait_ge(rows_stored, 16)
            for b in range(NB):
                if b >= 2:
                    product(pool, moe_job(b - 2, "turn") + 1)
                pool.indirect_dma_start(xg[:, b % 2, :], None, rows_dram[:, :],
                                        bass.IndirectOffsetOnAxis(ap=slot_token[:, b:b + 1], axis=0))\
                    .then_inc(gathered[b % 2], 16)
            for p in range(2):
                pool.wait_ge(y_written[p], 16 * ((NB + 1 - p) // 2))
            for t in range(NT):
                if t >= 2:
                    pool.wait_ge(combined, t - 1)
                for k, buf in ((0, ya), (1, yb)):
                    c = k * NT + t
                    pool.indirect_dma_start(buf[:, t % 2, :], None, y_dram[:, :],
                                            bass.IndirectOffsetOnAxis(ap=yrow[:, c:c + 1], axis=0))\
                        .then_inc(picked[t % 2], 16)
            pool.wait_ge(combined, NT)
            nc.gpsimd.memset(wuk.rearrange("p m h d -> p (m h d)"), 0.0).then_inc(latent_zeroed, 1)
            nc.gpsimd.memset(scr[:, 2, :], 0.0).then_inc(latent_zeroed, 1)
            pool.wait_ge(latent_zeroed, 2)
            for m in range(2):
                pool.dma_start(wuk[:, m, :, 2 * ROT:HD], w["a_w_uk_2"][0][m * P:(m + 1) * P])\
                    .then_inc(latent_weights, 16)
            pool.dma_start(wuv[:, :, :], w["a_w_uv_2"][0].rearrange("(m p) h d -> p m (h d)", p=P))\
                .then_inc(latent_weights, 16)
            pool.wait_ge(acc_ready, 2 * NT)
            nc.gpsimd.memset(vcBD.rearrange("p g n -> p (g n)"), 0.0).then_inc(cmp_zeroed, 1)
            nc.gpsimd.memset(a4["hid"], 0.0).then_inc(cmp_zeroed, 1)

        @block.tensor
        def _(pe):
            def need(name):
                pe.wait_ge(w_arrived[slot_of[name]], arrived_at[name])

            def begin(n, i=0):
                if isinstance(i, int) and n // 2 + 6 * i <= 0:
                    return bank(n)
                pe.wait_ge(proj_evacuated[n % 2], i * 6 + n // 2)
                return bank(n)

            def turn(n, sources, i=0):
                o = begin(n, i)
                for c, a in enumerate(sources):
                    k = a.shape[0]
                    ins = pe.transpose(o[:, c * P:c * P + k], a, ident[0:k, 0:k])
                ins.then_inc(proj_ready, 1)

            def token_major(first, name, width, src=hT):
                need(name)
                s = slot(name)
                for t in range(NT):
                    o = begin(first + t)
                    for k in range(KD):
                        ins = pe.matmul(o[:, 0:width], src[:, k, t * P:(t + 1) * P], s[:, k * width:(k + 1) * width],
                                        start=(k == 0), stop=(k == KD - 1))
                    ins.then_inc(proj_ready, 1)

            def feature_major(first, name):
                need(name)
                s = slot(name)
                for m in range(4):
                    o = begin(first + m)
                    for k in range(KD):
                        ins = pe.matmul(o[:, :], s[:, k * 512 + m * P:k * 512 + (m + 1) * P], hT[:, k, :],
                                        start=(k == 0), stop=(k == KD - 1))
                    ins.then_inc(proj_ready, 1)

            def norm(n):
                pe.wait_ge(normed, NT * (n + 1))
                for k in range(KD):
                    turn(JOBS[f"norm{n}"] + k, [tok[:, t, k * P:(k + 1) * P] for t in range(NT)])
                copied_all(pe, f"norm{n}", KD)

            def latent_queries(i):
                h = (i + 2 - first_latent) // NT
                r = 64 * (h % 2)
                for m in range(2):
                    pe.matmul(begin(LATENT["up", h, m])[:, :], wukT[r:r + 64, h // 2, m * P:(m + 1) * P],
                              aqT[r:r + 64, h // 2, :], start=True, stop=True).then_inc(proj_ready, 1)

            def attention(first, count):
                for i in range(first, first + count + 4):
                    if i in starts_head:
                        latent_queries(i)
                    if i < first + count:
                        it = items[i]
                        if it["kind"] == "latent" and it["t"] == 0:
                            for m in range(2):
                                copied(pe, LATENT["up", it["head"], m])
                        if i >= 2:
                            pe.wait_ge(masked, i - 1)
                        o = psS[i % 2]
                        if it["kind"] == "cmp":
                            g = it["g"]
                            for j in range(8):
                                ins = pe.matmul(o[:, j * 32:(j + 1) * 32],
                                                qT2[64 * g:64 * g + 64, j, it["t"] * P:(it["t"] + 1) * P],
                                                kcT[64 * g:64 * g + 64, 0:32], start=True, stop=True)
                        else:
                            for c, (a, b) in enumerate(it["scores"]):
                                ins = pe.matmul(o[:, 0:it["n"]], a, b, start=(c == 0),
                                                stop=(c == len(it["scores"]) - 1))
                        ins.then_inc(scores_ready, 1)
                    k = i - 2
                    if first <= k < first + count:
                        pe.wait_ge(probs_ready, k + 1)
                        if k >= 2:
                            pe.wait_ge(turned_copied[k % 2], k // 2)
                        for b in range(len(items[k]["blocks"])):
                            ins = pe.transpose(psT[k % 2][:, b * P:(b + 1) * P], PR[k % 3][:, b * P:(b + 1) * P], ident)
                        ins.then_inc(turned, 1)
                    k = i - 3
                    if first <= k < first + count:
                        it = items[k]
                        pe.wait_ge(turned_copied[k % 2], k // 2 + 1)
                        if k >= 2:
                            pe.wait_ge(out_taken[k % 2], k // 2)
                        o, pt = psO[k % 2], PT[k % 2]
                        nb = len(it["blocks"])
                        if it["kind"] == "cmp":
                            for b in range(2):
                                ins = pe.matmul(o[:, b * 256:(b + 1) * 256], pt[:, b * P:(b + 1) * P],
                                                vcBD[:, it["g"], :], start=True, stop=True)
                        elif it["kind"] == "latent":
                            for m in range(2):
                                for b, kb in enumerate(it["blocks"]):
                                    ins = pe.matmul(o[:, m * P:(m + 1) * P], ckv[:, kb, m * P:(m + 1) * P],
                                                    pt[:, b * P:(b + 1) * P], start=(b == 0), stop=(b == nb - 1))
                        else:
                            for b, kb in enumerate(it["blocks"]):
                                ins = pe.matmul(o[:, 0:HD], pt[:, b * P:(b + 1) * P], it["values"][:, kb, :],
                                                start=(b == 0), stop=(b == nb - 1))
                        ins.then_inc(values_ready, 1)
                    k = i - 4
                    if first <= k < first + count and items[k]["kind"] == "latent":
                        n, h = LATENT["out", k - first_latent], items[k]["head"]
                        o = begin(n)
                        pe.wait_ge(out_taken[k % 2], k // 2 + 1)
                        for m in range(2):
                            ins = pe.matmul(o[:, 0:HD], olat[:, k % 2, m * P:(m + 1) * P],
                                            wuv[:, m, h * HD:(h + 1) * HD], start=(m == 0), stop=(m == 1))
                        ins.then_inc(proj_ready, 1)

            def attended(count):
                for k in (count - 2, count - 1):
                    pe.wait_ge(out_taken[k % 2], k // 2 + 1)

            def out_projection(n, first, name):
                for k in range(KD):
                    turn(JOBS[f"turn_o{n}"] + k, [tok[:, t, k * P:(k + 1) * P] for t in range(NT)])
                copied_all(pe, f"turn_o{n}", KD)
                for c in range(2):
                    token_major(first + NT * c, f"{name}{c}", 512)

            def mlp(l):
                for c in range(8):
                    feature_major(JOBS[f"up{l}"] + 4 * c, f"up{l}{c}")
                copied_all(pe, f"up{l}", NF)
                acc = [psS[0], psS[1], psT[0], psT[1]]
                for c in range(2):
                    if 2 * l + c > 0:
                        pe.wait_ge(acc_taken, NT * (2 * l + c))
                    for q in range(4):
                        need(f"down{l}{c}{q}")
                        s = slot(f"down{l}{c}{q}")
                        for f in range(8):
                            for t in range(NT):
                                ins = pe.matmul(acc[t][:, :], hid[:, q * 8 + f, t * P:(t + 1) * P],
                                                s[:, f * 512:(f + 1) * 512], start=(q == 0 and f == 0),
                                                stop=(q == 3 and f == 7))
                                if q == 3 and f == 7:
                                    ins.then_inc(acc_ready, 1)
                        if q < 3:
                            ins.then_inc(down_used, 1)

            pe.wait_ge(const_loaded, CONST_LOADS * 16)
            turn(JOBS["vec"], [vec_rows[:, :]])
            copied(pe, JOBS["vec"])
            norm(0)
            token_major(JOBS["q"], "q", 512)
            token_major(JOBS["kv"], "kv", 256)
            feature_major(JOBS["cc"], "cc")
            feature_major(JOBS["cx"], "cx")
            feature_major(JOBS["cb"], "cb")
            for c in range(2):
                feature_major(JOBS["ga"] + 4 * c, f"ga{c}")
            for c in range(2):
                feature_major(JOBS["gc"] + 4 * c, f"gc{c}")
            pe.wait_ge(heads_ready, 1)
            for j in range(5):
                turn(JOBS["turn_q"] + j, [qk[:, t, j * P:(j + 1) * P] for t in range(NT)])
            copied_all(pe, "turn_q", 5)
            attention(0, n_band)
            attended(n_band)
            for c in range(4):
                turn(JOBS["turn_o0"] + c, [tok[:, t, c * P:(c + 1) * P] for t in range(NT)])
            copied_all(pe, "turn_o0", 4)
            copied_all(pe, "gc", KD)
            need("ap")
            need("cp")
            for m in range(KD):
                for c, (name, src) in enumerate((("ap", attnT), ("cp", conv))):
                    n = JOBS["merge"] + 2 * m + c
                    o = begin(n)
                    for k in range(4):
                        ins = pe.matmul(o[:, :], slot(name)[:, k * D + m * P:k * D + (m + 1) * P], src[:, k, :],
                                        start=(k == 0), stop=(k == 3))
                    ins.then_inc(proj_ready, 1)
            pe.wait_ge(merged, KD)
            for c in range(2):
                token_major(JOBS["wo"] + NT * c, f"wo{c}", 512)

            norm(1)
            n = JOBS["logits"]
            o = begin(n)
            router_w = prm("router_w").rearrange("p (k n) -> p k n", k=KD)
            for t in range(NT):
                for k in range(KD):
                    ins = pe.matmul(o[:, t * 36:(t + 1) * 36], hT[:, k, t * P:(t + 1) * P], router_w[:, k, :],
                                    start=(k == 0), stop=(k == KD - 1))
            ins.then_inc(proj_ready, 1)
            n = JOBS["ranks"]
            o = begin(n)
            pe.wait_ge(assigned, 1)
            for t in range(NT + 1):
                for s in range(min(t + 1, NT)):
                    ins = pe.matmul(o[:, t * E:(t + 1) * E], before if s == t else ones, asg[:, s, :],
                                    start=(s == 0), stop=(s == min(t, NT - 1)))
            ins.then_inc(proj_ready, 1)

            def turn_rows(p, i, n, count):
                pe.wait_ge(gathered[p], count * 16)
                for c in range(2):
                    turn(n + c, [xg[:, p, (4 * c + k) * P:(4 * c + k + 1) * P] for k in range(4)], i)

            def expert_block(p, i, last=False):
                turns, gate, hidn, down = moe_products(p, i, last)
                o = begin(gate, i)
                pe.wait_ge(gu_arrived[p], i * 32 + 32)
                for m in range(2):
                    copied(pe, turns + m, i)
                for k in range(KD):
                    ins = pe.matmul(o[:, :], xT[:, p, k, :], gu[p][:, k, :], start=(k == 0), stop=(k == KD - 1))
                ins.then_inc(proj_ready, 1)
                if not last:
                    turn_rows(1 - p, i, gate + 1, i + (1 + p))
                copied(pe, gate, i)
                turn(hidn, [ehid[:, p, k * P:(k + 1) * P] for k in range(2)], i)
                copied(pe, hidn, i)
                pe.wait_ge(dn_arrived[p], i * 16 + 16)
                for half in range(2):
                    o = begin(down + half, i)
                    for k in range(2):
                        ins = pe.matmul(o[:, :], ehidT[:, p, k * P:(k + 1) * P], dn[p][:, k, half * 512:(half + 1) * 512],
                                        start=(k == 0), stop=(k == 1))
                    ins.then_inc(proj_ready, 1)

            turn_rows(0, 0, moe_job(0, "turn"), 1)
            moe_pairs(pe, expert_block)

            norm(2)
            token_major(JOBS["ai"], "ai", 512)
            token_major(JOBS["ax"], "ax", 352)
            token_major(JOBS["aq"], "aq", 512)
            token_major(JOBS["bv"], "bv", 512)
            pe.wait_ge(heads_ready, 2)
            turn(JOBS["turn_small"], [kid[:, t, :] for t in range(NT)])
            turn(JOBS["turn_small"] + 1, [krd[:, t, :] for t in range(NT)])
            for m in range(2):
                turn(JOBS["turn_small"] + 2 + m, [ckv[:, t, m * P:(m + 1) * P] for t in range(NT)])
            pe.wait_ge(latent_weights, 48)
            for c in range(2):
                turn(JOBS["turn_uk"] + c, [wuk[:, m, 2 * j:2 * j + 2, :].rearrange("p h d -> p (h d)")
                                           for j in (2 * c, 2 * c + 1) for m in range(2)])
            for j in range(4):
                turn(JOBS["turn_qi"] + j, [tok[:, t, 512 + j * P:512 + (j + 1) * P] for t in range(NT)])
            o = begin(JOBS["forget"])
            for t in range(NT):
                ins = pe.matmul(o[0:8, t * P:T], sp_terms[:, t, :], upto[:, 0:T - t * P], start=(t == 0),
                                stop=(t == NT - 1))
            ins.then_inc(proj_ready, 1)
            copied_all(pe, "turn_qi", 4)
            for t in range(1, NT):
                for h in range(8):
                    n, r = JOBS["index"] + 8 * (t - 1) + h, 64 * (h % 2)
                    pe.matmul(begin(n)[:, 0:(t + 1) * P], qiT[r:r + 64, h // 2, t * P:(t + 1) * P],
                              kiT[r:r + 64, 0:(t + 1) * P], start=True, stop=True).then_inc(proj_ready, 1)
            feature_major(JOBS["bq"], "bq")
            feature_major(JOBS["bk"], "bk")
            for j in range(4):
                turn(JOBS["turn_aq"] + j, [tok[:, t, j * P:(j + 1) * P] for t in range(NT)])
            copied_all(pe, "turn_aq", 4)
            attention(first_fox, first_nsa - first_fox)
            attended(first_nsa)
            for c in range(2):
                copied(pe, JOBS["latent"] + len(LATENT) - 2 + c)
            out_projection(1, JOBS["ao"], "ao")
            norm(3)
            mlp(0)

            norm(4)
            token_major(JOBS["nk"], "nk", 512)
            token_major(JOBS["nv"], "nv", 304)
            for c in range(2):
                token_major(JOBS["nq"] + NT * c, f"nq{c}", 512)
            pe.wait_ge(heads_ready, 3)
            for j in range(8):
                turn(JOBS["turn_nq"] + j, [tok[:, t, j * P:(j + 1) * P] for t in range(NT)])
            for c, col in enumerate((0, 128, 256, 512)):
                turn(JOBS["turn_nk"] + c, [kv2[:, t, col:col + P] for t in range(NT)])
            turn(JOBS["cmp"], [pe_rows[:, :]])
            copied_all(pe, "turn_nk", 4)
            copied(pe, JOBS["cmp"])
            for s, kind in enumerate("kv"):
                need("w1" + kind)
                w1 = slot("w1" + kind)
                for g in range(2):
                    o = begin(JOBS["cmp"] + 1 + 2 * s + g)
                    for i in range(CMP_LEN):
                        ins = pe.matmul(o[:, 0:N_CMP], w1[64 * g:64 * g + 64, i * P:(i + 1) * P],
                                        kT4[64 * g:64 * g + 64, s, i:i + CMP_STRIDE * (N_CMP - 1) + 1:CMP_STRIDE],
                                        start=(i == 0), stop=(i == CMP_LEN - 1))
                    if g == s:
                        for i in range(CMP_LEN):
                            ins = pe.matmul(o[:, 32:33], w1[64 * g:64 * g + 64, i * P:(i + 1) * P],
                                            peT[64 * g:64 * g + 64, i:i + 1], start=(i == 0), stop=(i == CMP_LEN - 1))
                    ins.then_inc(proj_ready, 1)
            pe.wait_ge(gelu_out, 1)
            cmp_w2 = prm("cmp_w2").rearrange("p (s n) -> p s n", s=2)
            o = begin(JOBS["cmp"] + 5)
            for g in range(2):
                ins = pe.matmul(o[64 * g:64 * g + 64, 0:32], cmp_w2[:, 0, :], chid[:, 6, 32 * g:32 * g + 32],
                                start=True, stop=True)
            ins.then_inc(proj_ready, 1)
            o = begin(JOBS["cmp"] + 6)
            for j in range(4):
                for g in range(2):
                    ins = pe.matmul(o[32 * j:32 * j + 32, 64 * g:64 * g + 64], chid[:, 7, 32 * g:32 * g + 32],
                                    cmp_w2[:, 1, :], start=True, stop=True)
            ins.then_inc(proj_ready, 1)
            for c in range(2):
                copied(pe, JOBS["cmp"] + 5 + c)
            attention(first_nsa, n_items - first_nsa)
            attended(n_items)
            out_projection(2, JOBS["no"], "no")
            norm(5)
            mlp(1)

        @block.scalar
        def _(act):
            chain = [0]

            def link(ins):
                chain[0] += 1
                ins.then_inc(act_chain, 1)
                act.wait_ge(act_chain, chain[0])

            def A(o, i, f, **kw):
                return nc.scalar.activation(o, i, f, **kw)

            def evac(n, o, width=512, f=ACT.Copy, **kw):
                product(act, n)
                A(o, bank(n)[:, 0:width], f, **kw).then_inc(proj_evacuated[n % 2], 1)

            def norm(n):
                c = slice(NT * n, NT * n + NT)
                for t in range(NT):
                    A(tok[:, t, :], x[:, t, :], ACT.Square, accum_out=ss[:, NT * n + t:NT * n + t + 1])\
                        .then_inc(sumsq_ready, 1)
                act.wait_ge(mean_ready, n + 1)
                A(rstd[:, c], ss[:, c], ACT.Sqrt).then_inc(root_ready, 1)
                if n == len(NORMS):
                    return
                act.wait_ge(rstd_ready, n + 1)
                for t in range(NT):
                    A(tok[:, t, :], x[:, t, :], ACT.Copy, scale=rstd[:, NT * n + t:NT * n + t + 1]).then_inc(normed, 1)
                if n == 1:
                    act.wait_ge(normed, NT * 2)
                    act.dma_start(rows_dram.rearrange("(t p) d -> p t d", p=P), tok[:, :, :]).then_inc(rows_stored, 16)
                for k in range(1, KD, 2):
                    g = GAINS[NORMS[n]] + k
                    evac(JOBS[f"norm{n}"] + k, hT[:, k, :], scale=vec[:, g:g + 1])

            def attention(first, count):
                for i in range(first, first + count + 3):
                    if i in starts_head:
                        h = (i + 2 - first_latent) // NT
                        if h >= 2:
                            act.wait_ge(scores_ready, first_latent + (h - 1) * NT)
                        for m in range(2):
                            evac(LATENT["up", h, m], qabs[:, h % 2, m, :])
                    if i < first + count:
                        it = items[i]
                        act.wait_ge(masked, i + 1)
                        if i >= 3:
                            act.wait_ge(turned, i - 2)
                            if items[i - 3]["kind"] == "cmp":
                                act.wait_ge(factor_ready, i - 2)
                        if it["kind"] == "cmp":
                            A(PR[i % 3][:, 0:256], S[i % 2][:, 0:256], ACT.Exp).then_inc(probs_ready, 1)
                        else:
                            if it["kind"] == "band":
                                A(esink[:, i:i + 1], prm("sink")[:, it["head"]:it["head"] + 1], ACT.Exp,
                                  bias=negm[:, i:i + 1])
                            A(PR[i % 3][:, 0:it["n"]], S[i % 2][:, 0:it["n"]], ACT.Exp, bias=negm[:, i:i + 1],
                              scale=-1.0, accum_out=sums[:, i:i + 1]).then_inc(probs_ready, 1)
                    k = i - 2
                    if first <= k < first + count and k % 2 == 0:
                        act.wait_ge(turned, k + 1)
                        if k >= 2:
                            act.wait_ge(values_ready, k - 1)
                        n = P * len(items[k]["blocks"])
                        A(PT[0][:, 0:n], psT[0][:, 0:n], ACT.Copy).then_inc(turned_copied[0], 1)
                    k = i - 3
                    if first <= k < first + count and items[k]["kind"] == "latent":
                        act.wait_ge(values_ready, k + 1)
                        if k - first_latent >= 2:
                            product(act, LATENT["out", k - first_latent - 2])
                        A(olat[:, k % 2, :], psO[k % 2][:, 0:256], ACT.Copy).then_inc(out_taken[k % 2], 1)

            def mlp(l):
                for f in range(NF):
                    n = JOBS[f"up{l}"] + f
                    product(act, n)
                    link(A(hid[:, f, :], bank(n)[:, :], ACT.Relu))
                    A(hid[:, f, :], hid[:, f, :], ACT.Square).then_inc(proj_evacuated[n % 2], 1)

            for dst, src in loads:
                act.dma_start(dst, src).then_inc(const_loaded, 16)
            act.wait_ge(const_loaded, CONST_LOADS * 16)
            evac(JOBS["vec"], vec[:, :], 64)
            copied(act, JOBS["vec"])

            act.wait_ge(x_loaded, 16)
            norm(0)
            for t in range(NT):
                n = JOBS["kv"] + t
                product(act, n)
                A(qk[:, t, 512:640], bank(n)[:, 0:P], ACT.Copy)
                A(v1[:, t, :], bank(n)[:, P:2 * P], ACT.Copy).then_inc(proj_evacuated[n % 2], 1)
            for m in range(4):
                evac(JOBS["cc"] + m, u[:, m, 1:T + 1])
            act.wait_ge(head_mean, 1)
            A(qss[:, 0:40], qss[:, 0:40], ACT.Sqrt).then_inc(head_root, 1)
            for m in range(KD):
                evac(JOBS["ga"] + m, ga[:, m, :], f=ACT.Sigmoid)
            for m in range(KD):
                evac(JOBS["gc"] + m, gc[:, m, :], f=ACT.Sigmoid)
            for j in range(5):
                evac(JOBS["turn_q"] + j, qT1[:, j, :] if j < 4 else kT1)
            attention(0, n_band)
            for c in range(4):
                evac(JOBS["turn_o0"] + c, attnT[:, c, :])

            copied_all(act, "wo", 2 * NT)
            norm(1)
            act.wait_ge(logits_shifted, 1)
            A(gexp, gexp, ACT.Exp).then_inc(logits_exp, 1)
            A(pexp, pexp, ACT.Exp).then_inc(logits_exp, 1)

            def expert_block(p, i, last=False):
                _, gate, hidn, down = moe_products(p, i, last)
                product(act, gate, i)
                if not first(i):
                    copied(act, gate - 12, i)
                A(sg[:, p, :], bank(gate)[:, 0:F_E], ACT.Sigmoid).then_inc(silu_ready, 1)
                product(act, hidn, i)
                A(ehidT[:, p, :], bank(hidn)[:, 0:F_E], ACT.Copy).then_inc(proj_evacuated[hidn % 2], 1)
                for half in range(2):
                    n = down + half
                    product(act, n, i)
                    if half == 0 and not first(i):
                        act.wait_ge(y_written[p], i * 16)
                    A(ey[:, p, half * 512:(half + 1) * 512], bank(n)[:, :], ACT.Copy).then_inc(proj_evacuated[n % 2], 1)
                for half in range(2):
                    copied(act, down + half, i)
                row = i * (2 * P) + p * P
                act.dma_start(y_dram[bass.ds(row, P), :], ey[:, p, :]).then_inc(y_written[p], 16)

            moe_pairs(act, expert_block)

            act.wait_ge(combined, NT)
            norm(2)
            for t in range(NT):
                n = JOBS["ax"] + t
                product(act, n)
                if t == 0:
                    act.wait_ge(latent_zeroed, 2)
                o = bank(n)
                A(ckv[:, t, :], o[:, 0:256], ACT.Copy)
                A(krd[:, t, 0:2 * ROT], o[:, 256:272], ACT.Copy)
                A(kid[:, t, 0:HD], o[:, 272:336], ACT.Copy)
                A(wb[:, t, :], o[:, 336:352], ACT.Copy).then_inc(proj_evacuated[n % 2], 1)
            act.wait_ge(head_mean, 2)
            A(qss[:, 0:8], qss[:, 0:8], ACT.Sqrt).then_inc(head_root, 1)
            act.wait_ge(forget_z, 1)
            link(A(sp_part(1), sp_part(0), ACT.Abs))
            link(A(sp_part(1), sp_part(1), ACT.Exp, scale=-1.0))
            A(sp_part(1), sp_part(1), ACT.Ln, bias=1.0).then_inc(forget_ln, 1)
            for t in range(NT):
                evac(JOBS["bv"] + t, bv[:, t, :])
            evac(JOBS["turn_small"], kiT)
            evac(JOBS["turn_small"] + 1, krT)
            for m in range(2):
                evac(JOBS["turn_small"] + 2 + m, ckvT[:, m, :])
            for c in range(2):
                evac(JOBS["turn_uk"] + c, wukT[:, 2 * c:2 * c + 2, :].rearrange("p j n -> p (j n)"))
            for j in range(4):
                evac(JOBS["turn_qi"] + j, qiT[:, j, :])
            n = JOBS["forget"]
            product(act, n)
            A(ncum[0:8, :], bank(n)[0:8, :], ACT.Copy).then_inc(proj_evacuated[n % 2], 1)
            for c in range(8 * (NT - 1)):
                if c >= 2:
                    act.wait_ge(relu_used, c - 1)
                n = (c // 8 + 2) * P
                evac(JOBS["index"] + c, S[c % 2][:, 0:n], n, ACT.Relu)
            for m in range(4):
                evac(JOBS["bq"] + m, bqT[:, m, :], scale=SCALE)
            for m in range(4):
                evac(JOBS["bk"] + m, bkT[:, m, :])
            for j in range(4):
                evac(JOBS["turn_aq"] + j, aqT[:, j, :])
            attention(first_fox, first_nsa - first_fox)
            for k in range(KD):
                evac(JOBS["turn_o1"] + k, hT[:, k, :])
            copied_all(act, "ao", 2 * NT)
            norm(3)
            mlp(0)

            act.wait_ge(acc_taken, 2 * NT)
            norm(4)
            for t in range(NT):
                evac(JOBS["nk"] + t, kv2[:, t, 0:512])
            for t in range(NT):
                n = JOBS["nv"] + t
                product(act, n)
                A(kv2[:, t, 512:768], bank(n)[:, 0:256], ACT.Copy)
                A(gate2[:, t, :], bank(n)[:, 256:304], ACT.Copy).then_inc(proj_evacuated[n % 2], 1)
            act.wait_ge(gate_ready, 1)
            A(a4["gate"], a4["gate"], ACT.Sigmoid).then_inc(gate_ready, 1)
            for j in range(8):
                evac(JOBS["turn_nq"] + j, qT2[:, j, :])
            for c in range(4):
                evac(JOBS["turn_nk"] + c, kT4[:, c, :])
            evac(JOBS["cmp"], peT, 32)
            act.wait_ge(gelu_in, 1)
            A(cpart(2), cpart(1), ACT.Sigmoid, scale=2 * GELU_C).then_inc(gelu_sig, 1)
            evac(JOBS["cmp"] + 5, kcT, 32)
            attention(first_nsa, n_items - first_nsa)
            for k in range(KD):
                evac(JOBS["turn_o2"] + k, hT[:, k, :])
            copied_all(act, "no", 2 * NT)
            norm(5)
            mlp(1)
            act.wait_ge(acc_taken, 4 * NT)
            norm(6)

        @block.vector
        def _(dve):
            chain = [0]

            def link(ins):
                chain[0] += 1
                ins.then_inc(dve_chain, 1)
                dve.wait_ge(dve_chain, chain[0])

            def tt(o, a, b, op):
                return nc.vector.tensor_tensor(o, a, b, op)

            def ts(o, a, s1, s2=None, op0=ALU.mult, op1=None):
                if op1 is None:
                    return nc.vector.tensor_scalar(o, a, s1, None, op0)
                return nc.vector.tensor_scalar(o, a, s1, s2, op0, op1)

            def evac_to(n):
                product(dve, n)
                return bank(n)

            def norm(n):
                c = slice(NT * n, NT * n + NT)
                dve.wait_ge(sumsq_ready, NT * (n + 1))
                ts(ss[:, c], ss[:, c], 1.0 / D, EPS, ALU.mult, ALU.add).then_inc(mean_ready, 1)
                dve.wait_ge(root_ready, n + 1)
                nc.vector.reciprocal(rstd[:, c], rstd[:, c]).then_inc(rstd_ready, 1)
                if n == len(NORMS):
                    return
                for k in range(0, KD, 2):
                    g, j = GAINS[NORMS[n]] + k, JOBS[f"norm{n}"] + k
                    ts(hT[:, k, :], evac_to(j)[:, :], vec[:, g:g + 1]).then_inc(proj_evacuated[j % 2], 1)

            def add_to_x(first):
                for c in range(2):
                    for t in range(NT):
                        n = first + NT * c + t
                        o = evac_to(n)
                        xs = x[:, t, c * 512:(c + 1) * 512]
                        tt(xs, o[:, :], xs, ALU.add).then_inc(proj_evacuated[n % 2], 1)

            def rope(view, heads, temps, signal=None):
                x1, x2 = view[:, :, :, 0:ROT], view[:, :, :, ROT:2 * ROT]
                shape = [P, NT, heads, ROT]
                n = NT * heads * ROT
                t1, t2, t3, t4 = (temps[:, k * n:(k + 1) * n].rearrange("p (t h c) -> p t h c", t=NT, h=heads)
                                  for k in range(4))
                c, s = cos4.unsqueeze(2).broadcast_to(shape), sin4.unsqueeze(2).broadcast_to(shape)
                tt(t1, x1, c, ALU.mult)
                tt(t2, x2, s, ALU.mult)
                tt(t3, x2, c, ALU.mult)
                link(tt(t4, x1, s, ALU.mult))
                tt(x1, t1, t2, ALU.subtract)
                if signal is None:
                    link(tt(x2, t3, t4, ALU.add))
                else:
                    tt(x2, t3, t4, ALU.add).then_inc(signal, 1)

            def attention(first, count):
                for i in range(first, first + count + 4):
                    if i < first + count:
                        it = items[i]
                        dve.wait_ge(scores_ready, i + 1)
                        if i >= 2:
                            dve.wait_ge(probs_ready, i - 1)
                        if it["kind"] == "cmp":
                            s3 = S[i % 2][:, 0:256].rearrange("p (j n) -> p j n", j=8)
                            st = cmpst[:, it["index"], :]
                            link(tt(s3, psS[i % 2][:, 0:256].rearrange("p (j n) -> p j n", j=8),
                                    cmpmask[:, it["t"], :].unsqueeze(1).broadcast_to([P, 8, 32]), ALU.add))
                            link(nc.vector.tensor_reduce(st, s3, X, ALU.max))
                            tt(s3, s3, st.unsqueeze(2).broadcast_to([P, 8, 32]), ALU.subtract).then_inc(masked, 1)
                        else:
                            floor = negsink[:, it["head"]:it["head"] + 1] if it["kind"] == "band" else 3e38
                            nc.vector.tensor_tensor_reduce(
                                out=S[i % 2][:, 0:it["n"]], in0=psS[i % 2][:, 0:it["n"]], in1=it["mask"], scale=-1.0,
                                scalar=floor, op0=ALU.add, op1=ALU.min, accum_out=negm[:, i:i + 1]).then_inc(masked, 1)
                    k = i - 2
                    if first <= k < first + count:
                        if k % 2 == 1:
                            dve.wait_ge(turned, k + 1)
                            if k >= 2:
                                dve.wait_ge(values_ready, k - 1)
                            n = P * len(items[k]["blocks"])
                            nc.vector.tensor_copy(PT[1][:, 0:n], psT[1][:, 0:n]).then_inc(turned_copied[1], 1)
                        factor(k)
                    k = i - 3
                    if first <= k < first + count and items[k]["kind"] != "latent":
                        finish(k)
                    k = i - 4
                    if first <= k < first + count and items[k]["kind"] == "latent":
                        it, n = items[k], LATENT["out", k - first_latent]
                        o = evac_to(n)
                        dve.wait_ge(factor_ready, k + 1)
                        ts(tok[:, it["t"], it["head"] * HD:(it["head"] + 1) * HD], o[:, 0:HD], fac[:, k:k + 1])\
                            .then_inc(proj_evacuated[n % 2], 1)

            def factor(k):
                it, t = items[k], items[k]["t"]
                f, total = fac[:, k:k + 1], sums[:, k:k + 1]
                dve.wait_ge(probs_ready, k + 1)
                if it["kind"] == "cmp":
                    st, g = cmpst[:, it["index"], :], it["g"]
                    link(nc.vector.tensor_reduce(st, PR[k % 3][:, 0:256].rearrange("p (j n) -> p j n", j=8), X, ALU.add))
                    link(nc.vector.reciprocal(st, st))
                    nc.vector.scalar_tensor_tensor(
                        out=st, in0=st, scalar=cmpok[:, t:t + 1],
                        in1=gate2[:, t, g * 24:g * 24 + 24].rearrange("p (j r) -> p j r", r=3)[:, :, 0],
                        op0=ALU.mult, op1=ALU.mult).then_inc(factor_ready, 1)
                elif it["kind"] == "pair":
                    link(nc.vector.reciprocal(f, total))
                    tt(f, f, it["gate"], ALU.mult).then_inc(factor_ready, 1)
                else:
                    if it["kind"] == "band":
                        link(tt(total, total, esink[:, k:k + 1], ALU.add))
                    nc.vector.reciprocal(f, total).then_inc(factor_ready, 1)

            def finish(k):
                it, t = items[k], items[k]["t"]
                f, o = fac[:, k:k + 1], psO[k % 2]
                dve.wait_ge(values_ready, k + 1)
                dve.wait_ge(factor_ready, k + 1)
                if it["kind"] == "cmp":
                    st, g = cmpst[:, it["index"], :], it["g"]
                    tt(tok[:, t, g * 512:(g + 1) * 512].rearrange("p (j d) -> p j d", d=HD),
                       o[:, :].rearrange("p (j d) -> p j d", d=HD), st.unsqueeze(2).broadcast_to([P, 8, HD]),
                       ALU.mult).then_inc(out_taken[k % 2], 1)
                    return
                dst = tok[:, t, it["head"] * HD:(it["head"] + 1) * HD]
                if it["kind"] == "pair":
                    before_k = k - NT if it["branch"] else first_nsa + (it["head"] // 8) * NT + t
                    dve.wait_ge(out_taken[before_k % 2], before_k // 2 + 1)
                    nc.vector.scalar_tensor_tensor(out=dst, in0=o[:, 0:HD], scalar=f, in1=dst, op0=ALU.mult,
                                                   op1=ALU.add).then_inc(out_taken[k % 2], 1)
                else:
                    ts(dst, o[:, 0:HD], f).then_inc(out_taken[k % 2], 1)

            def mlp(l):
                acc = [psS[0], psS[1], psT[0], psT[1]]
                for c in range(2):
                    for t in range(NT):
                        dve.wait_ge(acc_ready, NT * (2 * l + c) + t + 1)
                        xs = x[:, t, c * 512:(c + 1) * 512]
                        tt(xs, acc[t][:, :], xs, ALU.add).then_inc(acc_taken, 1)

            nc.vector.memset(u[:, :, 0:T + 2:T + 1], 0.0)
            dve.wait_ge(const_loaded, CONST_LOADS * 16)
            copied(dve, JOBS["vec"])
            link(ts(negsink, prm("sink"), -1.0))
            norm(0)
            for t in range(NT):
                n = JOBS["q"] + t
                o = evac_to(n)
                nc.vector.tensor_copy(qk[:, t, 0:512].rearrange("p (j g d) -> p j g d", j=4, g=2),
                                      o[:, :].rearrange("p (g j d) -> p j g d", j=4, g=2))\
                    .then_inc(proj_evacuated[n % 2], 1)
            copied_all(dve, "q", NT)
            copied_all(dve, "kv", NT)
            qk4 = qk.rearrange("p t (h d) -> p (t h) d", d=HD)
            sq4 = tok[:, :, 0:640].rearrange("p t (h d) -> p t h d", d=HD)
            qss3 = qss[:, 0:40].rearrange("p (t h) -> p t h", t=NT)
            for t in range(NT):
                last = tt(tok[:, t, 0:640], qk[:, t, :], qk[:, t, :], ALU.mult)
            link(last)
            link(nc.vector.tensor_reduce(qss3, sq4, X, ALU.add))
            ts(qss[:, 0:40], qss[:, 0:40], 1.0 / HD, EPS, ALU.mult, ALU.add).then_inc(head_mean, 1)
            for m in range(4):
                n = JOBS["cx"] + m
                o = evac_to(n)
                copied(dve, JOBS["cc"] + m)
                tt(u[:, m, 1:T + 1], o[:, :], u[:, m, 1:T + 1], ALU.mult).then_inc(proj_evacuated[n % 2], 1)
            copied_all(dve, "cx", 4)
            for m in range(4):
                cw = [vec[:, CONVW + 4 * j + m:CONVW + 4 * j + m + 1] for j in range(3)]
                cb = vec[:, CONVB + m:CONVB + m + 1]
                link(ts(conv[:, m, :], u[:, m, 0:T], cw[0], cb, ALU.mult, ALU.add))
                for j in (1, 2):
                    link(nc.vector.scalar_tensor_tensor(out=conv[:, m, :], in0=u[:, m, j:j + T], scalar=cw[j],
                                                        in1=conv[:, m, :], op0=ALU.mult, op1=ALU.add))
                n = JOBS["cb"] + m
                o = evac_to(n)
                tt(conv[:, m, :], o[:, :], conv[:, m, :], ALU.mult).then_inc(proj_evacuated[n % 2], 1)
            dve.wait_ge(head_root, 1)
            link(nc.vector.reciprocal(qss[:, 0:40], qss[:, 0:40]))
            link(ts(qss3[:, :, 0:8], qss3[:, :, 0:8], SCALE))
            link(tt(qk4, qk4, qss[:, 0:40].unsqueeze(2).broadcast_to([P, 40, HD]), ALU.mult))
            link(tt(qk, qk, prm("qk_gain").unsqueeze(1).broadcast_to([P, NT, 640]), ALU.mult))
            rope(qk.rearrange("p t (h d) -> p t h d", d=HD), 10, scr.rearrange("p a n -> p (a n)"),
                 heads_ready)
            attention(0, n_band)
            for m in range(KD):
                for c, gate in enumerate((ga, gc)):
                    n = JOBS["merge"] + 2 * m + c
                    o = evac_to(n)
                    tt(gate[:, m, :], o[:, :], gate[:, m, :], ALU.mult).then_inc(proj_evacuated[n % 2], 1)
                for c in range(2):
                    copied(dve, JOBS["merge"] + 2 * m + c)
                tt(hT[:, m, :], ga[:, m, :], gc[:, m, :], ALU.add).then_inc(merged, 1)
            add_to_x(JOBS["wo"])

            norm(1)
            logit = a2["logit"].rearrange("p (t n) -> p t n", t=NT)
            n = JOBS["logits"]
            o = evac_to(n)
            tt(logit, o[:, 0:NT * 36].rearrange("p (t n) -> p t n", t=NT),
               prm("router_b").unsqueeze(1).broadcast_to([P, NT, 36]), ALU.add).then_inc(proj_evacuated[n % 2], 1)
            copied(dve, n)
            gl, el = logit[:, :, 0:G], logit[:, :, G:36]

            def bc(a, shape):
                return a.unsqueeze(2).broadcast_to(shape)

            def first_max(values, width, best, work, hot):
                shape = [P, NT, width]
                link(nc.vector.tensor_reduce(best, values, X, ALU.max))
                link(tt(work, values, bc(best, shape), ALU.is_equal))
                link(tt(work, work, iota[:, 0:width].unsqueeze(1).broadcast_to(shape), ALU.mult))
                link(nc.vector.tensor_reduce(where, work, X, ALU.min))
                link(tt(hot, iota[:, 0:width].unsqueeze(1).broadcast_to(shape), bc(where, shape), ALU.is_equal))

            def s4(k):
                return a2["s"][:, 4 * k:4 * k + 4]

            where, gbest, best1, best2, den, pick = (s4(k) for k in range(6))
            g16 = a2["w1"][:, 0:16].rearrange("p (t n) -> p t n", t=NT)
            hot_g = a2["w1"][:, 16:32].rearrange("p (t n) -> p t n", t=NT)
            work = a2["w2"][:, 0:128].rearrange("p (t n) -> p t n", t=NT)
            inside = a2["w3"][:, 0:128].rearrange("p (t n) -> p t n", t=NT)
            oh = [a2[k].rearrange("p (t n) -> p t n", t=NT) for k in ("oh1", "oh2")]
            first_max(gl, G, gbest, g16, hot_g)
            link(tt(gexp.rearrange("p (t n) -> p t n", t=NT), gl, bc(gbest, [P, NT, G]), ALU.subtract))
            link(ts(g16, hot_g, -1.0, -NEG, ALU.add, ALU.mult))
            link(tt(inside.rearrange("p t (g e) -> p t g e", g=G), el.rearrange("p t (g e) -> p t g e", g=G),
                    g16.unsqueeze(3).broadcast_to([P, NT, G, EG]), ALU.add))
            first_max(inside, E, best1, work, oh[0])
            link(ts(work, oh[0], NEG))
            link(tt(inside, inside, work, ALU.add))
            first_max(inside, E, best2, work, oh[1])
            tt(asg, oh[0], oh[1], ALU.add).then_inc(assigned, 1)
            tt(pexp, best2, best1, ALU.subtract).then_inc(logits_shifted, 1)
            dve.wait_ge(logits_exp, 2)
            link(nc.vector.tensor_reduce(den, gexp.rearrange("p (t n) -> p t n", t=NT), X, ALU.add))
            link(ts(pick, pexp, 1.0, None, ALU.add))
            link(tt(den, den, pick, ALU.mult))
            link(nc.vector.reciprocal(g12[:, 0, :], den))
            link(tt(g12[:, 1, :], g12[:, 0, :], pexp, ALU.mult))
            n = JOBS["ranks"]
            o = evac_to(n)
            rank = a2["rank"].rearrange("p (t n) -> p t n", t=NT)
            cnt, spill, incl, obase = a2["cnt"], a2["spill"], a2["incl"], a2["obase"]
            nc.vector.tensor_copy(a2["rank"], o[:, 0:P])
            nc.vector.tensor_copy(cnt, o[:, P:P + E]).then_inc(proj_evacuated[n % 2], 1)
            copied(dve, n)

            def over(dst, src, tmp, strict):
                op = ALU.is_gt if strict else ALU.is_ge
                link(ts(dst, src, float(P), None, op))
                for k in (2, 3):
                    link(ts(tmp, src, float(k * P), None, op))
                    link(tt(dst, dst, tmp, ALU.add))

            w2_32 = a2["w2"][:, 128:160]
            over(spill, cnt, w2_32, True)
            link(nc.vector.memset(a2["w2"][:, 160:192], 1.0))
            link(nc.vector.tensor_tensor_scan(incl, a2["w2"][:, 160:192], spill, 0.0, ALU.mult, ALU.add))
            link(tt(obase, incl, spill, ALU.subtract))
            link(ts(obase, obase, float(E - 1), None, ALU.add))
            for k in range(2):
                rk, ek, ob, q, tmp, blk, row = (s4(8 + j) for j in range(7))
                link(tt(work, rank, oh[k], ALU.mult))
                link(nc.vector.tensor_reduce(rk, work, X, ALU.add))
                link(tt(work, oh[k], iota.unsqueeze(1).broadcast_to([P, NT, E]), ALU.mult))
                link(nc.vector.tensor_reduce(ek, work, X, ALU.add))
                link(ts(ek, ek, 64.0, None, ALU.add))
                link(tt(work, oh[k], obase.unsqueeze(1).broadcast_to([P, NT, E]), ALU.mult))
                link(nc.vector.tensor_reduce(ob, work, X, ALU.add))
                over(q, rk, tmp, False)
                link(tt(blk, ob, q, ALU.add))
                link(tt(blk, blk, ek, ALU.subtract))
                link(ts(tmp, q, 0.0, None, ALU.is_gt))
                link(tt(blk, blk, tmp, ALU.mult))
                link(tt(blk, blk, ek, ALU.add))
                link(nc.vector.scalar_tensor_tensor(out=row, in0=q, scalar=-float(P), in1=rk, op0=ALU.mult, op1=ALU.add))
                link(nc.vector.scalar_tensor_tensor(out=tmp, in0=blk, scalar=float(P), in1=row, op0=ALU.mult, op1=ALU.add))
                link(nc.vector.tensor_copy(yrow[:, NT * k:NT * k + NT], tmp))
                link(nc.vector.scalar_tensor_tensor(out=tmp, in0=row, scalar=float(TABW), in1=blk, op0=ALU.mult,
                                                    op1=ALU.add))
                link(nc.vector.tensor_copy(trow[:, NT * k:NT * k + NT], tmp))
            for j in range(SPILL):
                link(ts(w2_32, incl, float(j), None, ALU.is_le))
                link(nc.vector.tensor_reduce(a2["s"][:, 80 + j:81 + j], w2_32, X, ALU.add))
            link(ts(a2["s"][:, 80:80 + SPILL], a2["s"][:, 80:80 + SPILL], float(E - 1), None, ALU.min))
            link(nc.vector.tensor_copy(token_id, cst("token")))
            nc.vector.tensor_copy(spill_expert[:, 0:SPILL], a2["s"][:, 80:80 + SPILL]).then_inc(slots_ready, 1)

            gain2 = vec[:, GAINS["norm2_g"]:GAINS["norm2_g"] + KD]

            def turned_rows(p, n, i):
                for half in range(2):
                    o = bank(n + half)
                    product(dve, n + half, i)
                    tt(xT[:, p, 4 * half:4 * half + 4, :], o[:, :].rearrange("p (k n) -> p k n", k=4),
                       gain2[:, 4 * half:4 * half + 4].unsqueeze(2).broadcast_to([P, 4, P]), ALU.mult)\
                        .then_inc(proj_evacuated[(n + half) % 2], 1)

            def expert_block(p, i, last=False):
                _, gate, _, _ = moe_products(p, i, last)
                o = bank(gate)
                nth = i * 2 + (p + 1)
                dve.wait_ge(silu_ready, nth)
                tt(ehid[:, p, :], o[:, 0:F_E], sg[:, p, :], ALU.mult).then_inc(hidden_part, 1)
                dve.wait_ge(hidden_part, nth)
                tt(ehid[:, p, :], o[:, F_E:2 * F_E], ehid[:, p, :], ALU.mult).then_inc(proj_evacuated[gate % 2], 1)
                if not last:
                    turned_rows(1 - p, gate + 1, i)

            turned_rows(0, moe_job(0, "turn"), 0)
            moe_pairs(dve, expert_block)
            for t in range(NT):
                dve.wait_ge(picked[t % 2], 32 * (t // 2 + 1))
                for k, buf in ((0, ya), (1, yb)):
                    ins = nc.vector.scalar_tensor_tensor(out=x[:, t, :], in0=buf[:, t % 2, :], scalar=g12[:, k, t:t + 1],
                                                         in1=x[:, t, :], op0=ALU.mult, op1=ALU.add)
                    if k == 0:
                        link(ins)
                ins.then_inc(combined, 1)

            norm(2)
            for t in range(NT):
                n = JOBS["ai"] + t
                nc.vector.tensor_copy(tok[:, t, 512:1024], evac_to(n)[:, :]).then_inc(proj_evacuated[n % 2], 1)
            copied_all(dve, "ax", NT)
            sq = scr[:, 4:6, :].rearrange("p a n -> p (a n)")
            temps = scr.rearrange("p a n -> p (a n)")[:, 0:1024]
            link(tt(sq, a3["ckv"], a3["ckv"], ALU.mult))
            link(nc.vector.tensor_reduce(qss[:, 0:4], sq.rearrange("p (t n) -> p t n", t=NT), X, ALU.add))
            link(ts(qss[:, 0:4], qss[:, 0:4], 1.0 / 256, EPS, ALU.mult, ALU.add))
            kid1 = kid[:, :, 0:HD]
            sq1 = sq[:, 0:256].rearrange("p (t n) -> p t n", t=NT)
            link(tt(sq1, kid1, kid1, ALU.mult))
            link(nc.vector.tensor_reduce(qss[:, 4:8], sq1, X, ALU.add))
            ts(qss[:, 4:8], qss[:, 4:8], 1.0 / HD, EPS, ALU.mult, ALU.add).then_inc(head_mean, 1)
            tt(sp_part(0).rearrange("p (t n) -> p t n", t=NT), wb[:, :, 8:16],
               prm("forget_b").unsqueeze(1).broadcast_to([P, NT, 8]), ALU.add).then_inc(forget_z, 1)
            link(ts(wb[:, :, 0:8], wb[:, :, 0:8], 8 ** -0.5 * 64 ** -0.5))
            dve.wait_ge(head_root, 2)
            link(nc.vector.reciprocal(qss[:, 0:8], qss[:, 0:8]))
            link(tt(ckv, ckv, qss[:, 0:4].unsqueeze(2).broadcast_to([P, NT, 256]), ALU.mult))
            link(tt(ckv, ckv, prm("ckv_gain").unsqueeze(1).broadcast_to([P, NT, 256]), ALU.mult))
            link(tt(kid1, kid1, qss[:, 4:8].unsqueeze(2).broadcast_to([P, NT, HD]), ALU.mult))
            link(tt(kid1, kid1, prm("kidx_gain").unsqueeze(1).broadcast_to([P, NT, HD]), ALU.mult))
            rope(kid1.unsqueeze(2), 1, temps)
            rope(krd[:, :, 0:HD].unsqueeze(2), 1, temps)
            nc.vector.tensor_copy(kid[:, :, HD:P], kid1)
            nc.vector.tensor_copy(krd[:, :, HD:HD + 2 * ROT], krd[:, :, 0:2 * ROT])
            for t in range(NT):
                n = JOBS["aq"] + t
                ts(tok[:, t, 0:512], evac_to(n)[:, :], SCALE).then_inc(proj_evacuated[n % 2], 1)
            copied_all(dve, "ai", NT)
            rope(tok[:, :, 512:1024].rearrange("p t (h d) -> p t h d", d=HD), 8, temps)
            copied_all(dve, "aq", NT)
            rope(tok[:, :, 0:512].rearrange("p t (h d) -> p t h d", d=HD), 8, temps)
            dve.wait_ge(forget_ln, 1)
            link(ts(sp_part(0), sp_part(0), -1.0, 0.0, ALU.mult, ALU.max))
            tt(sp_part(2), sp_part(0), sp_part(1), ALU.add).then_inc(heads_ready, 1)
            for c in range(8 * (NT - 1)):
                t, h = c // 8 + 1, c % 8
                copied(dve, JOBS["index"] + c)
                if c >= 1:
                    dve.wait_ge(relu_used, c)
                nc.vector.scalar_tensor_tensor(out=sel[t], in0=S[c % 2][:, 0:(t + 1) * P], scalar=wb[:, t, h:h + 1],
                                               in1=cmask(t) if h == 0 else sel[t], op0=ALU.mult, op1=ALU.add)\
                    .then_inc(relu_used, 1)
            dve.wait_ge(relu_used, 8 * (NT - 1))
            top8 = small[:, 288:296]
            for t in range(1, NT):
                for _ in range(KEEP // 8):
                    link(nc.vector.max(top8, sel[t]))
                    link(nc.vector.match_replace(sel[t], top8, sel[t], TAKEN))
                link(ts(sel[t], sel[t], 0.7 * TAKEN, NEG, ALU.is_gt, ALU.mult))
            attention(first_fox, first_nsa - first_fox)
            add_to_x(JOBS["ao"])
            norm(3)
            mlp(0)

            norm(4)
            copied_all(dve, "nv", NT)
            tt(gate2, gate2, prm("gate_b").unsqueeze(1).broadcast_to([P, NT, 48]), ALU.add).then_inc(gate_ready, 1)
            for c in range(2):
                for t in range(NT):
                    n = JOBS["nq"] + NT * c + t
                    ts(tok[:, t, :].rearrange("p (j g d) -> p j g d", g=2, d=HD)[:, :, c, :],
                       evac_to(n)[:, :].rearrange("p (j d) -> p j d", d=HD), SCALE).then_inc(proj_evacuated[n % 2], 1)
            copied_all(dve, "nk", NT)
            copied_all(dve, "nq", 2 * NT)
            temps = scr.rearrange("p a n -> p (a n)")
            for col in (0, 256, 512):
                rope(kv2[:, :, col:col + P].rearrange("p t (h d) -> p t h d", d=HD), 2, temps)
            rope(tok.rearrange("p t (h d) -> p t h d", d=HD), 16, temps, heads_ready)
            dve.wait_ge(cmp_zeroed, 2)
            for s in range(2):
                for g in range(2):
                    n = JOBS["cmp"] + 1 + 2 * s + g
                    o = evac_to(n)
                    if g == s:
                        nc.vector.tensor_copy(small[:, 304 + s:305 + s], o[:, 32:33])
                    nc.vector.tensor_copy(chid[:, s, 32 * g:32 * g + N_CMP], o[:, 0:N_CMP])\
                        .then_inc(proj_evacuated[n % 2], 1)
            for c in range(2):
                copied(dve, JOBS["cmp"] + 3 + c)
            for s in range(2):
                windows = chid[:, s, :].rearrange("p (g n) -> p g n", g=2)[:, :, 0:N_CMP]
                link(ts(windows, windows, small[:, 304 + s:305 + s], None, ALU.add))
            link(tt(cpart(1), cpart(0), cpart(0), ALU.mult))
            link(ts(cpart(1), cpart(1), 0.044715, 1.0, ALU.mult, ALU.add))
            tt(cpart(1), cpart(1), cpart(0), ALU.mult).then_inc(gelu_in, 1)
            dve.wait_ge(gelu_sig, 1)
            tt(cpart(3), cpart(2), cpart(0), ALU.mult).then_inc(gelu_out, 1)
            n = JOBS["cmp"] + 6
            o = evac_to(n)
            for j in range(4):
                last = nc.vector.tensor_copy(vcBD[32 * j:32 * j + 32, :, HD * j:HD * j + HD],
                                             o[32 * j:32 * j + 32, 0:P].rearrange("p (g d) -> p g d", g=2))
            last.then_inc(proj_evacuated[n % 2], 1)
            dve.wait_ge(gate_ready, 2)
            attention(first_nsa, n_items - first_nsa)
            add_to_x(JOBS["no"])
            norm(5)
            mlp(1)
            norm(6)
            for t in range(NT):
                dve.wait_ge(rstd_ready, 7)
                nc.vector.scalar_tensor_tensor(out=tok[:, t, :], in0=x[:, t, :], scalar=rstd[:, 24 + t:25 + t],
                                               in1=prm("final"), op0=ALU.mult, op1=ALU.mult).then_inc(final_ready, 1)


_INS = ["x", "norm1_g", "w_in", "q_norm_g", "k_norm_g", "attn_sink", "conv_w", "conv_b", "w_attn_proj", "w_conv_proj",
        "w_out", "norm2_g", "w_router_group", "b_router_group", "w_router_expert", "b_router_expert", "w_gate_e",
        "w_up_e", "w_down_e", "attn_norm_2", "mlp_norm_2", "mlp_w1_2", "mlp_w2_2", "ab_w_in_2", "ab_b_forget_2",
        "a_kv_norm_2", "a_w_uk_2", "a_w_uv_2", "a_kidx_norm_2", "ab_w_out_2", "c_w_in_2", "c_b_gate_2", "c_pe_k_2",
        "c_pe_v_2", "c_cmp_k_w1_2", "c_cmp_k_w2_2", "c_cmp_v_w1_2", "c_cmp_v_w2_2", "c_w_out_2", "final_norm_2"]


def kernel(**inputs):
    import numpy as _np
    import concourse.bacc as _bacc
    from concourse import mybir as _mybir
    from concourse.bass_utils import run_bass_kernel_spmd as _run

    nc = _bacc.Bacc("TRN2", target_bir_lowering=False, num_devices=1)
    arrays, w = {}, {}
    for name in _INS:
        a = _np.ascontiguousarray(inputs[name])
        arrays[f"in_{name}"] = a
        w[name] = nc.dram_tensor(f"in_{name}", a.shape, _mybir.dt.float32, kind="ExternalInput").ap()
    arrays["in_constants"] = constants()
    w["constants"] = nc.dram_tensor("in_constants", (P, NCONST), _mybir.dt.float32, kind="ExternalInput").ap()
    out = nc.dram_tensor("out_x", (1, T, D), _mybir.dt.float32, kind="ExternalOutput").ap()
    build(nc, w, out)
    r = _run(nc, [arrays], core_ids=[0])
    return r.results[0]["out_x"]
```

```python
import concourse.bass as bass
from concourse import mybir
from concourse.alu_op_type import AluOpType as ALU
from contextlib import ExitStack
import numpy as np

F32 = mybir.dt.float32
F32R = mybir.dt.float32r
I32 = mybir.dt.int32
ACT = mybir.ActivationFunctionType
X = mybir.AxisListType.X

P = 128
T = 512
NT = T // P
D = 1024
KD = D // P
HD = 64
ROT = 8
EPS = 1e-6
NEG = -1e30
SCALE = HD ** -0.5
E = 32
G = 4
EG = E // G
F_E = 256
SPILL = 7
NB = E + SPILL
TABW = 40
F = 4096
NF = F // P
N_CMP = 31
CMP_LEN, CMP_STRIDE = 32, 16
KEEP = 128
RING = 3
BIG = 18000
SLOT = 4096
GELU_C = float((2 / np.pi) ** 0.5)
TAKEN = -3e38

CONST = {}
_at = 0
for _n, _w in (("ident", P), ("before", P), ("upto", T), ("band", 3 * P), ("causal", T), ("cmp", NT * 32),
               ("cmpok", NT), ("cos", NT * ROT), ("sin", NT * ROT), ("iota", E), ("token", NT)):
    CONST[_n] = (_at, _at + _w)
    _at += _w
NCONST = _at

GAINS = {"norm1_g": 0, "norm2_g": 8, "attn0": 16, "mlp0": 24, "attn1": 32, "mlp1": 40}
NORMS = tuple(GAINS)
CONVW, CONVB = 48, 60

PAR = {}
_at = 0
for _n, _w in (("qk_gain", 640), ("router_b", 36), ("final", D), ("sink", 8), ("forget_b", 8), ("ckv_gain", 256),
               ("kidx_gain", 64), ("gate_b", 48), ("router_w", KD * 36), ("cmp_w2", 2 * HD)):
    PAR[_n] = (_at, _at + _w)
    _at += _w
NPAR = _at


def constants():
    c = np.zeros((P, NCONST), np.float32)
    p, j = np.arange(P)[:, None], np.arange(P)[None, :]

    def put(name, a):
        c[:, CONST[name][0]:CONST[name][1]] = a

    put("ident", p == j)
    put("before", p < j)
    put("upto", np.concatenate([p <= j, np.ones((P, T - P), bool)], 1))
    band = np.zeros((P, 3 * P), np.float32)
    band[:, :P] = np.where(j >= p, 0, NEG)
    band[:, 2 * P:] = np.where(j <= p, 0, NEG)
    put("band", band)
    put("causal", np.concatenate([np.zeros((P, T - P)), np.where(j <= p, 0, NEG)], 1))
    t = (np.arange(NT)[None, :] * P + p)
    n = np.arange(32)
    ok = (n[None, None, :] * CMP_STRIDE + CMP_LEN - 1 <= t[:, :, None]) & (n < N_CMP)[None, None, :]
    put("cmp", np.where(ok, 0, NEG).reshape(P, -1))
    put("cmpok", t >= CMP_LEN - 1)
    inv = np.float32(500000.0) ** (-np.arange(0, 2 * ROT, 2, dtype=np.float32) / np.float32(2 * ROT))
    ang = t.astype(np.float32)[:, :, None] * inv.astype(np.float32)[None, None, :]
    put("cos", np.cos(ang).reshape(P, -1))
    put("sin", np.sin(ang).reshape(P, -1))
    put("iota", np.arange(E)[None, :] - 64.0 + 0 * p)
    put("token", t)
    return c


EIGHTHS = 8
UP_JOBS, DOWN_JOBS = NF // EIGHTHS, 2 * NT


def mlp_steps():
    steps, job = [], 0
    order = [("up", 0)]
    for e in range(1, EIGHTHS):
        order += [("up", e), ("down", e - 1)]
    for n, (kind, e) in enumerate(order + [("down", EIGHTHS - 1)]):
        steps.append((kind, e, job, 2 * n))
        job += UP_JOBS if kind == "up" else DOWN_JOBS
    return steps


MLP_STEPS = mlp_steps()
MLP_JOBS = EIGHTHS * (UP_JOBS + DOWN_JOBS)
MLP_PIECES = 2 * len(MLP_STEPS)

JOBS = {}
_at = 0
for _n, _w in (("vec", 1),
               ("norm0", KD), ("q", NT), ("kv", NT), ("cc", 4), ("cx", 4), ("cb", 4), ("ga", KD),
               ("turn_q", 5), ("gc", KD), ("turn_o0", 4), ("merge", 2 * KD), ("wo", 2 * NT),
               ("norm1", KD), ("logits", 1), ("ranks", 1), ("moe", 5 * NB),
               ("norm2", KD), ("ai", NT), ("ax", NT), ("aq", NT), ("bv", NT), ("turn_small", 4), ("kh", 4), ("vh", NT),
               ("turn_qi", 4), ("forget", 1), ("index", 8 * (NT - 1)), ("bq", 4), ("turn_aq", 4), ("bk", 4),
               ("turn_o1", KD), ("ao", 2 * NT),
               ("norm3", KD), ("mlp0", MLP_JOBS),
               ("norm4", KD), ("nk", NT), ("nv", NT), ("nq", 2 * NT), ("turn_nk", 6), ("cmp", 3), ("turn_nq", 8), ("cmp2", 2),
               ("turn_o2", KD), ("no", 2 * NT),
               ("norm5", KD), ("mlp1", MLP_JOBS)):
    JOBS[_n] = _at
    _at += _w


def moe_job(b, what):
    n = JOBS["moe"] + 5 * b
    last = b - (NB - 2)
    if what == "turn":
        return n - 5 if b >= 2 else JOBS["moe"] + 2 * b
    if what == "hidden":
        return n + 4 if last < 1 else n + 2
    return n + 7 if last < 0 else n + 5 if last == 0 else n + 3


def weight_plan(w):
    plan = []

    def kview(a):
        return a.rearrange("(k p) n -> p k n", p=P)

    def cols(name, a, c0, c1, last):
        plan.append((name, [(0, KD * (c1 - c0), c1 - c0, 0, c1 - c0, kview(a)[:, :, c0:c1])], last))

    def whole(name, src, last):
        plan.append((name, [(0, SLOT, SLOT // src.shape[1], 0, SLOT // src.shape[1], src)], last))

    w_in = w["w_in"][0]
    for name, c0, c1, last in (("q", 0, 512, "q+3"), ("kv", 512, 768, "kv+3"), ("cc", 1280, 1792, "cc+3"),
                               ("cx", 1792, 2304, "cx+3"), ("cb", 768, 1280, "cb+3"),
                               ("ga0", 2304, 2816, "ga+3"), ("ga1", 2816, 3328, "ga+7"),
                               ("gc0", 3328, 3840, "gc+3"), ("gc1", 3840, 4352, "gc+7")):
        cols(name, w_in, c0, c1, last)
    whole("ap", kview(w["w_attn_proj"][0]), "merge+14")
    whole("cp", kview(w["w_conv_proj"][0]), "merge+15")
    for c in range(2):
        cols(f"wo{c}", w["w_out"][0], c * 512, c * 512 + 512, f"wo+{4 * c + 3}")
    plan.append(("experts", None, None))
    ab = w["ab_w_in_2"][0]
    cols("ai", ab, 784, 1296, "ai+3")
    plan.append(("ax", [(0, KD * 352, 352, o, o + c1 - c0, kview(ab)[:, :, c0:c1])
                        for o, c0, c1 in ((0, 512, 784), (272, 1296, 1368), (344, 2904, 2912))], "ax+3"))
    cols("aq", ab, 0, 512, "aq+3")
    cols("bv", ab, 2392, 2904, "bv+3")
    cols("bq", ab, 1368, 1880, "bq+3")
    cols("bk", ab, 1880, 2392, "bk+3")
    for c in range(2):
        cols(f"ao{c}", w["ab_w_out_2"][0], c * 512, c * 512 + 512, f"ao+{4 * c + 3}")

    def mlp(l):
        down = kview(w["mlp_w2_2"][l])
        for kind, e, _, piece in MLP_STEPS:
            last = ("split", l * MLP_PIECES + piece + 2)
            if kind == "up":
                cols(f"up{l}{e}", w["mlp_w1_2"][l], e * 512, (e + 1) * 512, last)
            else:
                whole(f"down{l}{e}", down[:, e * UP_JOBS:(e + 1) * UP_JOBS, :], last)

    mlp(0)
    cw = w["c_w_in_2"][0]
    for name, c0, c1, last in (("nk", 1024, 1536, "nk+3"), ("nv", 1536, 1840, "nv+3"), ("nq0", 0, 512, "nq+3"),
                               ("nq1", 512, 1024, "nq+7")):
        cols(name, cw, c0, c1, last)
    for n, kind in enumerate("kv"):
        a = kview(w[f"c_cmp_{kind}_w1_2"][0])
        plan.append((f"w1{kind}", [(0, CMP_LEN * HD, P, 0, P, a)], f"cmp+{n + 1}"))
    for c in range(2):
        cols(f"no{c}", w["c_w_out_2"][0], c * 512, c * 512 + 512, f"no+{4 * c + 3}")
    mlp(1)
    return plan


def build(nc, w, out):
    ctx = ExitStack()
    with ctx:
        address = {}
        free = [-(-nc.sbuf_base // 64) * 64]

        def sb(name, shape):
            address[name] = free[0]
            free[0] += -(-4 * int(np.prod(shape[1:])) // 32) * 32
            return nc.alloc_sbuf_tensor_at(name, shape, F32, offset=address[name])

        def over(name, shape, under, word):
            return nc.alloc_sbuf_tensor_at(name, shape, F32R, offset=address[under] + 4 * word)

        def sem(name):
            return ctx.enter_context(nc.semaphore(name))

        rows_dram = nc.dram_tensor("rows_dram", [T, D], F32, kind="Internal").ap()
        y_dram = nc.dram_tensor("y_dram", [NB * P, D], F32, kind="Internal").ap()
        tab_dram = nc.dram_tensor("tab_dram", [P * TABW, 1], I32, kind="Internal").ap()

        x = sb("x", [P, NT, D])
        hT = sb("hT", [P, KD, T])
        tok = sb("tok", [P, NT, D])
        ring = sb("ring", [P, RING, SLOT])
        big = sb("big", [P, BIG])
        scr = sb("scr", [P, 7, T])
        const = sb("const", [P, NCONST])
        par = sb("par", [P, NPAR])
        vec_rows = sb("vec_rows", [64, P])
        vec = sb("vec", [P, 64])
        pe_rows = sb("pe_rows", [32, P])
        stat = sb("stat", [P, 3, 256])
        small = sb("small", [P, 512])
        psA = [ctx.enter_context(nc.psum_tensor(f"psA{i}", [P, 512], F32)) for i in range(2)]
        psS = [ctx.enter_context(nc.psum_tensor(f"psS{i}", [P, 512], F32)) for i in range(2)]
        psT = [ctx.enter_context(nc.psum_tensor(f"psT{i}", [P, 512], F32)) for i in range(2)]
        psO = [ctx.enter_context(nc.psum_tensor(f"psO{i}", [P, 512], F32)) for i in range(2)]

        def cst(name):
            return const[:, CONST[name][0]:CONST[name][1]]

        def prm(name):
            return par[:, PAR[name][0]:PAR[name][1]]

        ident = cst("ident")
        upto = cst("upto")
        ones = upto[:, P:2 * P]
        earlier = cst("before")
        iota = cst("iota")
        cos4 = cst("cos").rearrange("p (t c) -> p t c", c=ROT)
        sin4 = cst("sin").rearrange("p (t c) -> p t c", c=ROT)
        negm, sums, fac = stat[:, 0, :], stat[:, 1, :], stat[:, 2, :]

        def carve(sizes):
            at, got = 0, {}
            for name, n in sizes:
                got[name] = big[:, at:at + n]
                at += n
            assert at <= BIG, at
            return got

        a1 = carve((("qk", 2560), ("v", 512), ("qT", 2048), ("kT", 512), ("u", 2056), ("conv", 2048),
                    ("ga", 4096), ("gc", 4096)))
        qk = a1["qk"].rearrange("p (t n) -> p t n", t=NT)
        v1 = a1["v"].rearrange("p (t n) -> p t n", t=NT)
        qT1 = a1["qT"].rearrange("p (j n) -> p j n", j=4)
        kT1 = a1["kT"]
        u = a1["u"].rearrange("p (m n) -> p m n", m=4)
        conv = a1["conv"].rearrange("p (m n) -> p m n", m=4)
        ga = a1["ga"].rearrange("p (m n) -> p m n", m=KD)
        gc = a1["gc"].rearrange("p (m n) -> p m n", m=KD)
        attnT = a1["qk"][:, 0:2048].rearrange("p (c n) -> p c n", c=4)
        moe_parts = (("logit", 144), ("w1", 512), ("w2", 512), ("w3", 512), ("oh1", 128), ("oh2", 128), ("asg", 128),
                    ("rank", 128), ("cnt", 32), ("spill", 32), ("incl", 32), ("obase", 32), ("s", 256), ("xg", 2048),
                    ("xT", 2048), ("sg", 512), ("hid", 512), ("hidT", 512), ("y", 2048), ("picked", NT * D))
        a2 = carve(moe_parts)
        a3 = carve((("bv", 2048), ("bqT", 2048), ("bkT", 2048), ("aqT", 2048), ("kiT", 512), ("krT", 512),
                    ("ckvT", 1024), ("wb", 64), ("sel", 1152), ("kh", 2048), ("vh", 2048),
                    ("ncum", 512), ("sp", 96)))
        a4 = carve((("qT", 4096), ("kv", 3072), ("kT2", 1024), ("win", 3072), ("gate", 192), ("kcT", 32), ("vcBD", 512),
                    ("hid", 512), ("cmpst", 512)))
        hT_hi = over("hT_hi", [P, KD, T], "hT", 0)
        hT_lo = over("hT_lo", [P, KD, T], "big", 0)
        w_hi = [over(f"w_hi{i}", [P, 2048], "big", 4096 + 2048 * i) for i in range(2)]
        w_lo = [over(f"w_lo{i}", [P, 2048], "big", 8192 + 2048 * i) for i in range(2)]
        hid_hi = [over(f"hid_hi{i}", [P, UP_JOBS, T], *at) for i, at in enumerate((("tok", 0), ("big", 12288)))]
        hid_lo = [over(f"hid_lo{i}", [P, UP_JOBS, T], *at) for i, at in enumerate((("tok", 2048), ("big", 14336)))]

        x_loaded = sem("x_loaded")
        const_loaded = sem("const_loaded")
        w_arrived = [sem(f"w_arrived{i}") for i in range(RING)]
        proj_ready = sem("proj_ready")
        proj_evacuated = [sem(f"proj_evacuated{i}") for i in range(2)]
        sumsq_ready = sem("sumsq_ready")
        mean_ready = sem("mean_ready")
        root_ready = sem("root_ready")
        rstd_ready = sem("rstd_ready")
        normed = sem("normed")
        head_mean = sem("head_mean")
        head_root = sem("head_root")
        heads_ready = sem("heads_ready")
        scores_ready = sem("scores_ready")
        masked = sem("masked")
        probs_ready = sem("probs_ready")
        turned = sem("turned")
        turned_copied = sem("turned_copied")
        values_ready = sem("values_ready")
        inverted = sem("inverted")
        factor_ready = sem("factor_ready")
        out_taken = [sem(f"out_taken{i}") for i in range(2)]
        normed_hi = sem("normed_hi")
        weight_hi = sem("weight_hi")
        weight_lo = sem("weight_lo")
        squared = sem("squared")
        hidden_hi = sem("hidden_hi")
        hidden_lo = sem("hidden_lo")
        logits_shifted = sem("logits_shifted")
        logits_exp = sem("logits_exp")
        assigned = sem("assigned")
        slots_ready = sem("slots_ready")
        table_zeroed = sem("table_zeroed")
        zeros_made = sem("zeros_made")
        rows_stored = sem("rows_stored")
        scattered = sem("scattered")
        table_loaded = sem("table_loaded")
        gathered = [sem(f"gathered{i}") for i in range(2)]
        gu_ready = sem("gu_ready")
        gu_taken = sem("gu_taken")
        silu_ready = sem("silu_ready")
        y_written = [sem(f"y_written{i}") for i in range(2)]
        picked = [sem(f"picked{i}") for i in range(NT)]
        combined = sem("combined")
        forget_z = sem("forget_z")
        forget_ln = sem("forget_ln")
        relu_used = sem("relu_used")
        gate_ready = sem("gate_ready")
        gelu_in = sem("gelu_in")
        gelu_sig = sem("gelu_sig")
        gelu_out = sem("gelu_out")
        final_ready = sem("final_ready")
        stored = sem("stored")
        merged = sem("merged")
        gu_arrived = [sem(f"gu_arrived{i}") for i in range(2)]
        dn_arrived = [sem(f"dn_arrived{i}") for i in range(2)]
        hidden_part = sem("hidden_part")
        latent_zeroed = sem("latent_zeroed")
        latent_weights = sem("latent_weights")
        cmp_zeroed = sem("cmp_zeroed")
        dve_chain = sem("dve_chain")
        act_chain = sem("act_chain")

        block = ctx.enter_context(nc.Block())

        items = []

        band, causal = cst("band"), cst("causal")
        for j in range(4):
            for g in range(2):
                for t in range(NT):
                    lo, hi = max(0, t - 1), min(NT - 1, t + 1)
                    n = (hi - lo + 1) * P
                    items.append(dict(kind="band", head=4 * g + j, t=t, n=n, blocks=list(range(lo, hi + 1)),
                                      mask=band[:, (lo - t + 1) * P:(lo - t + 1) * P + n],
                                      scores=[(qT1[64 * g:64 * g + 64, j, t * P:(t + 1) * P],
                                               kT1[64 * g:64 * g + 64, lo * P:lo * P + n])],
                                      values=v1[:, :, 64 * g:64 * g + 64]))
        n_band = len(items)

        bv = a3["bv"].rearrange("p (t n) -> p t n", t=NT)
        bqT = a3["bqT"].rearrange("p (j n) -> p j n", j=4)
        bkT = a3["bkT"].rearrange("p (j n) -> p j n", j=4)
        aqT = a3["aqT"].rearrange("p (j n) -> p j n", j=4)
        qiT = bqT
        ckvT = a3["ckvT"].rearrange("p (m n) -> p m n", m=2)
        ckv = a3["sel"][:, 0:1024].rearrange("p (t n) -> p t n", t=NT)
        khT = a3["kh"].rearrange("p (j n) -> p j n", j=4)
        vh = a3["vh"].rearrange("p (t n) -> p t n", t=NT)
        wuv = a3["aqT"][:, 1024:2048].rearrange("p (m n) -> p m n", m=2)
        ncum = a3["ncum"]
        wb = a3["wb"].rearrange("p (t n) -> p t n", t=NT)
        sel = {1: a3["sel"][:, 0:256], 2: a3["sel"][:, 256:640], 3: a3["sel"][:, 640:1152]}

        def cmask(t):
            return causal[:, T - (t + 1) * P:T]

        for h in range(8):
            for t in range(NT):
                r = 64 * (h % 2)
                n = (t + 1) * P
                items.append(dict(kind="fox", head=8 + h, t=t, n=n, blocks=list(range(t + 1)), mask=cmask(t),
                                  scores=[(bqT[r:r + 64, h // 2, t * P:(t + 1) * P], bkT[r:r + 64, h // 2, 0:n]),
                                          (ident[:, h:h + 1].broadcast_to([P, P]), ncum[:, 0:n])],
                                  values=bv[:, :, 64 * h:64 * h + 64]))

        for h in range(8):
            for t in range(NT):
                r = 64 * (h % 2)
                n = (t + 1) * P
                items.append(dict(kind="latent", head=h, t=t, n=n, blocks=list(range(t + 1)),
                                  mask=cmask(t) if t == 0 else sel[t],
                                  scores=[(aqT[r:r + 64, h // 2, t * P:(t + 1) * P], khT[r:r + 64, h // 2, 0:n])],
                                  values=vh[:, :, 64 * h:64 * h + 64]))
        first_fox, first_nsa = n_band, n_band + 16 * NT

        qT2 = a4["qT"].rearrange("p (j n) -> p j n", j=8)
        kv2 = a4["kv"].rearrange("p (t n) -> p t n", t=NT)
        kT2 = a4["kT2"].rearrange("p (s n) -> p s n", s=2)
        win = a4["win"].rearrange("p (s g n) -> p s g n", s=2, g=3)
        gate2 = a4["gate"].rearrange("p (t n) -> p t n", t=NT)
        kcT = a4["kcT"]
        vcBD = a4["vcBD"].rearrange("p (g n) -> p g n", g=2)
        chid = a4["hid"].rearrange("p (s n) -> p s n", s=8)
        cmpmask = cst("cmp").rearrange("p (t n) -> p t n", t=NT)
        cmpok = cst("cmpok")
        cmpst = a4["cmpst"].rearrange("p (i n) -> p i n", n=8)
        for g in range(2):
            for t in range(NT):
                items.append(dict(kind="cmp", g=g, t=t, n=256, blocks=[0, 1], index=len(items) - first_nsa))
        first_pair = len(items)
        for h in range(16):
            g, j = h // 8, h % 8
            for branch in range(2):
                for t in range(NT):
                    n = (t + 1) * P
                    items.append(dict(kind="pair", head=h, branch=branch, t=t, n=n, blocks=list(range(t + 1)), mask=cmask(t),
                                      gate=gate2[:, t, h * 3 + 1 + branch:h * 3 + 2 + branch],
                                      scores=[(qT2[64 * g:64 * g + 64, j, t * P:(t + 1) * P],
                                               kT2[64 * g:64 * g + 64, branch, 0:n])],
                                      values=kv2[:, :, 64 * g + (640 if branch else 384):64 * g + (704 if branch else 448)]))
        n_items = len(items)
        kiT, krT = a3["kiT"], a3["krT"]
        S, PR, PT = ([scr[:, i, :] for i in at] for at in ((0, 1), (2, 3, 4), (5, 6)))

        yrow = small[:, 0:8].bitcast(I32)
        trow = small[:, 8:16].bitcast(I32)
        spill_expert = small[:, 16:24].bitcast(I32)
        token_id = small[:, 24:28].bitcast(I32)
        slot_token = small[:, 32:32 + TABW].bitcast(I32)
        zeros_i = small[:, 80:80 + TABW].bitcast(I32)
        g12 = small[:, 120:128].rearrange("p (k t) -> p k t", k=2)
        ss = small[:, 128:160]
        rstd = small[:, 160:192]
        qss = small[:, 192:232]
        negsink = small[:, 240:248]
        esink = small[:, 256:288]
        xg = a2["xg"].rearrange("p (b n) -> p b n", b=2)
        xT = a2["xT"].rearrange("p (b k n) -> p b k n", b=2, k=KD)
        sg = a2["sg"].rearrange("p (b n) -> p b n", b=2)
        ehid = a2["hid"].rearrange("p (b n) -> p b n", b=2)
        ehidT = a2["hidT"].rearrange("p (b n) -> p b n", b=2)
        ey = a2["y"].rearrange("p (b n) -> p b n", b=2)
        at_oh = sum(n for _, n in moe_parts[:[k for k, _ in moe_parts].index("oh1")])
        at = sum(n for _, n in moe_parts[:[k for k, _ in moe_parts].index("xg")])
        rows_of = [a2["picked"].rearrange("p (t n) -> p t n", t=NT),
                   big[:, at:at + NT * D].rearrange("p (t n) -> p t n", t=NT)]
        krd = scr[:, 2, :].rearrange("p (t n) -> p t n", t=NT)
        kid = scr[:, 3, :].rearrange("p (t n) -> p t n", t=NT)
        wuk = a3["aqT"][:, 0:1024].rearrange("p (m h d) -> p m h d", m=2, h=8)
        asg = a2["asg"].rearrange("p (t n) -> p t n", t=NT)
        gexp, pexp = a2["w1"][:, 32:48], a2["s"][:, 24:28]
        sp_terms = a3["sp"][:, 64:96].rearrange("p (t n) -> p t n", t=NT)

        def sp_part(k):
            return a3["sp"][:, 32 * k:32 * k + 32]

        def cpart(k):
            return a4["hid"][:, 128 * k:128 * k + 128]

        def rows(a):
            return a.rearrange("(k p) -> k p", p=P)

        def everywhere(a):
            return a.partition_broadcast(P)

        def heads(a, n):
            return a.unsqueeze(0).unsqueeze(0).broadcast_to([P, n, HD])

        qk_gain = prm("qk_gain").rearrange("p (h d) -> p h d", d=HD)
        router_w3 = prm("router_w").rearrange("p (k n) -> p k n", k=KD)
        loads = [(const[:, :], w["constants"]),
                 (vec_rows[0:8, :], rows(w["norm1_g"][0])), (vec_rows[8:16, :], rows(w["norm2_g"][0])),
                 (vec_rows[16:24, :], rows(w["attn_norm_2"][0])), (vec_rows[24:32, :], rows(w["mlp_norm_2"][0])),
                 (vec_rows[32:40, :], rows(w["attn_norm_2"][1])), (vec_rows[40:48, :], rows(w["mlp_norm_2"][1])),
                 (vec_rows[CONVB:CONVB + 4, :], rows(w["conv_b"][0])),
                 (pe_rows[:, 0:HD], w["c_pe_k_2"][0]), (pe_rows[:, HD:P], w["c_pe_v_2"][0]),
                 (qk_gain[:, 0:8, :], heads(w["q_norm_g"][0], 8)), (qk_gain[:, 8:10, :], heads(w["k_norm_g"][0], 2)),
                 (prm("router_b")[:, 0:G], everywhere(w["b_router_group"][0])),
                 (prm("router_b")[:, G:G + E], everywhere(w["b_router_expert"][0])),
                 (prm("final"), everywhere(w["final_norm_2"])), (prm("sink"), everywhere(w["attn_sink"][0])),
                 (prm("forget_b"), everywhere(w["ab_b_forget_2"][0])),
                 (prm("ckv_gain"), everywhere(w["a_kv_norm_2"][0])),
                 (prm("kidx_gain"), everywhere(w["a_kidx_norm_2"][0])), (prm("gate_b"), everywhere(w["c_b_gate_2"][0])),
                 (router_w3[:, :, 0:G], w["w_router_group"][0].rearrange("(k p) n -> p k n", p=P)),
                 (router_w3[:, :, G:G + E], w["w_router_expert"][0].rearrange("(k p) n -> p k n", p=P)),
                 (prm("cmp_w2")[:, 0:HD], w["c_cmp_k_w2_2"][0]), (prm("cmp_w2")[:, HD:2 * HD], w["c_cmp_v_w2_2"][0])]
        for j in range(3):
            loads.append((vec_rows[CONVW + 4 * j:CONVW + 4 * j + 4, :], rows(w["conv_w"][0][j])))
        CONST_LOADS = len(loads)

        plan = weight_plan(w)
        names = [name for name, _, _ in plan]
        experts_at = names.index("experts")
        in_ring = [n for n in names if n != "experts"]
        slot_of = {n: i % RING for i, n in enumerate(in_ring)}
        gu_slot = [experts_at % RING, (experts_at + 1) % RING]
        dn_slot = (experts_at + 2) % RING
        arrived_at, total = {}, [0] * RING
        for name, pieces, _ in plan:
            if name != "experts":
                total[slot_of[name]] += 16 * len(pieces)
                arrived_at[name] = total[slot_of[name]]

        def slot(name):
            return ring[:, slot_of[name], :]

        gu = [ring[:, i, :].rearrange("p (k n) -> p k n", k=KD) for i in gu_slot]
        dn = [ring[:, dn_slot, p * 2048:(p + 1) * 2048].rearrange("p (k n) -> p k n", k=2) for p in range(2)]

        def last_use(last):
            if isinstance(last, str):
                name, n = last.split("+")
                return proj_ready, JOBS[name] + int(n) + 1
            return weight_lo, last[1]

        def product(eng, n, i=0):
            eng.wait_ge(proj_ready, i * 10 + (n + 1))

        def copied(eng, n, i=0):
            eng.wait_ge(proj_evacuated[n % 2], i * 5 + (n // 2 + 1))

        def copied_all(eng, name, count):
            for n in range(max(0, count - 2), count):
                copied(eng, JOBS[name] + n)

        def bank(n):
            return psA[n % 2]

        def raw_piece(l, c):
            kind, e, _, _ = MLP_STEPS[c // 2]
            name = f"{kind}{l}{e}"
            k = KD if kind == "up" else UP_JOBS
            half = SLOT // k // 2
            return slot(name).rearrange("p (k n) -> p k n", k=k)[:, :, (c % 2) * half:(c % 2 + 1) * half], name, k

        def piece_used(eng, l, c):
            if c >= 2:
                kind, _, job, piece = MLP_STEPS[(c - 2) // 2]
                per = UP_JOBS if kind == "up" else DOWN_JOBS
                product(eng, JOBS[f"mlp{l}"] + job + (per // 2) * (c % 2 + 1) - 1)

        def shifted(n, dst, copy, eng):
            product(eng, n)
            copy(dst[0:HD, :], bank(n)[0:HD, :])
            copy(dst[HD:P, 0:T - 1], bank(n)[HD:P, 1:T]).then_inc(proj_evacuated[n % 2], 1)

        def moe_pairs(eng, expert_block):
            for b in range(4):
                expert_block(b % 2, b // 2)
            with eng.Fori(2, (NB - 1) // 2) as i:
                for p in range(2):
                    expert_block(p, i)
            expert_block(0, (NB - 1) // 2, last=True)

        def moe_product(p, i, what, ahead=0):
            if isinstance(i, int):
                return moe_job(2 * i + p + ahead, what) - 10 * i
            return JOBS["moe"] + 5 * (p + ahead) + {"turn": -5, "hidden": 4, "down": 7}[what]

        def before(p, i, least):
            return isinstance(i, int) and 2 * i + p < least

        @block.sync
        def _(sp):
            sp.dma_start(x[:, :, :], w["x"][0].rearrange("(t p) d -> p t d", p=P)).then_inc(x_loaded, 16)
            held = {}

            def load_block(p, e):
                for o, a in ((0, w["w_gate_e"]), (F_E, w["w_up_e"])):
                    src = a[0][bass.ds(e, 1)].rearrange("e (k p) n -> p (e k) n", p=P)
                    sp.dma_start(gu[p][:, :, o:o + F_E], src).then_inc(gu_arrived[p], 16)

            def load_down(p, e):
                src = w["w_down_e"][0][bass.ds(e, 1)].rearrange("e (k p) n -> p (e k) n", p=P)
                sp.dma_start(dn[p], src).then_inc(dn_arrived[p], 16)

            def experts():
                def gate_up(p, i, e):
                    if not before(p, i, 2):
                        sp.wait_ge(gu_ready, i * 2 + (p - 1))
                    load_block(p, e)

                def down(p, i, e):
                    if not before(p, i, 2):
                        product(sp, moe_product(p, i, "down", -2) + 1, i)
                    load_down(p, e)

                for p in range(2):
                    sp.wait_ge(*held[gu_slot[p]])
                    gate_up(p, 0, p)
                sp.wait_ge(*held[dn_slot])
                down(0, 0, 0)
                for p in range(2):
                    gate_up(p, 1, 2 + p)
                    down(1 - p, p, 1 + p)
                with sp.Fori(2, E // 2) as i:
                    for p in range(2):
                        gate_up(p, i, i * 2 + p)
                        if p == 0:
                            product(sp, moe_product(1, i, "down", -4) + 1, i)
                        else:
                            product(sp, moe_product(0, i, "down", -2) + 1, i)
                        load_down(1 - p, i * 2 + (p - 1))
                sp.wait_ge(slots_ready, 2)

                def expert_of(b):
                    if b < E:
                        return b
                    return sp.value_load(spill_expert[0:1, b - E:b - E + 1], min_val=0, max_val=E - 1)

                for b in range(E, NB + 1):
                    if b < NB:
                        gate_up(b % 2, b // 2, expert_of(b))
                    down((b - 1) % 2, (b - 1) // 2, expert_of(b - 1))
                held[gu_slot[(NB - 1) % 2]] = (gu_ready, NB)
                held[gu_slot[NB % 2]] = (gu_ready, NB - 1)
                held[dn_slot] = (proj_ready, moe_job(NB - 1, "down") + 2)

            for name, pieces, last in plan:
                if name == "experts":
                    experts()
                    continue
                s = slot_of[name]
                if s in held:
                    sp.wait_ge(*held[s])
                for piece in pieces:
                    first, words, width, c0, c1, src = piece
                    dst = ring[:, s, first:first + words].rearrange("p (k n) -> p k n", n=width)[:, :, c0:c1]
                    sp.dma_start(dst, src).then_inc(w_arrived[s], 16)
                held[s] = last_use(last)
            sp.wait_ge(final_ready, NT)
            sp.dma_start(out[0].rearrange("(t p) d -> p t d", p=P), tok[:, :, :]).then_inc(stored, 16)
            sp.wait_ge(stored, 16)

        @block.gpsimd
        def _(pool):
            nc.gpsimd.memset(zeros_i.bitcast(F32), 0.0).then_inc(zeros_made, 1)
            pool.wait_ge(zeros_made, 1)
            pool.dma_start(tab_dram.rearrange("(p n) o -> p (n o)", p=P), zeros_i).then_inc(table_zeroed, 16)
            pool.wait_ge(table_zeroed, 16)
            pool.wait_ge(slots_ready, 1)
            for c in range(2 * NT):
                pool.indirect_dma_start(tab_dram[:, :], bass.IndirectOffsetOnAxis(ap=trow[:, c:c + 1], axis=0),
                                        token_id[:, c % NT:c % NT + 1], None).then_inc(scattered, 16)
            pool.wait_ge(scattered, 2 * NT * 16)
            pool.dma_start(slot_token, tab_dram.rearrange("(p n) o -> p (n o)", p=P)).then_inc(table_loaded, 16)
            pool.wait_ge(table_loaded, 16)
            pool.wait_ge(rows_stored, 16)
            for b in range(NB):
                if b >= 2:
                    product(pool, moe_job(b - 2, "turn") + 1)
                pool.indirect_dma_start(xg[:, b % 2, :], None, rows_dram[:, :],
                                        bass.IndirectOffsetOnAxis(ap=slot_token[:, b:b + 1], axis=0))\
                    .then_inc(gathered[b % 2], 16)
            for p in range(2):
                pool.wait_ge(y_written[p], 16 * ((NB + 1 - p) // 2))
            for t in range(NT):
                for k in range(2):
                    c = k * NT + t
                    pool.indirect_dma_start(rows_of[k][:, t, :], None, y_dram[:, :],
                                            bass.IndirectOffsetOnAxis(ap=yrow[:, c:c + 1], axis=0))\
                        .then_inc(picked[t], 16)
            pool.wait_ge(combined, NT)
            nc.gpsimd.memset(wuk.rearrange("p m h d -> p (m h d)"), 0.0).then_inc(latent_zeroed, 1)
            nc.gpsimd.memset(scr[:, 2, :], 0.0).then_inc(latent_zeroed, 1)
            nc.gpsimd.memset(ncum, 0.0).then_inc(latent_zeroed, 1)
            pool.wait_ge(latent_zeroed, 3)
            for m in range(2):
                pool.dma_start(wuk[:, m, :, 2 * ROT:HD], w["a_w_uk_2"][0][m * P:(m + 1) * P])\
                    .then_inc(latent_weights, 16)
            pool.dma_start(wuv[:, :, :], w["a_w_uv_2"][0].rearrange("(m p) h d -> p m (h d)", p=P))\
                .then_inc(latent_weights, 16)
            product(pool, JOBS["mlp0"] + MLP_JOBS - 1)
            nc.gpsimd.memset(vcBD.rearrange("p g n -> p (g n)"), 0.0).then_inc(cmp_zeroed, 1)
            nc.gpsimd.memset(a4["hid"], 0.0).then_inc(cmp_zeroed, 1)
            nc.gpsimd.memset(win[:, :, 2, :], 0.0).then_inc(cmp_zeroed, 1)

        @block.tensor
        def _(pe):
            def need(name):
                pe.wait_ge(w_arrived[slot_of[name]], arrived_at[name])

            def begin(n, i=0):
                if isinstance(i, int) and n // 2 + 5 * i <= 0:
                    return bank(n)
                pe.wait_ge(proj_evacuated[n % 2], i * 5 + n // 2)
                return bank(n)

            def turn(n, sources, i=0):
                o = begin(n, i)
                for c, a in enumerate(sources):
                    k = a.shape[0]
                    ins = pe.transpose(o[:, c * P:c * P + k], a, ident[0:k, 0:k])
                ins.then_inc(proj_ready, 1)

            def token_major(first, name, width, src=hT):
                need(name)
                s = slot(name)
                for t in range(NT):
                    o = begin(first + t)
                    for k in range(KD):
                        ins = pe.matmul(o[:, 0:width], src[:, k, t * P:(t + 1) * P], s[:, k * width:(k + 1) * width],
                                        start=(k == 0), stop=(k == KD - 1))
                    ins.then_inc(proj_ready, 1)

            def feature_major(first, name, some=range(4)):
                need(name)
                s = slot(name)
                for m in some:
                    o = begin(first + m)
                    for k in range(KD):
                        ins = pe.matmul(o[:, :], s[:, k * 512 + m * P:k * 512 + (m + 1) * P], hT[:, k, :],
                                        start=(k == 0), stop=(k == KD - 1))
                    ins.then_inc(proj_ready, 1)

            def norm(n):
                pe.wait_ge(normed, NT * (n + 1))
                for k in range(KD):
                    turn(JOBS[f"norm{n}"] + k, [tok[:, t, k * P:(k + 1) * P] for t in range(NT)])
                copied_all(pe, f"norm{n}", KD)

            def attention(first, count, meanwhile=None):
                for i in range(first, first + count + 3):
                    if i == first + 2 and meanwhile:
                        meanwhile()
                    if i < first + count:
                        it = items[i]
                        if i >= 2:
                            pe.wait_ge(masked, i - 1)
                        o = psS[i % 2]
                        if it["kind"] == "cmp":
                            g = it["g"]
                            for j in range(8):
                                ins = pe.matmul(o[:, j * 32:(j + 1) * 32],
                                                qT2[64 * g:64 * g + 64, j, it["t"] * P:(it["t"] + 1) * P],
                                                kcT[64 * g:64 * g + 64, 0:32], start=True, stop=True)
                        else:
                            for c, (a, b) in enumerate(it["scores"]):
                                ins = pe.matmul(o[:, 0:it["n"]], a, b, start=(c == 0),
                                                stop=(c == len(it["scores"]) - 1))
                        ins.then_inc(scores_ready, 1)
                    k = i - 2
                    if first <= k < first + count:
                        pe.wait_ge(probs_ready, k + 1)
                        if k >= 2:
                            pe.wait_ge(turned_copied, k - 1)
                        for b in range(len(items[k]["blocks"])):
                            ins = pe.transpose(psT[k % 2][:, b * P:(b + 1) * P], PR[k % 3][:, b * P:(b + 1) * P], ident)
                        ins.then_inc(turned, 1)
                    k = i - 3
                    if first <= k < first + count:
                        it = items[k]
                        pe.wait_ge(turned_copied, k + 1)
                        if k >= 2:
                            pe.wait_ge(out_taken[k % 2], k // 2)
                        o, pt = psO[k % 2], PT[k % 2]
                        nb = len(it["blocks"])
                        if it["kind"] == "cmp":
                            for b in range(2):
                                ins = pe.matmul(o[:, b * 256:(b + 1) * 256], pt[:, b * P:(b + 1) * P],
                                                vcBD[:, it["g"], :], start=True, stop=True)
                        else:
                            for b, kb in enumerate(it["blocks"]):
                                ins = pe.matmul(o[:, 0:HD], pt[:, b * P:(b + 1) * P], it["values"][:, kb, :],
                                                start=(b == 0), stop=(b == nb - 1))
                        ins.then_inc(values_ready, 1)

            def attended(count):
                for k in (count - 2, count - 1):
                    pe.wait_ge(out_taken[k % 2], k // 2 + 1)

            def out_projection(n, first, name):
                for k in range(KD):
                    turn(JOBS[f"turn_o{n}"] + k, [tok[:, t, k * P:(k + 1) * P] for t in range(NT)])
                copied_all(pe, f"turn_o{n}", KD)
                for c in range(2):
                    token_major(first + NT * c, f"{name}{c}", 512)

            def split_product(o, terms):
                n = 0
                for a_hi, a_lo, b_hi, b_lo in terms:
                    for a, b in ((a_hi, b_hi), (a_hi, b_lo), (a_lo, b_hi)):
                        n += 1
                        ins = pe.matmul(o, a, b, start=(n == 1), stop=(n == 3 * len(terms)))
                ins.then_inc(proj_ready, 1)

            def mlp(l):
                for kind, e, job, piece in MLP_STEPS:
                    for half in range(2):
                        c = piece + half
                        pe.wait_ge(weight_lo, l * MLP_PIECES + c + 1)
                        pe.wait_ge(weight_hi, l * MLP_PIECES + c + 1)
                        if kind == "up":
                            wh, wl = (a[c % 2][:, :].rearrange("p (k n) -> p k n", k=KD) for a in (w_hi, w_lo))
                            for f in range(2):
                                split_product(begin(JOBS[f"mlp{l}"] + job + 2 * half + f)[:, :],
                                              [(wh[:, k, f * P:(f + 1) * P], wl[:, k, f * P:(f + 1) * P],
                                                hT_hi[:, k, :], hT_lo[:, k, :]) for k in range(KD)])
                        else:
                            pe.wait_ge(hidden_lo, l * NF + (e + 1) * UP_JOBS)
                            pe.wait_ge(hidden_hi, l * NF + (e + 1) * UP_JOBS)
                            wh, wl = (a[c % 2][:, :].rearrange("p (k n) -> p k n", k=UP_JOBS) for a in (w_hi, w_lo))
                            for t in range(NT):
                                split_product(begin(JOBS[f"mlp{l}"] + job + NT * half + t)[:, :],
                                              [(hid_hi[e % 2][:, k, t * P:(t + 1) * P], hid_lo[e % 2][:, k, t * P:(t + 1) * P],
                                                wh[:, k, :], wl[:, k, :]) for k in range(UP_JOBS)])

            pe.wait_ge(const_loaded, CONST_LOADS * 16)
            turn(JOBS["vec"], [vec_rows[:, :]])
            copied(pe, JOBS["vec"])
            norm(0)
            token_major(JOBS["q"], "q", 512)
            token_major(JOBS["kv"], "kv", 256)
            feature_major(JOBS["cc"], "cc")
            feature_major(JOBS["cx"], "cx")
            feature_major(JOBS["cb"], "cb")
            for c in range(2):
                feature_major(JOBS["ga"] + 4 * c, f"ga{c}")
            pe.wait_ge(heads_ready, 1)
            for j in range(5):
                turn(JOBS["turn_q"] + j, [qk[:, t, j * P:(j + 1) * P] for t in range(NT)])
            copied_all(pe, "turn_q", 5)

            def conv_gates():
                for c in range(2):
                    feature_major(JOBS["gc"] + 4 * c, f"gc{c}")

            attention(0, n_band, conv_gates)
            attended(n_band)
            for c in range(4):
                turn(JOBS["turn_o0"] + c, [tok[:, t, c * P:(c + 1) * P] for t in range(NT)])
            copied_all(pe, "turn_o0", 4)
            copied_all(pe, "gc", KD)
            need("ap")
            need("cp")
            for m in range(KD):
                for c, (name, src) in enumerate((("ap", attnT), ("cp", conv))):
                    n = JOBS["merge"] + 2 * m + c
                    o = begin(n)
                    for k in range(4):
                        ins = pe.matmul(o[:, :], slot(name)[:, k * D + m * P:k * D + (m + 1) * P], src[:, k, :],
                                        start=(k == 0), stop=(k == 3))
                    ins.then_inc(proj_ready, 1)
            pe.wait_ge(merged, KD)
            for c in range(2):
                token_major(JOBS["wo"] + NT * c, f"wo{c}", 512)

            norm(1)
            n = JOBS["logits"]
            o = begin(n)
            router_w = prm("router_w").rearrange("p (k n) -> p k n", k=KD)
            for t in range(NT):
                for k in range(KD):
                    ins = pe.matmul(o[:, t * 36:(t + 1) * 36], hT[:, k, t * P:(t + 1) * P], router_w[:, k, :],
                                    start=(k == 0), stop=(k == KD - 1))
            ins.then_inc(proj_ready, 1)
            n = JOBS["ranks"]
            o = begin(n)
            pe.wait_ge(assigned, 1)
            rank3 = o[:, 0:(NT + 1) * E].rearrange("p (t n) -> p t n", n=E)
            pe.matmul(o[:, 0:P], earlier, asg, start=True, stop=False)
            for s in range(NT - 1):
                pe.matmul(rank3[:, s + 1:NT, :], ones, asg[:, s:s + 1, :].broadcast_to([P, NT - 1 - s, E]), start=False,
                          stop=(s == NT - 2))
            for s in range(NT):
                ins = pe.matmul(rank3[:, NT, :], ones, asg[:, s, :], start=(s == 0), stop=(s == NT - 1))
            ins.then_inc(proj_ready, 1)

            def turn_rows(p, i, n, count):
                pe.wait_ge(gathered[p], count * 16)
                for c in range(2):
                    turn(n + c, [xg[:, p, (4 * c + k) * P:(4 * c + k + 1) * P] for k in range(4)], i)

            def down(p, i, ahead):
                q = (p + ahead) % 2
                hidn, n = moe_product(p, i, "hidden", ahead), moe_product(p, i, "down", ahead)
                copied(pe, hidn, i)
                pe.wait_ge(dn_arrived[q], i * 16 + 16 * ((p + ahead) // 2 + 1))
                for half in range(2):
                    o = begin(n + half, i)
                    for k in range(2):
                        ins = pe.matmul(o[:, :], ehidT[:, q, k * P:(k + 1) * P], dn[q][:, k, half * 512:(half + 1) * 512],
                                        start=(k == 0), stop=(k == 1))
                    ins.then_inc(proj_ready, 1)

            def hidden(p, i, ahead):
                pe.wait_ge(gu_taken, i * 2 + (p + ahead + 1))
                turn(moe_product(p, i, "hidden", ahead), [ehid[:, (p + ahead) % 2, k * P:(k + 1) * P] for k in range(2)], i)

            def expert_block(p, i, last=False):
                turns = moe_product(p, i, "turn")
                if not before(p, i, 1):
                    hidden(p, i, -1)
                pe.wait_ge(gu_arrived[p], i * 32 + 32)
                for m in range(2):
                    copied(pe, turns + m, i)
                if not before(p, i, 2):
                    pe.wait_ge(gu_taken, i * 2 + (p - 1))
                for k in range(KD):
                    if k == KD // 2 and not last:
                        turn_rows(1 - p, i, moe_product(p, i, "turn", 1), i + (1 + p))
                    ins = pe.matmul(psS[p][:, :], xT[:, p, k, :], gu[p][:, k, :], start=(k == 0), stop=(k == KD - 1))
                ins.then_inc(gu_ready, 1)
                if not before(p, i, 1):
                    down(p, i, -1)
                if last:
                    hidden(p, i, 0)
                    down(p, i, 0)

            turn_rows(0, 0, moe_job(0, "turn"), 1)
            moe_pairs(pe, expert_block)

            norm(2)
            token_major(JOBS["ai"], "ai", 512)
            token_major(JOBS["ax"], "ax", 352)
            token_major(JOBS["aq"], "aq", 512)
            token_major(JOBS["bv"], "bv", 512)
            pe.wait_ge(heads_ready, 2)
            turn(JOBS["turn_small"], [kid[:, t, :] for t in range(NT)])
            turn(JOBS["turn_small"] + 1, [krd[:, t, :] for t in range(NT)])
            for m in range(2):
                turn(JOBS["turn_small"] + 2 + m, [ckv[:, t, m * P:(m + 1) * P] for t in range(NT)])
            copied_all(pe, "turn_small", 4)
            pe.wait_ge(latent_weights, 48)
            for j in range(4):
                o = begin(JOBS["kh"] + j)
                for m in range(2):
                    ins = pe.matmul(o[:, :], wuk[:, m, 2 * j:2 * j + 2, :].rearrange("p h d -> p (h d)"), ckvT[:, m, :],
                                    start=(m == 0), stop=(m == 1))
                ins.then_inc(proj_ready, 1)
            for t in range(NT):
                o = begin(JOBS["vh"] + t)
                for m in range(2):
                    ins = pe.matmul(o[:, :], ckvT[:, m, t * P:(t + 1) * P], wuv[:, m, :], start=(m == 0), stop=(m == 1))
                ins.then_inc(proj_ready, 1)
            for j in range(4):
                turn(JOBS["turn_qi"] + j, [tok[:, t, 512 + j * P:512 + (j + 1) * P] for t in range(NT)])
            o = begin(JOBS["forget"])
            for t in range(NT):
                ins = pe.matmul(o[0:8, t * P:T], sp_terms[:, t, :], upto[:, 0:T - t * P], start=(t == 0),
                                stop=(t == NT - 1))
            ins.then_inc(proj_ready, 1)
            copied_all(pe, "turn_qi", 4)
            for t in range(1, NT):
                for h in range(8):
                    n, r = JOBS["index"] + 8 * (t - 1) + h, 64 * (h % 2)
                    pe.matmul(begin(n)[:, 0:(t + 1) * P], qiT[r:r + 64, h // 2, t * P:(t + 1) * P],
                              kiT[r:r + 64, 0:(t + 1) * P], start=True, stop=True).then_inc(proj_ready, 1)
            feature_major(JOBS["bq"], "bq")
            for j in range(4):
                turn(JOBS["turn_aq"] + j, [tok[:, t, j * P:(j + 1) * P] for t in range(NT)])
            feature_major(JOBS["bk"], "bk", range(1))
            copied(pe, JOBS["bk"])

            def further_keys():
                feature_major(JOBS["bk"], "bk", range(1, 4))
                copied_all(pe, "bk", 4)

            attention(first_fox, first_nsa - first_fox, further_keys)
            attended(first_nsa)
            out_projection(1, JOBS["ao"], "ao")
            norm(3)
            mlp(0)

            norm(4)
            token_major(JOBS["nk"], "nk", 512)
            token_major(JOBS["nv"], "nv", 304)
            for c in range(2):
                token_major(JOBS["nq"] + NT * c, f"nq{c}", 512)
            def turn_twice(n, sources):
                o = begin(n)
                for c, a in enumerate(sources):
                    k = a.shape[0]
                    for half in range(2):
                        ins = pe.matmul(o[HD * half:HD * (half + 1), c * P:c * P + k], a, ident[0:k, 0:k],
                                        start=True, stop=True)
                ins.then_inc(proj_ready, 1)

            pe.wait_ge(heads_ready, 3)
            for c in range(4):
                s, g = c // 2, c % 2
                turn_twice(JOBS["turn_nk"] + c, [kv2[:, t, P * s + HD * g:P * s + HD * (g + 1)] for t in range(NT)])
            for c, col in enumerate((256, 512)):
                turn(JOBS["turn_nk"] + 4 + c, [kv2[:, t, col:col + P] for t in range(NT)])
            turn_twice(JOBS["cmp"], [pe_rows[:, HD * s:HD * (s + 1)] for s in range(2)])
            copied_all(pe, "turn_nk", 6)
            copied(pe, JOBS["cmp"])
            for s, kind in enumerate("kv"):
                need("w1" + kind)
                w1 = slot("w1" + kind)
                o = begin(JOBS["cmp"] + 1 + s)
                for j in range(CMP_LEN // 2):
                    ins = pe.matmul(o[:, 0:3 * N_CMP], w1[:, j * P:(j + 1) * P],
                                    win[:, s, :, 2 * j:2 * j + CMP_STRIDE * (N_CMP - 1) + 1:CMP_STRIDE],
                                    start=(j == 0), stop=(j == CMP_LEN // 2 - 1))
                ins.then_inc(proj_ready, 1)
            pe.wait_ge(heads_ready, 4)
            for j in range(8):
                turn(JOBS["turn_nq"] + j, [tok[:, t, j * P:(j + 1) * P] for t in range(NT)])
            pe.wait_ge(gelu_out, 1)
            cmp_w2 = prm("cmp_w2").rearrange("p (s n) -> p s n", s=2)
            o = begin(JOBS["cmp2"])
            for g in range(2):
                ins = pe.matmul(o[64 * g:64 * g + 64, 0:32], cmp_w2[:, 0, :], chid[:, 6, 32 * g:32 * g + 32],
                                start=True, stop=True)
            ins.then_inc(proj_ready, 1)
            o = begin(JOBS["cmp2"] + 1)
            for j in range(4):
                for g in range(2):
                    ins = pe.matmul(o[32 * j:32 * j + 32, 64 * g:64 * g + 64], chid[:, 7, 32 * g:32 * g + 32],
                                    cmp_w2[:, 1, :], start=True, stop=True)
            ins.then_inc(proj_ready, 1)
            for c in range(2):
                copied(pe, JOBS["cmp2"] + c)
            attention(first_nsa, n_items - first_nsa)
            attended(n_items)
            out_projection(2, JOBS["no"], "no")
            norm(5)
            mlp(1)

        @block.scalar
        def _(act):
            chain = [0]

            def link(ins):
                chain[0] += 1
                ins.then_inc(act_chain, 1)
                act.wait_ge(act_chain, chain[0])

            def A(o, i, f, **kw):
                return nc.scalar.activation(o, i, f, **kw)

            def evac(n, o, width=512, f=ACT.Copy, **kw):
                product(act, n)
                A(o, bank(n)[:, 0:width], f, **kw).then_inc(proj_evacuated[n % 2], 1)

            def norm(n):
                c = slice(NT * n, NT * n + NT)
                for t in range(NT):
                    A(tok[:, t, :], x[:, t, :], ACT.Square, accum_out=ss[:, NT * n + t:NT * n + t + 1])\
                        .then_inc(sumsq_ready, 1)
                act.wait_ge(mean_ready, n + 1)
                A(rstd[:, c], ss[:, c], ACT.Sqrt).then_inc(root_ready, 1)
                if n == len(NORMS):
                    return
                act.wait_ge(rstd_ready, n + 1)
                for t in range(NT):
                    A(tok[:, t, :], x[:, t, :], ACT.Copy, scale=rstd[:, NT * n + t:NT * n + t + 1]).then_inc(normed, 1)
                if n == 1:
                    act.wait_ge(normed, NT * 2)
                    act.dma_start(rows_dram.rearrange("(t p) d -> p t d", p=P), tok[:, :, :]).then_inc(rows_stored, 16)
                if n in (3, 5):
                    for k in range(KD):
                        g = GAINS[NORMS[n]] + k
                        product(act, JOBS[f"norm{n}"] + k)
                        A(hT_hi[:, k, :], bank(JOBS[f"norm{n}"] + k)[:, :], ACT.Copy, scale=vec[:, g:g + 1]).then_inc(normed_hi, 1)
                    return
                for k in range(1, KD, 2):
                    g = GAINS[NORMS[n]] + k
                    evac(JOBS[f"norm{n}"] + k, hT[:, k, :], scale=vec[:, g:g + 1])

            def attention(first, count, meanwhile=None):
                for i in range(first, first + count + 2):
                    if i == first + 2 and meanwhile:
                        meanwhile()
                    k = i - 2
                    if first <= k < first + count:
                        act.wait_ge(turned, k + 1)
                        if k >= 2:
                            act.wait_ge(values_ready, k - 1)
                        n = P * len(items[k]["blocks"])
                        A(PT[k % 2][:, 0:n], psT[k % 2][:, 0:n], ACT.Copy).then_inc(turned_copied, 1)
                    if i < first + count:
                        it = items[i]
                        act.wait_ge(masked, i + 1)
                        if i >= 3:
                            act.wait_ge(turned, i - 2)
                            if items[i - 3]["kind"] == "cmp":
                                act.wait_ge(factor_ready, i - 2)
                        if it["kind"] == "cmp":
                            A(PR[i % 3][:, 0:256], S[i % 2][:, 0:256], ACT.Exp).then_inc(probs_ready, 1)
                        else:
                            if it["kind"] == "band":
                                A(esink[:, i:i + 1], prm("sink")[:, it["head"]:it["head"] + 1], ACT.Exp,
                                  bias=negm[:, i:i + 1])
                            A(PR[i % 3][:, 0:it["n"]], S[i % 2][:, 0:it["n"]], ACT.Exp, bias=negm[:, i:i + 1],
                              scale=-1.0, accum_out=sums[:, i:i + 1]).then_inc(probs_ready, 1)

            def split_weight(l, c):
                if c >= MLP_PIECES:
                    return
                raw, name, k = raw_piece(l, c)
                act.wait_ge(w_arrived[slot_of[name]], arrived_at[name])
                piece_used(act, l, c)
                A(w_hi[c % 2][:, :].rearrange("p (k n) -> p k n", k=k), raw, ACT.Copy).then_inc(weight_hi, 1)

            def mlp(l):
                for kind, e, job, piece in MLP_STEPS:
                    for half in range(2):
                        if kind == "up":
                            for f in range(2 * half, 2 * half + 2):
                                nth = l * NF + e * UP_JOBS + f
                                n = JOBS[f"mlp{l}"] + job + f
                                product(act, n)
                                if nth >= 2:
                                    act.wait_ge(hidden_lo, nth - 1)
                                A(S[f % 2], bank(n)[:, :], ACT.Relu).then_inc(proj_evacuated[n % 2], 1)
                                copied(act, n)
                                A(hid_hi[e % 2][:, f, :], S[f % 2], ACT.Square).then_inc(hidden_hi, 1)
                        split_weight(l, piece + half + 2)

            for dst, src in loads:
                act.dma_start(dst, src).then_inc(const_loaded, 16)
            act.wait_ge(const_loaded, CONST_LOADS * 16)
            evac(JOBS["vec"], vec[:, :], 64)
            copied(act, JOBS["vec"])

            act.wait_ge(x_loaded, 16)
            norm(0)
            for t in range(NT):
                n = JOBS["kv"] + t
                product(act, n)
                A(qk[:, t, 512:640], bank(n)[:, 0:P], ACT.Copy)
                A(v1[:, t, :], bank(n)[:, P:2 * P], ACT.Copy).then_inc(proj_evacuated[n % 2], 1)
            for m in range(4):
                evac(JOBS["cc"] + m, u[:, m, 1:T + 1])
            act.wait_ge(head_mean, 1)
            A(qss[:, 0:40], qss[:, 0:40], ACT.Sqrt).then_inc(head_root, 1)
            for m in range(KD):
                evac(JOBS["ga"] + m, ga[:, m, :], f=ACT.Sigmoid)
            for j in range(5):
                evac(JOBS["turn_q"] + j, qT1[:, j, :] if j < 4 else kT1)

            def conv_gates():
                for m in range(KD):
                    evac(JOBS["gc"] + m, gc[:, m, :], f=ACT.Sigmoid)

            attention(0, n_band, conv_gates)
            for c in range(4):
                evac(JOBS["turn_o0"] + c, attnT[:, c, :])

            copied_all(act, "wo", 2 * NT)
            norm(1)
            act.wait_ge(logits_shifted, 1)
            A(gexp, gexp, ACT.Exp).then_inc(logits_exp, 1)
            A(pexp, pexp, ACT.Exp).then_inc(logits_exp, 1)

            def hidden_out(p, i, ahead):
                n = moe_product(p, i, "hidden", ahead)
                product(act, n, i)
                A(ehidT[:, (p + ahead) % 2, :], bank(n)[:, 0:F_E], ACT.Copy).then_inc(proj_evacuated[n % 2], 1)

            def outputs(p, i, ahead):
                q, nth = (p + ahead) % 2, (p + ahead) // 2
                n = moe_product(p, i, "down", ahead)
                if not before(p, i, 2 - ahead):
                    act.wait_ge(y_written[q], i * 16 + 16 * nth)
                for half in range(2):
                    product(act, n + half, i)
                    A(ey[:, q, half * 512:(half + 1) * 512], bank(n + half)[:, :], ACT.Copy)\
                        .then_inc(proj_evacuated[(n + half) % 2], 1)

            def store(p, i, ahead):
                q, n = (p + ahead) % 2, moe_product(p, i, "down", ahead)
                for half in range(2):
                    copied(act, n + half, i)
                row = i * (2 * P) + (p + ahead) * P
                act.dma_start(y_dram[bass.ds(row, P), :], ey[:, q, :]).then_inc(y_written[q], 16)

            def expert_block(p, i, last=False):
                if not before(p, i, 1):
                    hidden_out(p, i, -1)
                if not before(p, i, 2):
                    store(p, i, -2)
                act.wait_ge(gu_ready, i * 2 + (p + 1))
                if not before(p, i, 2):
                    act.wait_ge(gu_taken, i * 2 + (p - 1))
                A(sg[:, p, :], psS[p][:, 0:F_E], ACT.Sigmoid).then_inc(silu_ready, 1)
                if not before(p, i, 1):
                    outputs(p, i, -1)
                if last:
                    hidden_out(p, i, 0)
                    store(p, i, -1)
                    outputs(p, i, 0)
                    store(p, i, 0)

            moe_pairs(act, expert_block)

            act.wait_ge(combined, NT)
            norm(2)
            for t in range(NT):
                n = JOBS["ax"] + t
                product(act, n)
                if t == 0:
                    act.wait_ge(latent_zeroed, 3)
                o = bank(n)
                A(ckv[:, t, :], o[:, 0:256], ACT.Copy)
                A(krd[:, t, 0:2 * ROT], o[:, 256:272], ACT.Copy)
                A(kid[:, t, 0:HD], o[:, 272:336], ACT.Copy)
                A(wb[:, t, :], o[:, 336:352], ACT.Copy).then_inc(proj_evacuated[n % 2], 1)
            act.wait_ge(head_mean, 2)
            A(qss[:, 0:8], qss[:, 0:8], ACT.Sqrt).then_inc(head_root, 1)
            act.wait_ge(forget_z, 1)
            link(A(sp_part(1), sp_part(0), ACT.Abs))
            link(A(sp_part(1), sp_part(1), ACT.Exp, scale=-1.0))
            A(sp_part(1), sp_part(1), ACT.Ln, bias=1.0).then_inc(forget_ln, 1)
            for t in range(NT):
                evac(JOBS["bv"] + t, bv[:, t, :])
            evac(JOBS["turn_small"], kiT)
            evac(JOBS["turn_small"] + 1, krT)
            for m in range(2):
                evac(JOBS["turn_small"] + 2 + m, ckvT[:, m, :])
            for t in range(NT):
                evac(JOBS["vh"] + t, vh[:, t, :])
            for j in range(4):
                evac(JOBS["turn_qi"] + j, qiT[:, j, :])
            n = JOBS["forget"]
            product(act, n)
            A(ncum[0:8, :], bank(n)[0:8, :], ACT.Copy).then_inc(proj_evacuated[n % 2], 1)
            for c in range(8 * (NT - 1)):
                if c >= 2:
                    act.wait_ge(relu_used, c - 1)
                n = (c // 8 + 2) * P
                evac(JOBS["index"] + c, S[c % 2][:, 0:n], n, ACT.Relu)
            for m in range(4):
                evac(JOBS["bq"] + m, bqT[:, m, :], scale=SCALE)
            for j in range(4):
                evac(JOBS["turn_aq"] + j, aqT[:, j, :])
            evac(JOBS["bk"], bkT[:, 0, :])

            def further_keys():
                for m in range(1, 4):
                    evac(JOBS["bk"] + m, bkT[:, m, :])

            attention(first_fox, first_nsa - first_fox, further_keys)
            for k in range(KD):
                evac(JOBS["turn_o1"] + k, hT[:, k, :])
            for c in range(2):
                split_weight(0, c)
            copied_all(act, "ao", 2 * NT)
            norm(3)
            mlp(0)

            copied_all(act, "mlp0", MLP_JOBS)
            norm(4)
            for t in range(NT):
                evac(JOBS["nk"] + t, kv2[:, t, 0:512])
            for t in range(NT):
                n = JOBS["nv"] + t
                product(act, n)
                A(kv2[:, t, 512:768], bank(n)[:, 0:256], ACT.Copy)
                A(gate2[:, t, :], bank(n)[:, 256:304], ACT.Copy).then_inc(proj_evacuated[n % 2], 1)
            act.wait_ge(gate_ready, 1)
            A(a4["gate"], a4["gate"], ACT.Sigmoid).then_inc(gate_ready, 1)
            for g in range(2):
                shifted(JOBS["turn_nk"] + g, win[:, 0, g, :], lambda o, i: A(o, i, ACT.Copy), act)
            for c in range(2):
                evac(JOBS["turn_nk"] + 4 + c, kT2[:, c, :])
            n = JOBS["cmp"]
            product(act, n)
            act.wait_ge(cmp_zeroed, 3)
            for s in range(2):
                A(win[0:HD, s, 2, 0:CMP_LEN], bank(n)[0:HD, s * P:s * P + CMP_LEN], ACT.Copy)
                ins = A(win[HD:P, s, 2, 0:CMP_LEN - 1], bank(n)[HD:P, s * P + 1:s * P + CMP_LEN], ACT.Copy)
            ins.then_inc(proj_evacuated[n % 2], 1)
            for j in range(4):
                evac(JOBS["turn_nq"] + j, qT2[:, j, :])
            act.wait_ge(gelu_in, 1)
            A(cpart(2), cpart(1), ACT.Sigmoid, scale=2 * GELU_C).then_inc(gelu_sig, 1)
            for j in range(4, 8):
                evac(JOBS["turn_nq"] + j, qT2[:, j, :])
            evac(JOBS["cmp2"], kcT, 32)
            attention(first_nsa, n_items - first_nsa)
            for k in range(KD):
                evac(JOBS["turn_o2"] + k, hT[:, k, :])
            for c in range(2):
                split_weight(1, c)
            copied_all(act, "no", 2 * NT)
            norm(5)
            mlp(1)
            copied_all(act, "mlp1", MLP_JOBS)
            norm(6)

        @block.vector
        def _(dve):
            chain = [0]

            def link(ins):
                chain[0] += 1
                ins.then_inc(dve_chain, 1)
                dve.wait_ge(dve_chain, chain[0])

            def tt(o, a, b, op):
                return nc.vector.tensor_tensor(o, a, b, op)

            def ts(o, a, s1, s2=None, op0=ALU.mult, op1=None):
                if op1 is None:
                    return nc.vector.tensor_scalar(o, a, s1, None, op0)
                return nc.vector.tensor_scalar(o, a, s1, s2, op0, op1)

            def evac_to(n):
                product(dve, n)
                return bank(n)

            def norm(n):
                c = slice(NT * n, NT * n + NT)
                dve.wait_ge(sumsq_ready, NT * (n + 1))
                ts(ss[:, c], ss[:, c], 1.0 / D, EPS, ALU.mult, ALU.add).then_inc(mean_ready, 1)
                dve.wait_ge(root_ready, n + 1)
                nc.vector.reciprocal(rstd[:, c], rstd[:, c]).then_inc(rstd_ready, 1)
                if n == len(NORMS):
                    return
                if n in (3, 5):
                    for k in range(KD):
                        g, j = GAINS[NORMS[n]] + k, JOBS[f"norm{n}"] + k
                        dve.wait_ge(normed_hi, KD * (n // 2 - 1) + k + 1)
                        nc.vector.scalar_tensor_tensor(out=hT_lo[:, k, :], in0=evac_to(j)[:, :], scalar=vec[:, g:g + 1],
                                                       in1=hT_hi[:, k, :].bitcast(F32), op0=ALU.mult, op1=ALU.subtract)\
                            .then_inc(proj_evacuated[j % 2], 1)
                    return
                for k in range(0, KD, 2):
                    g, j = GAINS[NORMS[n]] + k, JOBS[f"norm{n}"] + k
                    ts(hT[:, k, :], evac_to(j)[:, :], vec[:, g:g + 1]).then_inc(proj_evacuated[j % 2], 1)

            def add_to_x(first):
                for c in range(2):
                    for t in range(NT):
                        n = first + NT * c + t
                        o = evac_to(n)
                        xs = x[:, t, c * 512:(c + 1) * 512]
                        tt(xs, o[:, :], xs, ALU.add).then_inc(proj_evacuated[n % 2], 1)

            def rope(view, heads, temps, signal=None):
                x1, x2 = view[:, :, :, 0:ROT], view[:, :, :, ROT:2 * ROT]
                shape = [P, NT, heads, ROT]
                n = NT * heads * ROT
                t1, t2, t3, t4 = (temps[:, k * n:(k + 1) * n].rearrange("p (t h c) -> p t h c", t=NT, h=heads)
                                  for k in range(4))
                c, s = cos4.unsqueeze(2).broadcast_to(shape), sin4.unsqueeze(2).broadcast_to(shape)
                tt(t1, x1, c, ALU.mult)
                tt(t2, x2, s, ALU.mult)
                tt(t3, x2, c, ALU.mult)
                link(tt(t4, x1, s, ALU.mult))
                tt(x1, t1, t2, ALU.subtract)
                if signal is None:
                    link(tt(x2, t3, t4, ALU.add))
                else:
                    tt(x2, t3, t4, ALU.add).then_inc(signal, 1)

            def attention(first, count, meanwhile=None):
                for i in range(first, first + count + 3):
                    if i < first + count:
                        it = items[i]
                        dve.wait_ge(scores_ready, i + 1)
                        if i >= 2:
                            dve.wait_ge(probs_ready, i - 1)
                        if it["kind"] == "cmp":
                            s3 = S[i % 2][:, 0:256].rearrange("p (j n) -> p j n", j=8)
                            st = cmpst[:, it["index"], :]
                            link(tt(s3, psS[i % 2][:, 0:256].rearrange("p (j n) -> p j n", j=8),
                                    cmpmask[:, it["t"], :].unsqueeze(1).broadcast_to([P, 8, 32]), ALU.add))
                            link(nc.vector.tensor_reduce(st, s3, X, ALU.max))
                            tt(s3, s3, st.unsqueeze(2).broadcast_to([P, 8, 32]), ALU.subtract).then_inc(masked, 1)
                        else:
                            floor = negsink[:, it["head"]:it["head"] + 1] if it["kind"] == "band" else 3e38
                            nc.vector.tensor_tensor_reduce(
                                out=S[i % 2][:, 0:it["n"]], in0=psS[i % 2][:, 0:it["n"]], in1=it["mask"], scale=-1.0,
                                scalar=floor, op0=ALU.add, op1=ALU.min, accum_out=negm[:, i:i + 1]).then_inc(masked, 1)
                    k = i - 2
                    if first <= k < first + count:
                        factor(k)
                    k = i - 3
                    if first <= k < first + count:
                        finish(k)
                    k = i - 2
                    if first <= k < first + count and items[k]["kind"] == "pair":
                        gate_factor(k)
                    if meanwhile:
                        meanwhile(i - first)

            def factor(k):
                it, t = items[k], items[k]["t"]
                f, total = fac[:, k:k + 1], sums[:, k:k + 1]
                dve.wait_ge(probs_ready, k + 1)
                if it["kind"] == "cmp":
                    st, g = cmpst[:, it["index"], :], it["g"]
                    link(nc.vector.tensor_reduce(st, PR[k % 3][:, 0:256].rearrange("p (j n) -> p j n", j=8), X, ALU.add))
                    link(nc.vector.reciprocal(st, st))
                    nc.vector.scalar_tensor_tensor(
                        out=st, in0=st, scalar=cmpok[:, t:t + 1],
                        in1=gate2[:, t, g * 24:g * 24 + 24].rearrange("p (j r) -> p j r", r=3)[:, :, 0],
                        op0=ALU.mult, op1=ALU.mult).then_inc(factor_ready, 1)
                elif it["kind"] == "pair":
                    nc.vector.reciprocal(f, total).then_inc(inverted, 1)
                else:
                    if it["kind"] == "band":
                        link(tt(total, total, esink[:, k:k + 1], ALU.add))
                    nc.vector.reciprocal(f, total).then_inc(factor_ready, 1)

            def gate_factor(k):
                f = fac[:, k:k + 1]
                dve.wait_ge(inverted, k - first_pair + 1)
                tt(f, f, items[k]["gate"], ALU.mult).then_inc(factor_ready, 1)

            def finish(k):
                it, t = items[k], items[k]["t"]
                f, o = fac[:, k:k + 1], psO[k % 2]
                dve.wait_ge(values_ready, k + 1)
                dve.wait_ge(factor_ready, k + 1)
                if it["kind"] == "cmp":
                    st, g = cmpst[:, it["index"], :], it["g"]
                    tt(tok[:, t, g * 512:(g + 1) * 512].rearrange("p (j d) -> p j d", d=HD),
                       o[:, :].rearrange("p (j d) -> p j d", d=HD), st.unsqueeze(2).broadcast_to([P, 8, HD]),
                       ALU.mult).then_inc(out_taken[k % 2], 1)
                    return
                dst = tok[:, t, it["head"] * HD:(it["head"] + 1) * HD]
                if it["kind"] == "pair":
                    before_k = k - NT if it["branch"] else first_nsa + (it["head"] // 8) * NT + t
                    dve.wait_ge(out_taken[before_k % 2], before_k // 2 + 1)
                    nc.vector.scalar_tensor_tensor(out=dst, in0=o[:, 0:HD], scalar=f, in1=dst, op0=ALU.mult,
                                                   op1=ALU.add).then_inc(out_taken[k % 2], 1)
                else:
                    ts(dst, o[:, 0:HD], f).then_inc(out_taken[k % 2], 1)

            def split_weight(l, c):
                if c >= MLP_PIECES:
                    return
                raw, _, k = raw_piece(l, c)
                piece_used(dve, l, c)
                dve.wait_ge(weight_hi, l * MLP_PIECES + c + 1)
                tt(w_lo[c % 2][:, :].rearrange("p (k n) -> p k n", k=k), raw,
                   w_hi[c % 2][:, :].rearrange("p (k n) -> p k n", k=k).bitcast(F32), ALU.subtract).then_inc(weight_lo, 1)

            def mlp(l):
                for kind, e, job, piece in MLP_STEPS:
                    for half in range(2):
                        c = piece + half
                        if kind == "up":
                            if c >= 1:
                                split_weight(l, c + 1)
                            for f in range(2 * half, 2 * half + 2):
                                nth = l * NF + e * UP_JOBS + f
                                dve.wait_ge(hidden_hi, nth + 1)
                                tt(PR[f % 2], S[f % 2], S[f % 2], ALU.mult).then_inc(squared, 1)
                                dve.wait_ge(squared, nth + 1)
                                tt(hid_lo[e % 2][:, f, :], PR[f % 2], hid_hi[e % 2][:, f, :].bitcast(F32), ALU.subtract)\
                                    .then_inc(hidden_lo, 1)
                        else:
                            for t in range(NT):
                                if t == NT // 2:
                                    split_weight(l, c + 1)
                                n = JOBS[f"mlp{l}"] + job + NT * half + t
                                xs = x[:, t, half * 512:(half + 1) * 512]
                                tt(xs, evac_to(n)[:, :], xs, ALU.add).then_inc(proj_evacuated[n % 2], 1)

            nc.vector.memset(u[:, :, 0:T + 2:T + 1], 0.0)
            dve.wait_ge(const_loaded, CONST_LOADS * 16)
            copied(dve, JOBS["vec"])
            link(ts(negsink, prm("sink"), -1.0))
            norm(0)
            for t in range(NT):
                n = JOBS["q"] + t
                o = evac_to(n)
                nc.vector.tensor_copy(qk[:, t, 0:512].rearrange("p (j g d) -> p j g d", j=4, g=2),
                                      o[:, :].rearrange("p (g j d) -> p j g d", j=4, g=2))\
                    .then_inc(proj_evacuated[n % 2], 1)
            copied_all(dve, "q", NT)
            copied_all(dve, "kv", NT)
            qk4 = qk.rearrange("p t (h d) -> p (t h) d", d=HD)
            sq4 = tok[:, :, 0:640].rearrange("p t (h d) -> p t h d", d=HD)
            qss3 = qss[:, 0:40].rearrange("p (t h) -> p t h", t=NT)
            for t in range(NT):
                last = tt(tok[:, t, 0:640], qk[:, t, :], qk[:, t, :], ALU.mult)
            link(last)
            link(nc.vector.tensor_reduce(qss3, sq4, X, ALU.add))
            ts(qss[:, 0:40], qss[:, 0:40], 1.0 / HD, EPS, ALU.mult, ALU.add).then_inc(head_mean, 1)
            for m in range(4):
                n = JOBS["cx"] + m
                o = evac_to(n)
                copied(dve, JOBS["cc"] + m)
                tt(u[:, m, 1:T + 1], o[:, :], u[:, m, 1:T + 1], ALU.mult).then_inc(proj_evacuated[n % 2], 1)
            copied_all(dve, "cx", 4)
            for m in range(4):
                cw = [vec[:, CONVW + 4 * j + m:CONVW + 4 * j + m + 1] for j in range(3)]
                cb = vec[:, CONVB + m:CONVB + m + 1]
                link(ts(conv[:, m, :], u[:, m, 0:T], cw[0], cb, ALU.mult, ALU.add))
                for j in (1, 2):
                    link(nc.vector.scalar_tensor_tensor(out=conv[:, m, :], in0=u[:, m, j:j + T], scalar=cw[j],
                                                        in1=conv[:, m, :], op0=ALU.mult, op1=ALU.add))
                n = JOBS["cb"] + m
                o = evac_to(n)
                tt(conv[:, m, :], o[:, :], conv[:, m, :], ALU.mult).then_inc(proj_evacuated[n % 2], 1)
            dve.wait_ge(head_root, 1)
            link(nc.vector.reciprocal(qss[:, 0:40], qss[:, 0:40]))
            link(ts(qss3[:, :, 0:8], qss3[:, :, 0:8], SCALE))
            link(tt(qk4, qk4, qss[:, 0:40].unsqueeze(2).broadcast_to([P, 40, HD]), ALU.mult))
            link(tt(qk, qk, prm("qk_gain").unsqueeze(1).broadcast_to([P, NT, 640]), ALU.mult))
            rope(qk.rearrange("p t (h d) -> p t h d", d=HD), 10, scr.rearrange("p a n -> p (a n)"),
                 heads_ready)
            attention(0, n_band)
            for m in range(KD):
                for c, gate in enumerate((ga, gc)):
                    n = JOBS["merge"] + 2 * m + c
                    o = evac_to(n)
                    tt(gate[:, m, :], o[:, :], gate[:, m, :], ALU.mult).then_inc(proj_evacuated[n % 2], 1)
                for c in range(2):
                    copied(dve, JOBS["merge"] + 2 * m + c)
                tt(hT[:, m, :], ga[:, m, :], gc[:, m, :], ALU.add).then_inc(merged, 1)
            add_to_x(JOBS["wo"])

            norm(1)
            logit = a2["logit"].rearrange("p (t n) -> p t n", t=NT)
            n = JOBS["logits"]
            o = evac_to(n)
            tt(logit, o[:, 0:NT * 36].rearrange("p (t n) -> p t n", t=NT),
               prm("router_b").unsqueeze(1).broadcast_to([P, NT, 36]), ALU.add).then_inc(proj_evacuated[n % 2], 1)
            copied(dve, n)
            gl, el = logit[:, :, 0:G], logit[:, :, G:36]

            def bc(a, shape):
                return a.unsqueeze(2).broadcast_to(shape)

            def first_max(values, width, best, work, hot):
                shape = [P, NT, width]
                link(nc.vector.tensor_reduce(best, values, X, ALU.max))
                link(tt(work, values, bc(best, shape), ALU.is_equal))
                link(tt(work, work, iota[:, 0:width].unsqueeze(1).broadcast_to(shape), ALU.mult))
                link(nc.vector.tensor_reduce(where, work, X, ALU.min))
                link(tt(hot, iota[:, 0:width].unsqueeze(1).broadcast_to(shape), bc(where, shape), ALU.is_equal))

            def s4(k):
                return a2["s"][:, 4 * k:4 * k + 4]

            where, gbest, best1, best2, den, pick = (s4(k) for k in range(6))
            g16 = a2["w1"][:, 0:16].rearrange("p (t n) -> p t n", t=NT)
            hot_g = a2["w1"][:, 16:32].rearrange("p (t n) -> p t n", t=NT)
            work = a2["w2"][:, 0:128].rearrange("p (t n) -> p t n", t=NT)
            inside = a2["w3"][:, 0:128].rearrange("p (t n) -> p t n", t=NT)
            oh = [a2[k].rearrange("p (t n) -> p t n", t=NT) for k in ("oh1", "oh2")]
            first_max(gl, G, gbest, g16, hot_g)
            link(tt(gexp.rearrange("p (t n) -> p t n", t=NT), gl, bc(gbest, [P, NT, G]), ALU.subtract))
            link(ts(g16, hot_g, -1.0, -NEG, ALU.add, ALU.mult))
            link(tt(inside.rearrange("p t (g e) -> p t g e", g=G), el.rearrange("p t (g e) -> p t g e", g=G),
                    g16.unsqueeze(3).broadcast_to([P, NT, G, EG]), ALU.add))
            first_max(inside, E, best1, work, oh[0])
            link(ts(work, oh[0], NEG))
            link(tt(inside, inside, work, ALU.add))
            first_max(inside, E, best2, work, oh[1])
            nc.vector.tensor_copy(token_id, cst("token"))
            tt(asg, oh[0], oh[1], ALU.add).then_inc(assigned, 1)
            tt(pexp, best2, best1, ALU.subtract).then_inc(logits_shifted, 1)
            dve.wait_ge(logits_exp, 2)
            link(nc.vector.tensor_reduce(den, gexp.rearrange("p (t n) -> p t n", t=NT), X, ALU.add))
            link(ts(pick, pexp, 1.0, None, ALU.add))
            link(tt(den, den, pick, ALU.mult))
            link(nc.vector.reciprocal(g12[:, 0, :], den))
            link(tt(g12[:, 1, :], g12[:, 0, :], pexp, ALU.mult))
            n = JOBS["ranks"]
            o = evac_to(n)
            rank = a2["rank"].rearrange("p (t n) -> p t n", t=NT)
            cnt, spill, incl, obase = a2["cnt"], a2["spill"], a2["incl"], a2["obase"]
            nc.vector.tensor_copy(a2["rank"], o[:, 0:P])
            nc.vector.tensor_copy(cnt, o[:, P:P + E]).then_inc(proj_evacuated[n % 2], 1)
            copied(dve, n)

            def over(dst, src, tmp, strict):
                op = ALU.is_gt if strict else ALU.is_ge
                link(ts(dst, src, float(P), None, op))
                for k in (2, 3):
                    link(ts(tmp, src, float(k * P), None, op))
                    link(tt(dst, dst, tmp, ALU.add))

            w2_32 = a2["w2"][:, 128:160]
            over(spill, cnt, w2_32, True)
            link(nc.vector.memset(a2["w2"][:, 160:192], 1.0))
            link(nc.vector.tensor_tensor_scan(incl, a2["w2"][:, 160:192], spill, 0.0, ALU.mult, ALU.add))
            link(tt(obase, incl, spill, ALU.subtract))
            link(ts(obase, obase, float(E - 1), None, ALU.add))
            rk, ek, ob, q, tmp, blk, row = (a2["s"][:, 32 + 8 * j:40 + 8 * j] for j in range(7))
            shape = [P, 2, NT, E]
            both = big[:, at_oh:at_oh + 2 * NT * E].rearrange("p (k t n) -> p k t n", k=2, t=NT)
            work4 = a2["w3"][:, 0:256].rearrange("p (k t n) -> p k t n", k=2, t=NT)
            work8 = a2["w3"][:, 0:256].rearrange("p (c n) -> p c n", n=E)

            def each(a):
                return a.unsqueeze(1).unsqueeze(1).broadcast_to(shape)

            link(tt(work4, both, rank.unsqueeze(1).broadcast_to(shape), ALU.mult))
            link(nc.vector.tensor_reduce(rk, work8, X, ALU.add))
            link(tt(work4, both, each(iota), ALU.mult))
            link(nc.vector.tensor_reduce(ek, work8, X, ALU.add))
            link(tt(work4, both, each(obase), ALU.mult))
            link(nc.vector.tensor_reduce(ob, work8, X, ALU.add))
            link(ts(ek, ek, 64.0, None, ALU.add))
            over(q, rk, tmp, False)
            link(tt(blk, ob, q, ALU.add))
            link(tt(blk, blk, ek, ALU.subtract))
            link(ts(tmp, q, 0.0, None, ALU.is_gt))
            link(tt(blk, blk, tmp, ALU.mult))
            link(tt(blk, blk, ek, ALU.add))
            link(nc.vector.scalar_tensor_tensor(out=row, in0=q, scalar=-float(P), in1=rk, op0=ALU.mult, op1=ALU.add))
            link(nc.vector.scalar_tensor_tensor(out=tmp, in0=row, scalar=float(TABW), in1=blk, op0=ALU.mult, op1=ALU.add))
            nc.vector.tensor_copy(trow, tmp).then_inc(slots_ready, 1)
            dve.wait_ge(slots_ready, 1)
            link(nc.vector.scalar_tensor_tensor(out=tmp, in0=blk, scalar=float(P), in1=row, op0=ALU.mult, op1=ALU.add))
            nc.vector.tensor_copy(yrow, tmp)
            which, number = a2["s"][:, 88:88 + SPILL], a2["s"][:, 96:96 + SPILL]
            reach = a2["w1"][:, 64:64 + SPILL * E].rearrange("p (j n) -> p j n", j=SPILL)
            link(ts(number, iota[:, 0:SPILL], 64.0, None, ALU.add))
            link(tt(reach, incl.unsqueeze(1).broadcast_to([P, SPILL, E]),
                    number.unsqueeze(2).broadcast_to([P, SPILL, E]), ALU.is_le))
            link(nc.vector.tensor_reduce(which, reach, X, ALU.add))
            link(ts(which, which, float(E - 1), None, ALU.min))
            nc.vector.tensor_copy(spill_expert[:, 0:SPILL], which).then_inc(slots_ready, 1)

            gain2 = vec[:, GAINS["norm2_g"]:GAINS["norm2_g"] + KD]

            def turned_rows(p, n, i):
                for half in range(2):
                    o = bank(n + half)
                    product(dve, n + half, i)
                    tt(xT[:, p, 4 * half:4 * half + 4, :], o[:, :].rearrange("p (k n) -> p k n", k=4),
                       gain2[:, 4 * half:4 * half + 4].unsqueeze(2).broadcast_to([P, 4, P]), ALU.mult)\
                        .then_inc(proj_evacuated[(n + half) % 2], 1)

            def expert_block(p, i, last=False):
                if not last:
                    turned_rows(1 - p, moe_product(p, i, "turn", 1), i)
                o = psS[p]
                nth = i * 2 + (p + 1)
                dve.wait_ge(silu_ready, nth)
                tt(ehid[:, p, :], o[:, 0:F_E], sg[:, p, :], ALU.mult).then_inc(hidden_part, 1)
                dve.wait_ge(hidden_part, nth)
                tt(ehid[:, p, :], o[:, F_E:2 * F_E], ehid[:, p, :], ALU.mult).then_inc(gu_taken, 1)

            turned_rows(0, moe_job(0, "turn"), 0)
            moe_pairs(dve, expert_block)
            for t in range(NT):
                dve.wait_ge(picked[t], 32)
                for k in range(2):
                    ins = nc.vector.scalar_tensor_tensor(out=x[:, t, :], in0=rows_of[k][:, t, :], scalar=g12[:, k, t:t + 1],
                                                         in1=x[:, t, :], op0=ALU.mult, op1=ALU.add)
                    if k == 0:
                        link(ins)
                ins.then_inc(combined, 1)

            norm(2)
            for t in range(NT):
                n = JOBS["ai"] + t
                nc.vector.tensor_copy(tok[:, t, 512:1024], evac_to(n)[:, :]).then_inc(proj_evacuated[n % 2], 1)
            copied_all(dve, "ax", NT)
            sq = scr[:, 4:6, :].rearrange("p a n -> p (a n)")
            temps = scr.rearrange("p a n -> p (a n)")[:, 0:1024]
            link(tt(sq, a3["sel"][:, 0:1024], a3["sel"][:, 0:1024], ALU.mult))
            link(nc.vector.tensor_reduce(qss[:, 0:4], sq.rearrange("p (t n) -> p t n", t=NT), X, ALU.add))
            link(ts(qss[:, 0:4], qss[:, 0:4], 1.0 / 256, EPS, ALU.mult, ALU.add))
            kid1 = kid[:, :, 0:HD]
            sq1 = sq[:, 0:256].rearrange("p (t n) -> p t n", t=NT)
            link(tt(sq1, kid1, kid1, ALU.mult))
            link(nc.vector.tensor_reduce(qss[:, 4:8], sq1, X, ALU.add))
            ts(qss[:, 4:8], qss[:, 4:8], 1.0 / HD, EPS, ALU.mult, ALU.add).then_inc(head_mean, 1)
            tt(sp_part(0).rearrange("p (t n) -> p t n", t=NT), wb[:, :, 8:16],
               prm("forget_b").unsqueeze(1).broadcast_to([P, NT, 8]), ALU.add).then_inc(forget_z, 1)
            link(ts(wb[:, :, 0:8], wb[:, :, 0:8], 8 ** -0.5 * 64 ** -0.5))
            dve.wait_ge(head_root, 2)
            link(nc.vector.reciprocal(qss[:, 0:8], qss[:, 0:8]))
            link(tt(ckv, ckv, qss[:, 0:4].unsqueeze(2).broadcast_to([P, NT, 256]), ALU.mult))
            link(tt(ckv, ckv, prm("ckv_gain").unsqueeze(1).broadcast_to([P, NT, 256]), ALU.mult))
            link(tt(kid1, kid1, qss[:, 4:8].unsqueeze(2).broadcast_to([P, NT, HD]), ALU.mult))
            link(tt(kid1, kid1, prm("kidx_gain").unsqueeze(1).broadcast_to([P, NT, HD]), ALU.mult))
            rope(kid1.unsqueeze(2), 1, temps)
            rope(krd[:, :, 0:HD].unsqueeze(2), 1, temps)
            nc.vector.tensor_copy(kid[:, :, HD:P], kid1)
            nc.vector.tensor_copy(krd[:, :, HD:HD + 2 * ROT], krd[:, :, 0:2 * ROT])
            for t in range(NT):
                n = JOBS["aq"] + t
                ts(tok[:, t, 0:512], evac_to(n)[:, :], SCALE).then_inc(proj_evacuated[n % 2], 1)
            copied_all(dve, "ai", NT)
            rope(tok[:, :, 512:1024].rearrange("p t (h d) -> p t h d", d=HD), 8, temps)
            copied_all(dve, "aq", NT)
            rope(tok[:, :, 0:512].rearrange("p t (h d) -> p t h d", d=HD), 8, temps)
            dve.wait_ge(forget_ln, 1)
            link(ts(sp_part(0), sp_part(0), -1.0, 0.0, ALU.mult, ALU.max))
            tt(sp_part(2), sp_part(0), sp_part(1), ALU.add).then_inc(heads_ready, 1)
            for j in range(4):
                n = JOBS["kh"] + j
                tt(khT[:, j, :], evac_to(n)[:, :], krT, ALU.add).then_inc(proj_evacuated[n % 2], 1)
            for c in range(8 * (NT - 1)):
                t, h = c // 8 + 1, c % 8
                copied(dve, JOBS["index"] + c)
                if c >= 1:
                    dve.wait_ge(relu_used, c)
                nc.vector.scalar_tensor_tensor(out=sel[t], in0=S[c % 2][:, 0:(t + 1) * P], scalar=wb[:, t, h:h + 1],
                                               in1=cmask(t) if h == 0 else sel[t], op0=ALU.mult, op1=ALU.add)\
                    .then_inc(relu_used, 1)
            dve.wait_ge(relu_used, 8 * (NT - 1))
            top8 = small[:, 288:296]

            def take(t, n):
                if n % 2 == 0:
                    link(nc.vector.max(top8, sel[t]))
                else:
                    link(nc.vector.match_replace(sel[t], top8, sel[t], TAKEN))
                if n == KEEP // 4 - 1:
                    link(ts(sel[t], sel[t], 0.7 * TAKEN, NEG, ALU.is_gt, ALU.mult))

            for t in range(1, NT - 1):
                for n in range(KEEP // 4):
                    take(t, n)
            attention(first_fox, first_nsa - first_fox,
                      lambda i: take(NT - 1, i) if i < KEEP // 4 else None)
            for c in range(2):
                split_weight(0, c)
            add_to_x(JOBS["ao"])
            norm(3)
            mlp(0)

            norm(4)
            copied_all(dve, "nv", NT)
            tt(gate2, gate2, prm("gate_b").unsqueeze(1).broadcast_to([P, NT, 48]), ALU.add).then_inc(gate_ready, 1)
            temps = scr.rearrange("p a n -> p (a n)")
            copied_all(dve, "nk", NT)
            for col in (0, 256, 512):
                rope(kv2[:, :, col:col + P].rearrange("p t (h d) -> p t h d", d=HD), 2, temps,
                     heads_ready if col == 512 else None)
            for c in range(2):
                for t in range(NT):
                    n = JOBS["nq"] + NT * c + t
                    ts(tok[:, t, :].rearrange("p (j g d) -> p j g d", g=2, d=HD)[:, :, c, :],
                       evac_to(n)[:, :].rearrange("p (j d) -> p j d", d=HD), SCALE).then_inc(proj_evacuated[n % 2], 1)
            for g in range(2):
                shifted(JOBS["turn_nk"] + 2 + g, win[:, 1, g, :], nc.vector.tensor_copy, dve)
            copied_all(dve, "nq", 2 * NT)
            dve.wait_ge(heads_ready, 3)
            rope(tok.rearrange("p t (h d) -> p t h d", d=HD), 16, temps, heads_ready)
            dve.wait_ge(cmp_zeroed, 3)
            for s in range(2):
                n = JOBS["cmp"] + 1 + s
                o = evac_to(n)
                nc.vector.tensor_copy(small[:, 304 + s:305 + s], o[:, 2 * N_CMP:2 * N_CMP + 1])
                nc.vector.tensor_copy(chid[:, s, :].rearrange("p (g n) -> p g n", g=2)[:, :, 0:N_CMP],
                                      o[:, 0:2 * N_CMP].rearrange("p (g n) -> p g n", g=2))\
                    .then_inc(proj_evacuated[n % 2], 1)
            copied_all(dve, "cmp", 3)
            for s in range(2):
                windows = chid[:, s, :].rearrange("p (g n) -> p g n", g=2)[:, :, 0:N_CMP]
                link(ts(windows, windows, small[:, 304 + s:305 + s], None, ALU.add))
            link(tt(cpart(1), cpart(0), cpart(0), ALU.mult))
            link(ts(cpart(1), cpart(1), 0.044715, 1.0, ALU.mult, ALU.add))
            tt(cpart(1), cpart(1), cpart(0), ALU.mult).then_inc(gelu_in, 1)
            dve.wait_ge(gelu_sig, 1)
            tt(cpart(3), cpart(2), cpart(0), ALU.mult).then_inc(gelu_out, 1)
            n = JOBS["cmp2"] + 1
            o = evac_to(n)
            for j in range(4):
                last = nc.vector.tensor_copy(vcBD[32 * j:32 * j + 32, :, HD * j:HD * j + HD],
                                             o[32 * j:32 * j + 32, 0:P].rearrange("p (g d) -> p g d", g=2))
            last.then_inc(proj_evacuated[n % 2], 1)
            dve.wait_ge(gate_ready, 2)
            attention(first_nsa, n_items - first_nsa)
            for c in range(2):
                split_weight(1, c)
            add_to_x(JOBS["no"])
            norm(5)
            mlp(1)
            norm(6)
            for t in range(NT):
                dve.wait_ge(rstd_ready, 7)
                nc.vector.scalar_tensor_tensor(out=tok[:, t, :], in0=x[:, t, :], scalar=rstd[:, 24 + t:25 + t],
                                               in1=prm("final"), op0=ALU.mult, op1=ALU.mult).then_inc(final_ready, 1)


_INS = ["x", "norm1_g", "w_in", "q_norm_g", "k_norm_g", "attn_sink", "conv_w", "conv_b", "w_attn_proj", "w_conv_proj",
        "w_out", "norm2_g", "w_router_group", "b_router_group", "w_router_expert", "b_router_expert", "w_gate_e",
        "w_up_e", "w_down_e", "attn_norm_2", "mlp_norm_2", "mlp_w1_2", "mlp_w2_2", "ab_w_in_2", "ab_b_forget_2",
        "a_kv_norm_2", "a_w_uk_2", "a_w_uv_2", "a_kidx_norm_2", "ab_w_out_2", "c_w_in_2", "c_b_gate_2", "c_pe_k_2",
        "c_pe_v_2", "c_cmp_k_w1_2", "c_cmp_k_w2_2", "c_cmp_v_w1_2", "c_cmp_v_w2_2", "c_w_out_2", "final_norm_2"]


def kernel(**inputs):
    import numpy as _np
    import concourse.bacc as _bacc
    from concourse import mybir as _mybir
    from concourse.bass_utils import run_bass_kernel_spmd as _run

    nc = _bacc.Bacc("TRN2", target_bir_lowering=False, num_devices=1)
    arrays, w = {}, {}
    for name in _INS:
        a = _np.ascontiguousarray(inputs[name])
        arrays[f"in_{name}"] = a
        w[name] = nc.dram_tensor(f"in_{name}", a.shape, _mybir.dt.float32, kind="ExternalInput").ap()
    arrays["in_constants"] = constants()
    w["constants"] = nc.dram_tensor("in_constants", (P, NCONST), _mybir.dt.float32, kind="ExternalInput").ap()
    out = nc.dram_tensor("out_x", (1, T, D), _mybir.dt.float32, kind="ExternalOutput").ap()
    build(nc, w, out)
    r = _run(nc, [arrays], core_ids=[0])
    return r.results[0]["out_x"]
```

```python
import concourse.bass as bass
from concourse import mybir
from concourse.alu_op_type import AluOpType as ALU
from contextlib import ExitStack
import numpy as np

F32 = mybir.dt.float32
F32R = mybir.dt.float32r
I32 = mybir.dt.int32
ACT = mybir.ActivationFunctionType
X = mybir.AxisListType.X

P = 128
T = 512
NT = T // P
D = 1024
KD = D // P
HD = 64
ROT = 8
EPS = 1e-6
NEG = -1e30
SCALE = HD ** -0.5
E = 32
G = 4
EG = E // G
F_E = 256
SPILL = 7
NB = E + SPILL
F = 4096
NF = F // P
N_CMP = 31
CMP_LEN, CMP_STRIDE = 32, 16
CMP_TURN, CMP_FIRST, CMP_SECOND = 2, 12, 36
KEEP = 128
RING = 3
BIG = 18952
SLOT = 4096
GELU_C = float((2 / np.pi) ** 0.5)
TAKEN = -3e38

CONST = {}
_at = 0
for _n, _w in (("ident", P), ("before", P), ("upto", T), ("band", 3 * P), ("causal", T), ("cmp", NT * 32),
               ("cmpok", NT), ("cos", NT * ROT), ("sin", NT * ROT), ("iota", P), ("token", NT)):
    CONST[_n] = (_at, _at + _w)
    _at += _w
NCONST = _at

GAINS = {"norm1_g": 0, "norm2_g": 8, "attn0": 16, "mlp0": 24, "attn1": 32, "mlp1": 40}
NORMS = tuple(GAINS)
CONVW, CONVB = 48, 60

PAR = {}
_at = 0
for _n, _w in (("qk_gain", 640), ("router_b", 36), ("final", D), ("sink", 8), ("forget_b", 8), ("ckv_gain", 256),
               ("kidx_gain", 64), ("gate_b", 48), ("router_w", KD * 36), ("cmp_w2", 2 * HD)):
    PAR[_n] = (_at, _at + _w)
    _at += _w
NPAR = _at


def constants():
    c = np.zeros((P, NCONST), np.float32)
    p, j = np.arange(P)[:, None], np.arange(P)[None, :]

    def put(name, a):
        c[:, CONST[name][0]:CONST[name][1]] = a

    put("ident", p == j)
    put("before", p < j)
    put("upto", np.concatenate([p <= j, np.ones((P, T - P), bool)], 1))
    band = np.zeros((P, 3 * P), np.float32)
    band[:, :P] = np.where(j >= p, 0, NEG)
    band[:, 2 * P:] = np.where(j <= p, 0, NEG)
    put("band", band)
    put("causal", np.concatenate([np.zeros((P, T - P)), np.where(j <= p, 0, NEG)], 1))
    t = (np.arange(NT)[None, :] * P + p)
    n = np.arange(32)
    ok = (n[None, None, :] * CMP_STRIDE + CMP_LEN - 1 <= t[:, :, None]) & (n < N_CMP)[None, None, :]
    put("cmp", np.where(ok, 0, NEG).reshape(P, -1))
    put("cmpok", t >= CMP_LEN - 1)
    inv = np.float32(500000.0) ** (-np.arange(0, 2 * ROT, 2, dtype=np.float32) / np.float32(2 * ROT))
    ang = t.astype(np.float32)[:, :, None] * inv.astype(np.float32)[None, None, :]
    put("cos", np.cos(ang).reshape(P, -1))
    put("sin", np.sin(ang).reshape(P, -1))
    put("iota", j - 64.0 + 0 * p)
    put("token", t)
    return c


EIGHTHS = 8
UP_JOBS, DOWN_JOBS = NF // EIGHTHS, 2 * NT


def mlp_steps():
    steps, job = [], 0
    order = [("up", 0)]
    for e in range(1, EIGHTHS):
        order += [("up", e), ("down", e - 1)]
    for kind, e in order + [("down", EIGHTHS - 1)]:
        steps.append((kind, e, job))
        job += UP_JOBS if kind == "up" else DOWN_JOBS
    return steps


MLP_STEPS = mlp_steps()
MLP_JOBS = EIGHTHS * (UP_JOBS + DOWN_JOBS)

JOBS, WIDTH = {}, {}
_at = 0
for _n, _w in (("vec", 1),
               ("norm0", KD), ("kv", NT), ("q", 2 * NT), ("cc", 4), ("cx", 4), ("cb", 4), ("ga", KD),
               ("gc0", 4), ("turn_q", 5), ("gc1", 4), ("turn_o0", 4), ("merge", 2 * KD), ("wo", 3 * NT), ("tail1", NT + KD),
               ("ranks", 1), ("table", 1), ("moe", 5 * E),
               ("norm2", KD), ("ax", NT), ("ai", 2 * NT), ("aq", 2 * NT), ("bv", 2 * NT), ("turn_small", 4), ("kh", 4), ("vh", NT),
               ("turn_qi", 4), ("forget", 1), ("index", 8 * (NT - 1)), ("bq", 4), ("turn_aq", 4), ("bk", 4),
               ("turn_o1", KD), ("ao", 3 * NT), ("tail3", NT + KD),
               ("mlp0", MLP_JOBS - NT), ("tail4", NT + KD),
               ("nk", 2 * NT), ("nv", 2 * NT), ("nq", 4 * NT), ("turn_nk", 2), ("turn_nq", 8), ("cmp", 9),
               ("turn_o2", KD), ("no", 3 * NT), ("tail5", NT + KD), ("mlp1", MLP_JOBS)):
    JOBS[_n], WIDTH[_n] = _at, _w
    _at += _w


TAIL = {"wo": 1, "ao": 3, "mlp0": 4, "no": 5}
SPLIT_NORMS = (3, 4, 5)


def job(stage, i):
    n = i - WIDTH[stage]
    return JOBS[stage] + i if n < 0 else JOBS[f"tail{TAIL[stage]}"] + (0, 1, 2, 5)[n]


def norm_turn(n, t, half):
    if n in TAIL.values():
        return JOBS[f"tail{n}"] + (3, 6, 8, 10)[t] + half
    return JOBS[f"norm{n}"] + 2 * t + half


EARLY = (("cc", "cc", 0), ("cx", "cx", 0), ("cb", "cb", 0), ("ga0", "ga", 0), ("ga1", "ga", 4), ("gc0", "gc0", 0),
         ("gc1", "gc1", 0))


def split_pieces():
    pieces = []

    def stage(chunk, k, cuts, name, first, per):
        for n, (c0, c1) in enumerate(cuts):
            pieces.append((chunk, k, c0, c1, job(name, first + per * (n + 1) - 1), start))

    halves = ((0, 256), (256, 512))
    start = 0
    stage("q", KD, halves, "q", 0, NT)
    start = len(pieces)
    for chunk, name, first in EARLY:
        stage(chunk, KD, [(m * P, (m + 1) * P) for m in range(4)], name, first, 1)
    start = len(pieces)
    for n in range(4):
        for c, chunk in enumerate(("cp", "ap")):
            pieces.append((chunk, 4, 2 * P * n, 2 * P * (n + 1), job("merge", 4 * n + 2 + c), start))
    start = len(pieces)
    for c in range(2):
        stage(f"wo{c}", KD, halves, "wo", 2 * NT * c, NT)
    start = len(pieces)
    for name in ("ai", "aq", "bv"):
        stage(name, KD, halves, name, 0, NT)
    for l, name in enumerate(("ao", "no")):
        start = len(pieces)
        for c in range(2):
            stage(f"{name}{c}", KD, halves, name, 2 * NT * c, NT)
        for kind, e, first in MLP_STEPS:
            if kind == "up":
                stage(f"up{l}{e}", KD, halves, f"mlp{l}", first, 2)
            else:
                stage(f"down{l}{e}", UP_JOBS, ((0, 512), (512, 1024)), f"mlp{l}", first, NT)
        if l == 0:
            stage("nk", KD, halves, "nk", 0, NT)
            stage("nv", KD, ((0, 152), (152, 304)), "nv", 0, NT)
            for c in range(2):
                stage(f"nq{c}", KD, halves, "nq", 2 * NT * c, NT)
    return pieces


SPLIT = split_pieces()
SPLIT_AT = {}
for _n, _piece in enumerate(SPLIT):
    SPLIT_AT.setdefault(_piece[0], _n)


def moe_job(b, what):
    n = JOBS["moe"] + 5 * b
    last = b - (E - 2)
    if what == "turn":
        return n - 5 if b >= 2 else JOBS["moe"] + 2 * b
    if what == "hidden":
        return n + 4 if last < 1 else n + 2
    return n + 7 if last < 0 else n + 5 if last == 0 else n + 3


def weight_plan(w):
    plan = []

    def kview(a):
        return a.rearrange("(k p) n -> p k n", p=P)

    def cols(name, a, c0, c1, last=None):
        plan.append((name, [(0, KD * (c1 - c0), c1 - c0, 0, c1 - c0, kview(a)[:, :, c0:c1])], last))

    def whole(name, src, last=None):
        plan.append((name, [(0, SLOT, SLOT // src.shape[1], 0, SLOT // src.shape[1], src)], last))

    w_in = w["w_in"][0]
    for name, c0, c1, last in (("kv", 512, 768, "kv+3"), ("q", 0, 512, "q+7"), ("cc", 1280, 1792, "cc+3"),
                               ("cx", 1792, 2304, "cx+3"), ("cb", 768, 1280, "cb+3"),
                               ("ga0", 2304, 2816, "ga+3"), ("ga1", 2816, 3328, "ga+7"),
                               ("gc0", 3328, 3840, "gc0+3"), ("gc1", 3840, 4352, "gc1+3")):
        cols(name, w_in, c0, c1, last)
    whole("ap", kview(w["w_attn_proj"][0]), "merge+15")
    whole("cp", kview(w["w_conv_proj"][0]), "merge+14")
    for c in range(2):
        cols(f"wo{c}", w["w_out"][0], c * 512, c * 512 + 512, ("wo", 2 * NT * (c + 1) - 1))
    plan.append(("experts", None, None))
    ab = w["ab_w_in_2"][0]
    plan.append(("ax", [(0, KD * 352, 352, o, o + c1 - c0, kview(ab)[:, :, c0:c1])
                        for o, c0, c1 in ((0, 512, 784), (272, 1296, 1368), (344, 2904, 2912))], "ax+3"))
    cols("ai", ab, 784, 1296, "ai+7")
    cols("aq", ab, 0, 512, "aq+7")
    cols("bv", ab, 2392, 2904, "bv+7")
    cols("bq", ab, 1368, 1880, "bq+3")
    cols("bk", ab, 1880, 2392, "bk+3")
    for c in range(2):
        cols(f"ao{c}", w["ab_w_out_2"][0], c * 512, c * 512 + 512)

    def mlp(l):
        down = kview(w["mlp_w2_2"][l])
        for kind, e, _ in MLP_STEPS:
            if kind == "up":
                cols(f"up{l}{e}", w["mlp_w1_2"][l], e * 512, (e + 1) * 512)
            else:
                whole(f"down{l}{e}", down[:, e * UP_JOBS:(e + 1) * UP_JOBS, :])

    mlp(0)
    cw = w["c_w_in_2"][0]
    for name, c0, c1 in (("nk", 1024, 1536), ("nv", 1536, 1840), ("nq0", 0, 512), ("nq1", 512, 1024)):
        cols(name, cw, c0, c1)
    for n, kind in enumerate("kv"):
        a = kview(w[f"c_cmp_{kind}_w1_2"][0])
        plan.append((f"w1{kind}", [(0, CMP_LEN * HD, P, 0, P, a)], f"cmp+{n + 5}"))
    for c in range(2):
        cols(f"no{c}", w["c_w_out_2"][0], c * 512, c * 512 + 512)
    mlp(1)
    return plan


def build(nc, w, out):
    ctx = ExitStack()
    with ctx:
        address = {}
        free = [-(-nc.sbuf_base // 64) * 64]

        def sb(name, shape):
            address[name] = free[0]
            free[0] += -(-4 * int(np.prod(shape[1:])) // 32) * 32
            return nc.alloc_sbuf_tensor_at(name, shape, F32, offset=address[name])

        def over(name, shape, under, word):
            return nc.alloc_sbuf_tensor_at(name, shape, F32R, offset=address[under] + 4 * word)

        def sem(name):
            return ctx.enter_context(nc.semaphore(name))

        rows_dram = nc.dram_tensor("rows_dram", [T, D], F32, kind="Internal").ap()
        y_dram = nc.dram_tensor("y_dram", [NB * P, D], F32, kind="Internal").ap()

        x = sb("x", [P, NT, D])
        hT = sb("hT", [P, KD, T])
        tok = sb("tok", [P, NT, D])
        ring = sb("ring", [P, RING, SLOT])
        big = sb("big", [P, BIG])
        scr = sb("scr", [P, 7, T])
        const = sb("const", [P, NCONST])
        par = sb("par", [P, NPAR])
        vec_rows = sb("vec_rows", [64, P])
        vec = sb("vec", [P, 64])
        pe_rows = sb("pe_rows", [32, P])
        stat = sb("stat", [P, 3, 256])
        small = sb("small", [P, 512])
        psA = [ctx.enter_context(nc.psum_tensor(f"psA{i}", [P, 512], F32)) for i in range(2)]
        psS = [ctx.enter_context(nc.psum_tensor(f"psS{i}", [P, 512], F32)) for i in range(2)]
        psT = [ctx.enter_context(nc.psum_tensor(f"psT{i}", [P, 512], F32)) for i in range(2)]
        psO = [ctx.enter_context(nc.psum_tensor(f"psO{i}", [P, 512], F32)) for i in range(2)]

        def cst(name):
            return const[:, CONST[name][0]:CONST[name][1]]

        def prm(name):
            return par[:, PAR[name][0]:PAR[name][1]]

        ident = cst("ident")
        upto = cst("upto")
        ones = upto[:, P:2 * P]
        earlier = cst("before")
        iota = cst("iota")
        cos4 = cst("cos").rearrange("p (t c) -> p t c", c=ROT)
        sin4 = cst("sin").rearrange("p (t c) -> p t c", c=ROT)
        negm, sums, fac = stat[:, 0, :], stat[:, 1, :], stat[:, 2, :]

        def carve(sizes):
            at, got = 0, {}
            for name, n in sizes:
                got[name] = big[:, at:at + n]
                at += n
            assert at <= BIG, at
            return got

        a1_parts = (("qk", 2560), ("v", 512), ("qT", 2048), ("kT", 512), ("u", 2056), ("conv", 2048),
                    ("ga", 4096), ("gc", 4096))
        a1 = carve(a1_parts)
        qk = a1["qk"].rearrange("p (t n) -> p t n", t=NT)
        v1 = a1["v"].rearrange("p (t n) -> p t n", t=NT)
        qT1 = a1["qT"].rearrange("p (j n) -> p j n", j=4)
        kT1 = a1["kT"]
        u = a1["u"].rearrange("p (m n) -> p m n", m=4)
        conv = a1["conv"].rearrange("p (m n) -> p m n", m=4)
        ga = a1["ga"].rearrange("p (m n) -> p m n", m=KD)
        gc = a1["gc"].rearrange("p (m n) -> p m n", m=KD)
        merged_whole = tok.rearrange("p t d -> p (t d)").rearrange("p (m n) -> p m n", m=KD)
        moe_parts = (("logit", 144), ("w1", 512), ("w2", 512), ("w3", 512), ("oh1", 128), ("oh2", 128), ("asg", 128),
                    ("rank", 128), ("cnt", 32), ("spill", 32), ("incl", 32), ("obase", 32), ("s", 256), ("xg", 2048),
                    ("xT", 2048), ("sg", 512), ("hid", 512), ("hidT", 512), ("y", 2048), ("picked", NT * D))
        a2 = carve(moe_parts)
        a3_parts = (("bv", 2048), ("bqT", 2048), ("bkT", 2048), ("aqT", 2048), ("kiT", 512), ("krT", 512),
                    ("ckvT", 1024), ("wb", 64), ("sel", 1152), ("kh", 2048), ("vh", 2048),
                    ("ncum", 512), ("sp", 96))
        a3 = carve(a3_parts)
        a4 = carve((("qT", 4096), ("kT2", 1024), ("win", 3072), ("weights", 4096), ("kv", 3072), ("gate", 192),
                    ("kcBD", 64), ("vcBD", 256), ("hid", 512), ("cmpst", 64), ("cmpout", 512)))
        hT_hi = over("hT_hi", [P, KD, T], "hT", 0)
        hT_lo = over("hT_lo", [P, KD, T], "big", 0)
        w_hi = [over(f"w_hi{i}", [P, 2048], "big", 4096 + 2048 * i) for i in range(2)]
        w_lo = [over(f"w_lo{i}", [P, 2048], "big", 8192 + 2048 * i) for i in range(2)]
        hid_hi = [over(f"hid_hi{i}", [P, UP_JOBS, T], *at) for i, at in enumerate((("tok", 0), ("big", 12288)))]
        hid_lo = [over(f"hid_lo{i}", [P, UP_JOBS, T], *at) for i, at in enumerate((("tok", 2048), ("big", 14336)))]

        a1_gc = sum(n for _, n in a1_parts[:-1])
        hT_hi_early = over("hT_hi_early", [P, KD, T], "big", a1_gc)
        hT_lo_early = over("hT_lo_early", [P, KD, T], "tok", 0)
        conv_hi, conv_lo = (over(name, [P, 4, T], "hT", at) for name, at in (("conv_hi", 0), ("conv_lo", 4 * T)))
        attn_hi = over("attn_hi", [P, 4, T], "big", 0)
        attn_lo = over("attn_lo", [P, 4, T], "scr", 0)
        merged_hi = over("merged_hi", [P, KD, T], "big", a1_gc - KD * T)
        merged_lo = over("merged_lo", [P, KD, T], "big", a1_gc)
        wo_hi = [over(f"wo_hi{i}", [P, 2048], "big", sum(n for _, n in a1_parts[:k])) for i, k in enumerate((2, 4))]
        second_hi = over("second_hi", [P, KD, T], "big", sum(n for _, n in a3_parts[:9]))
        second_lo = over("second_lo", [P, KD, T], "big", a3_parts[0][1])
        second_w_hi = [over(f"second_w_hi{i}", [P, 2048], "big", at)
                       for i, at in enumerate((sum(n for _, n in a3_parts[:4]), BIG - 2048))]
        assert BIG - 2048 >= sum(n for _, n in a3_parts)
        ring_lo = [over(f"ring_lo{i}", [P, SLOT], "ring", SLOT * i) for i in range(RING)]
        q_w_hi = [over(f"q_w_hi{i}", [P, 2048], "big", a1_gc - 4096 + 2048 * i) for i in range(2)]
        early_hi = [over(f"early_hi{i}", [P, KD * P], *at) for i, at in enumerate((("scr", 5 * T), ("big", BIG - KD * P)))]

        x_loaded = [sem(f"x_loaded{i}") for i in range(NT)]
        const_loaded = sem("const_loaded")
        params_loaded = sem("params_loaded")
        w_arrived = [sem(f"w_arrived{i}") for i in range(RING)]
        proj_ready = sem("proj_ready")
        proj_evacuated = [sem(f"proj_evacuated{i}") for i in range(2)]
        sumsq_ready = sem("sumsq_ready")
        mean_ready = sem("mean_ready")
        root_ready = sem("root_ready")
        rstd_ready = sem("rstd_ready")
        normed = sem("normed")
        head_mean = sem("head_mean")
        head_root = sem("head_root")
        heads_ready = sem("heads_ready")
        scores_ready = sem("scores_ready")
        masked = sem("masked")
        probs_ready = sem("probs_ready")
        turned = sem("turned")
        turned_copied = sem("turned_copied")
        values_ready = sem("values_ready")
        inverted = sem("inverted")
        factor_ready = sem("factor_ready")
        out_taken = [sem(f"out_taken{i}") for i in range(2)]
        normed_hi = sem("normed_hi")
        normed_lo = sem("normed_lo")
        out_hi = sem("out_hi")
        out_lo = sem("out_lo")
        early_in_hi = sem("early_in_hi")
        early_in_lo = sem("early_in_lo")
        early_in_moved = sem("early_in_moved")
        weight_hi = sem("weight_hi")
        weight_lo = sem("weight_lo")
        squared = sem("squared")
        hidden_hi = sem("hidden_hi")
        hidden_lo = sem("hidden_lo")
        logits_shifted = sem("logits_shifted")
        logits_exp = sem("logits_exp")
        assigned = sem("assigned")
        logits_ready = sem("logits_ready")
        slots_ready = sem("slots_ready")
        rows_stored = sem("rows_stored")
        gathered = [sem(f"gathered{i}") for i in range(2)]
        gu_ready = sem("gu_ready")
        gu_taken = sem("gu_taken")
        silu_ready = sem("silu_ready")
        y_written = [sem(f"y_written{i}") for i in range(2)]
        spill_free = sem("spill_free")
        spill_arrived = sem("spill_arrived")
        spill_gathered = sem("spill_gathered")
        spill_turned = sem("spill_turned")
        spill_scaled = sem("spill_scaled")
        spill_gu = sem("spill_gu")
        spill_silu = sem("spill_silu")
        spill_part = sem("spill_part")
        spill_hidden = sem("spill_hidden")
        spill_hidden_turned = sem("spill_hidden_turned")
        spill_hidden_copied = sem("spill_hidden_copied")
        spill_down = sem("spill_down")
        spill_copied = sem("spill_copied")
        spill_written = sem("spill_written")
        picked = [sem(f"picked{i}") for i in range(NT)]
        combined = sem("combined")
        forget_z = sem("forget_z")
        forget_ln = sem("forget_ln")
        relu_used = sem("relu_used")
        gate_ready = sem("gate_ready")
        gelu_in = sem("gelu_in")
        gelu_exp = sem("gelu_exp")
        gelu_out = sem("gelu_out")
        final_ready = sem("final_ready")
        stored = sem("stored")
        second_in_hi = sem("second_in_hi")
        second_in_lo = sem("second_in_lo")
        conv_in_hi = sem("conv_in_hi")
        conv_in_lo = sem("conv_in_lo")
        attn_in_hi = sem("attn_in_hi")
        attn_in_lo = sem("attn_in_lo")
        merged = sem("merged")
        merged_in_hi = sem("merged_in_hi")
        merged_in_lo = sem("merged_in_lo")
        gu_arrived = [sem(f"gu_arrived{i}") for i in range(2)]
        dn_arrived = [sem(f"dn_arrived{i}") for i in range(2)]
        hidden_part = sem("hidden_part")
        latent_zeroed = sem("latent_zeroed")
        latent_weights = sem("latent_weights")
        cmp_zeroed = sem("cmp_zeroed")
        cmp_added = sem("cmp_added")
        dve_chain = sem("dve_chain")
        act_chain = sem("act_chain")

        block = ctx.enter_context(nc.Block())

        items = []

        band, causal = cst("band"), cst("causal")
        for j in range(4):
            for g in range(2):
                for t in range(NT):
                    lo, hi = max(0, t - 1), min(NT - 1, t + 1)
                    n = (hi - lo + 1) * P
                    items.append(dict(kind="band", head=4 * g + j, t=t, n=n, blocks=list(range(lo, hi + 1)),
                                      mask=band[:, (lo - t + 1) * P:(lo - t + 1) * P + n],
                                      scores=[(qT1[64 * g:64 * g + 64, j, t * P:(t + 1) * P],
                                               kT1[64 * g:64 * g + 64, lo * P:lo * P + n])],
                                      values=v1[:, :, 64 * g:64 * g + 64]))
        n_band = len(items)

        bv = a3["bv"].rearrange("p (t n) -> p t n", t=NT)
        bqT = a3["bqT"].rearrange("p (j n) -> p j n", j=4)
        bkT = a3["bkT"].rearrange("p (j n) -> p j n", j=4)
        aqT = a3["aqT"].rearrange("p (j n) -> p j n", j=4)
        qiT = bqT
        ckvT = a3["ckvT"].rearrange("p (m n) -> p m n", m=2)
        ckv = a3["sel"][:, 0:1024].rearrange("p (t n) -> p t n", t=NT)
        khT = a3["kh"].rearrange("p (j n) -> p j n", j=4)
        vh = a3["vh"].rearrange("p (t n) -> p t n", t=NT)
        wuv = a3["aqT"][:, 1024:2048].rearrange("p (m n) -> p m n", m=2)
        ncum = a3["ncum"]
        wb = a3["wb"].rearrange("p (t n) -> p t n", t=NT)
        sel = {1: a3["sel"][:, 0:256], 2: a3["sel"][:, 256:640], 3: a3["sel"][:, 640:1152]}

        def cmask(t):
            return causal[:, T - (t + 1) * P:T]

        for h in range(8):
            for t in range(NT):
                r = 64 * (h % 2)
                n = (t + 1) * P
                items.append(dict(kind="fox", head=8 + h, t=t, n=n, blocks=list(range(t + 1)), mask=cmask(t),
                                  scores=[(bqT[r:r + 64, h // 2, t * P:(t + 1) * P], bkT[r:r + 64, h // 2, 0:n]),
                                          (ident[:, h:h + 1].broadcast_to([P, P]), ncum[:, 0:n])],
                                  values=bv[:, :, 64 * h:64 * h + 64]))

        for h in range(8):
            for t in range(NT):
                r = 64 * (h % 2)
                n = (t + 1) * P
                items.append(dict(kind="latent", head=h, t=t, n=n, blocks=list(range(t + 1)),
                                  mask=cmask(t) if t == 0 else sel[t],
                                  scores=[(aqT[r:r + 64, h // 2, t * P:(t + 1) * P], khT[r:r + 64, h // 2, 0:n])],
                                  values=vh[:, :, 64 * h:64 * h + 64]))
        first_fox, first_nsa = n_band, n_band + 16 * NT

        qT2 = a4["qT"].rearrange("p (j n) -> p j n", j=8)
        kv2 = a4["kv"].rearrange("p (t n) -> p t n", t=NT)
        kT2 = a4["kT2"].rearrange("p (s n) -> p s n", s=2)
        win = a4["win"].rearrange("p (s g n) -> p s g n", s=2, g=3)
        gate2 = a4["gate"].rearrange("p (t n) -> p t n", t=NT)
        kcBD, vcBD, cmpout = a4["kcBD"], a4["vcBD"], a4["cmpout"]
        chid = a4["hid"].rearrange("p (s n) -> p s n", s=8)
        cmpmask = cst("cmp").rearrange("p (t n) -> p t n", t=NT)
        cmpok = cst("cmpok")
        cmpst = a4["cmpst"].rearrange("p (i n) -> p i n", n=8)
        pair_at, cmp_items = {}, []

        def pair_items(h, branch):
            g, j = h // 8, h % 8
            for t in range(NT):
                n = (t + 1) * P
                pair_at[h, branch, t] = len(items)
                items.append(dict(kind="pair", head=h, branch=branch, t=t, n=n, blocks=list(range(t + 1)), mask=cmask(t),
                                  nth=len(pair_at), gate=gate2[:, t, h * 3 + 1 + branch:h * 3 + 2 + branch],
                                  scores=[(qT2[64 * g:64 * g + 64, j, t * P:(t + 1) * P],
                                           kT2[64 * g:64 * g + 64, branch, 0:n])],
                                  values=kv2[:, :, 64 * g + (640 if branch else 384):64 * g + (704 if branch else 448)]))

        def cmp_item(c, t):
            cmp_items.append(len(items))
            items.append(dict(kind="cmp", c=c, t=t, n=256, blocks=[0, 1], index=len(cmp_items) - 1))

        for c in range(2):
            runs = [(g * 8 + 4 * c + j, branch) for g in range(2) for j in range(4) for branch in range(2)]
            for n, (h, branch) in enumerate(runs):
                pair_items(h, branch)
                if n in ((11, 12, 13, 14), (1, 3, 5, 7))[c]:
                    cmp_item(1 - c, len(cmp_items) % NT)
        first_cmp = cmp_items[0]
        n_items = len(items)
        kiT, krT = a3["kiT"], a3["krT"]
        S, PR, PT = ([scr[:, i, :] for i in at] for at in ((0, 1), (2, 3, 4), (5, 6)))

        yrow = small[:, 0:8].bitcast(I32)
        spill_expert = small[:, 16:24].bitcast(I32)
        slot_token = small[:, 32:32 + NB].bitcast(I32)
        g12 = small[:, 120:128].rearrange("p (k t) -> p k t", k=2)
        ss = small[:, 128:160]
        rstd = small[:, 160:192]
        qss = small[:, 192:232]
        negsink = small[:, 240:248]
        esink = small[:, 256:288]
        xg = a2["xg"].rearrange("p (b n) -> p b n", b=2)
        xT = a2["xT"].rearrange("p (b k n) -> p b k n", b=2, k=KD)
        hot_row = a2["xg"][:, 0:2 * NT * P].rearrange("p (c n) -> p c n", c=2 * NT)
        hot_block = a2["xT"][:, 0:2 * NT * NB].rearrange("p (c n) -> p c n", c=2 * NT)
        sg = a2["sg"].rearrange("p (b n) -> p b n", b=2)
        ehid = a2["hid"].rearrange("p (b n) -> p b n", b=2)
        ehidT = a2["hidT"].rearrange("p (b n) -> p b n", b=2)
        ey = a2["y"].rearrange("p (b n) -> p b n", b=2)
        at_oh = sum(n for _, n in moe_parts[:[k for k, _ in moe_parts].index("oh1")])
        at = sum(n for _, n in moe_parts[:[k for k, _ in moe_parts].index("xg")])
        rows_of = [a2["picked"].rearrange("p (t n) -> p t n", t=NT),
                   big[:, at:at + NT * D].rearrange("p (t n) -> p t n", t=NT)]
        krd = scr[:, 2, :].rearrange("p (t n) -> p t n", t=NT)
        kid = scr[:, 3, :].rearrange("p (t n) -> p t n", t=NT)
        wuk = a3["aqT"][:, 0:1024].rearrange("p (m h d) -> p m h d", m=2, h=8)
        asg = a2["asg"].rearrange("p (t n) -> p t n", t=NT)
        gexp, pexp = a2["w1"][:, 32:48], a2["s"][:, 24:28]
        sp_terms = a3["sp"][:, 64:96].rearrange("p (t n) -> p t n", t=NT)

        def sp_part(k):
            return a3["sp"][:, 32 * k:32 * k + 32]

        def cpart(k):
            return a4["hid"][:, 128 * k:128 * k + 128]

        def rows(a):
            return a.rearrange("(k p) -> k p", p=P)

        def everywhere(a):
            return a.partition_broadcast(P)

        def heads(a, n):
            return a.unsqueeze(0).unsqueeze(0).broadcast_to([P, n, HD])

        qk_gain = prm("qk_gain").rearrange("p (h d) -> p h d", d=HD)
        router_w3 = prm("router_w").rearrange("p (k n) -> p k n", k=KD)
        loads = [(const[:, :], w["constants"]),
                 (vec_rows[0:8, :], rows(w["norm1_g"][0])), (vec_rows[8:16, :], rows(w["norm2_g"][0])),
                 (vec_rows[16:24, :], rows(w["attn_norm_2"][0])), (vec_rows[24:32, :], rows(w["mlp_norm_2"][0])),
                 (vec_rows[32:40, :], rows(w["attn_norm_2"][1])), (vec_rows[40:48, :], rows(w["mlp_norm_2"][1])),
                 (vec_rows[CONVB:CONVB + 4, :], rows(w["conv_b"][0]))]
        for j in range(3):
            loads.append((vec_rows[CONVW + 4 * j:CONVW + 4 * j + 4, :], rows(w["conv_w"][0][j])))
        CONST_LOADS = len(loads)
        later_loads = [
                 (pe_rows[:, 0:HD], w["c_pe_k_2"][0]), (pe_rows[:, HD:P], w["c_pe_v_2"][0]),
                 (qk_gain[:, 0:8, :], heads(w["q_norm_g"][0], 8)), (qk_gain[:, 8:10, :], heads(w["k_norm_g"][0], 2)),
                 (prm("router_b")[:, 0:G], everywhere(w["b_router_group"][0])),
                 (prm("router_b")[:, G:G + E], everywhere(w["b_router_expert"][0])),
                 (prm("final"), everywhere(w["final_norm_2"])), (prm("sink"), everywhere(w["attn_sink"][0])),
                 (prm("forget_b"), everywhere(w["ab_b_forget_2"][0])),
                 (prm("ckv_gain"), everywhere(w["a_kv_norm_2"][0])),
                 (prm("kidx_gain"), everywhere(w["a_kidx_norm_2"][0])), (prm("gate_b"), everywhere(w["c_b_gate_2"][0])),
                 (router_w3[:, :, 0:G], w["w_router_group"][0].rearrange("(k p) n -> p k n", p=P)),
                 (router_w3[:, :, G:G + E], w["w_router_expert"][0].rearrange("(k p) n -> p k n", p=P)),
                 (prm("cmp_w2")[:, 0:HD], w["c_cmp_k_w2_2"][0]), (prm("cmp_w2")[:, HD:2 * HD], w["c_cmp_v_w2_2"][0])]
        PARAM_LOADS = len(later_loads)

        plan = weight_plan(w)
        names = [name for name, _, _ in plan]
        experts_at = names.index("experts")
        in_ring = [n for n in names if n != "experts"]
        slot_of = {n: i % RING for i, n in enumerate(in_ring)}
        gu_slot = [experts_at % RING, (experts_at + 1) % RING]
        dn_slot = (experts_at + 2) % RING
        arrived_at, total = {}, [0] * RING
        for name, pieces, _ in plan:
            if name != "experts":
                total[slot_of[name]] += 16 * len(pieces)
                arrived_at[name] = total[slot_of[name]]

        def slot(name):
            return ring[:, slot_of[name], :]

        gu = [ring[:, i, :].rearrange("p (k n) -> p k n", k=KD) for i in gu_slot]
        dn = [ring[:, dn_slot, p * 2048:(p + 1) * 2048].rearrange("p (k n) -> p k n", k=2) for p in range(2)]

        def last_use(name, last):
            if isinstance(last, str):
                name, n = last.split("+")
                return proj_ready, JOBS[name] + int(n) + 1
            if last:
                return proj_ready, job(*last) + 1
            return weight_lo, max(n for n, piece in enumerate(SPLIT) if piece[0] == name) + 1

        def product(eng, n, i=0):
            eng.wait_ge(proj_ready, i * 10 + (n + 1))

        def copied(eng, n, i=0):
            eng.wait_ge(proj_evacuated[n % 2], i * 5 + (n // 2 + 1))

        def copied_all(eng, name, count):
            for n in range(max(0, count - 2), count):
                copied(eng, JOBS[name] + n)

        def bank(n):
            return psA[n % 2]

        def raw_piece(c):
            name, k, c0, c1, _, _ = SPLIT[c]
            words = [pieces[0][1] for n, pieces, _ in plan if n == name][0]
            return slot(name)[:, 0:words].rearrange("p (k n) -> p k n", k=k)[:, :, c0:c1]

        def part(parts, c):
            _, k, c0, c1, _, _ = SPLIT[c]
            if c < SPLIT_AT["ao0"]:
                if parts is w_lo:
                    return ring_lo[slot_of[SPLIT[c][0]]].rearrange("p (k n) -> p k n", k=k)[:, :, c0:c1]
                if c < SPLIT_AT["cc"]:
                    return q_w_hi[c % 2].rearrange("p (k n) -> p k n", k=k)
                if c >= SPLIT_AT["ai"]:
                    return second_w_hi[c % 2].rearrange("p (k n) -> p k n", k=k)
                if SPLIT_AT["cp"] <= c < SPLIT_AT["wo0"]:
                    return early_hi[1 - c % 2].rearrange("p (k n) -> p k n", k=k)
                if c >= SPLIT_AT["wo0"]:
                    return wo_hi[c % 2].rearrange("p (k n) -> p k n", k=k)
                return early_hi[c % 2].rearrange("p (k n) -> p k n", k=k)
            return parts[c % 2][:, 0:k * (c1 - c0)].rearrange("p (k n) -> p k n", k=k)

        def piece_used(eng, c):
            if c >= SPLIT[c][5] + 2:
                product(eng, SPLIT[c - 2][4])

        def turned_whole(t, half):
            return scr[:, (2 * t + half) % 6, :].rearrange("p (k n) -> p k n", k=4)

        def shifted(n, dst, copy, eng):
            product(eng, n)
            copy(dst[0:HD, :], bank(n)[0:HD, :])
            copy(dst[HD:P, 0:T - 1], bank(n)[HD:P, 1:T]).then_inc(proj_evacuated[n % 2], 1)

        def moe_pairs(eng, expert_block):
            for b in range(4):
                expert_block(b % 2, b // 2)
            with eng.Fori(2, E // 2 - 1) as i:
                for p in range(2):
                    expert_block(p, i)
            expert_block(0, E // 2 - 1)
            expert_block(1, E // 2 - 1, last=True)

        def spilled(eng):
            eng.wait_ge(slots_ready, 2)
            return eng.value_load(spill_expert[0:1, 0:1], min_val=0, max_val=SPILL)

        def moe_product(p, i, what, ahead=0):
            if isinstance(i, int):
                return moe_job(2 * i + p + ahead, what) - 10 * i
            return JOBS["moe"] + 5 * (p + ahead) + {"turn": -5, "hidden": 4, "down": 7}[what]

        def before(p, i, least):
            return isinstance(i, int) and 2 * i + p < least

        @block.sync
        def _(sp):
            for t in range(NT):
                sp.dma_start(x[:, t, :], w["x"][0][t * P:(t + 1) * P, :]).then_inc(x_loaded[t], 16)
            held = {}

            def load_block(p, e):
                for o, a in ((0, w["w_gate_e"]), (F_E, w["w_up_e"])):
                    src = a[0][bass.ds(e, 1)].rearrange("e (k p) n -> p (e k) n", p=P)
                    sp.dma_start(gu[p][:, :, o:o + F_E], src).then_inc(gu_arrived[p], 16)

            def load_down(p, e):
                src = w["w_down_e"][0][bass.ds(e, 1)].rearrange("e (k p) n -> p (e k) n", p=P)
                sp.dma_start(dn[p], src).then_inc(dn_arrived[p], 16)

            def experts():
                def gate_up(p, i, e):
                    if not before(p, i, 2):
                        sp.wait_ge(gu_ready, i * 2 + (p - 1))
                    load_block(p, e)

                def down(p, i, e):
                    if not before(p, i, 2):
                        product(sp, moe_product(p, i, "down", -2) + 1, i)
                    load_down(p, e)

                for p in range(2):
                    sp.wait_ge(*held[gu_slot[p]])
                    gate_up(p, 0, p)
                sp.wait_ge(*held[dn_slot])
                down(0, 0, 0)
                for p in range(2):
                    gate_up(p, 1, 2 + p)
                    down(1 - p, p, 1 + p)
                with sp.Fori(2, E // 2) as i:
                    for p in range(2):
                        gate_up(p, i, i * 2 + p)
                        if p == 0:
                            product(sp, moe_product(1, i, "down", -4) + 1, i)
                        else:
                            product(sp, moe_product(0, i, "down", -2) + 1, i)
                        load_down(1 - p, i * 2 + (p - 1))
                down(1, E // 2 - 1, E - 1)
                with sp.If(spilled(sp) > 0):
                    for j in range(SPILL):
                        sp.wait_ge(spill_free, j + 1)
                        e = sp.value_load(spill_expert[0:1, j + 1:j + 2], min_val=0, max_val=E - 1)
                        for o, a in ((0, w["w_gate_e"]), (F_E, w["w_up_e"])):
                            src = a[0][bass.ds(e, 1)].rearrange("e (k p) n -> p (e k) n", p=P)
                            sp.dma_start(gu[0][:, :, o:o + F_E], src).then_inc(spill_arrived, 16)
                        src = w["w_down_e"][0][bass.ds(e, 1)].rearrange("e (k p) n -> p (e k) n", p=P)
                        sp.dma_start(dn[0], src).then_inc(spill_arrived, 16)
                    sp.wait_ge(spill_free, SPILL + 1)
                held[gu_slot[1]] = (gu_ready, E)
                held[gu_slot[0]] = (gu_ready, E - 1)
                held[dn_slot] = (proj_ready, moe_job(E - 1, "down") + 2)

            sp.wait_ge(const_loaded, CONST_LOADS * 16)
            for name, pieces, last in plan:
                if name == "experts":
                    experts()
                    sp.wait_ge(picked[NT - 1], 32)
                    continue
                s = slot_of[name]
                if s in held:
                    sp.wait_ge(*held[s])
                for piece in pieces:
                    first, words, width, c0, c1, src = piece
                    dst = ring[:, s, first:first + words].rearrange("p (k n) -> p k n", n=width)[:, :, c0:c1]
                    sp.dma_start(dst, src).then_inc(w_arrived[s], 16)
                held[s] = last_use(name, last)
            for t in range(NT):
                sp.wait_ge(final_ready, t + 1)
                sp.dma_start(out[0][t * P:(t + 1) * P, :], tok[:, t, :]).then_inc(stored, 16)
            sp.wait_ge(stored, NT * 16)

        @block.gpsimd
        def _(pool):
            def split_weight(c):
                piece_used(pool, c)
                pool.wait_ge(weight_hi, c + 1)
                nc.gpsimd.tensor_tensor(part(w_lo, c), raw_piece(c), part(w_hi, c).bitcast(F32), ALU.subtract)\
                    .then_inc(weight_lo, 1)

            def then_split(c):
                if c + 2 < len(SPLIT) and SPLIT[c + 2][5] == SPLIT[c][5]:
                    split_weight(c + 2)

            for c in range(SPLIT_AT["cp"]):
                split_weight(c)
            product(pool, JOBS["gc1"] + 3)
            for m in (2, 3):
                copied(pool, JOBS["cb"] + m)
            for m in range(4):
                nc.gpsimd.tensor_copy(conv_hi[:, m, :], conv[:, m, :]).then_inc(conv_in_hi, 1)
                pool.wait_ge(conv_in_hi, m + 1)
                nc.gpsimd.tensor_tensor(conv_lo[:, m, :], conv[:, m, :], conv_hi[:, m, :].bitcast(F32), ALU.subtract)\
                    .then_inc(conv_in_lo, 1)
            for c in range(SPLIT_AT["cp"], SPLIT_AT["ai"]):
                split_weight(c)
            copied(pool, JOBS["table"])
            pool.wait_ge(rows_stored, 16)
            for b in range(E):
                if b >= 2:
                    product(pool, moe_job(b - 2, "turn") + 1)
                pool.indirect_dma_start(xg[:, b % 2, :], None, rows_dram[:, :],
                                        bass.IndirectOffsetOnAxis(ap=slot_token[:, b:b + 1], axis=0))\
                    .then_inc(gathered[b % 2], 16)

            def fetch(outputs):
                for p in range(2):
                    pool.wait_ge(y_written[p], 16 * (E // 2))
                for t in range(NT):
                    for k in range(2):
                        c = k * NT + t
                        pool.indirect_dma_start(rows_of[k][:, t, :], None, outputs,
                                                bass.IndirectOffsetOnAxis(ap=yrow[:, c:c + 1], axis=0))\
                            .then_inc(picked[t], 16)

            with pool.If(spilled(pool) > 0):
                for j in range(SPILL):
                    pool.wait_ge(spill_free, j + 1)
                    pool.indirect_dma_start(xg[:, 0, :], None, rows_dram[:, :],
                                            bass.IndirectOffsetOnAxis(ap=slot_token[:, E + j:E + j + 1], axis=0))\
                        .then_inc(spill_gathered, 16)
                pool.wait_ge(spill_written, 16 * SPILL)
                fetch(y_dram[:, :])
            with pool.Else():
                fetch(y_dram[0:E * P, :])
            pool.wait_ge(combined, NT)
            nc.gpsimd.memset(wuk.rearrange("p m h d -> p (m h d)"), 0.0).then_inc(latent_zeroed, 1)
            nc.gpsimd.memset(scr[:, 2, :], 0.0).then_inc(latent_zeroed, 1)
            nc.gpsimd.memset(ncum, 0.0).then_inc(latent_zeroed, 1)
            pool.wait_ge(latent_zeroed, 3)
            for m in range(2):
                pool.dma_start(wuk[:, m, :, 2 * ROT:HD], w["a_w_uk_2"][0][m * P:(m + 1) * P])\
                    .then_inc(latent_weights, 16)
            pool.dma_start(wuv[:, :, :], w["a_w_uv_2"][0].rearrange("(m p) h d -> p m (h d)", p=P))\
                .then_inc(latent_weights, 16)
            for c in range(SPLIT_AT["ai"], SPLIT_AT["ao0"]):
                split_weight(c)

            def layer(l, out):
                for c in range(2):
                    split_weight(SPLIT_AT[out + "0"] + c)
                for c in range(3):
                    then_split(SPLIT_AT[out + "0"] + c)
                then_split(SPLIT_AT[out + "0"] + 3)
                for kind, e, _ in MLP_STEPS:
                    for half in range(2):
                        then_split(SPLIT_AT[f"{kind}{l}{e}"] + half)

            layer(0, "ao")
            for name in ("nk", "nv", "nq0", "nq1"):
                for c in range(2):
                    then_split(SPLIT_AT[name] + c)
            product(pool, job("nq", WIDTH["nq"] - 1))
            nc.gpsimd.memset(vcBD, 0.0).then_inc(cmp_zeroed, 1)
            nc.gpsimd.memset(kcBD, 0.0).then_inc(cmp_zeroed, 1)
            nc.gpsimd.memset(a4["hid"], 0.0).then_inc(cmp_zeroed, 1)
            nc.gpsimd.memset(win[:, :, 2, :], 0.0).then_inc(cmp_zeroed, 1)
            layer(1, "no")

        @block.tensor
        def _(pe):
            def need(name):
                pe.wait_ge(w_arrived[slot_of[name]], arrived_at[name])

            def begin(n, i=0):
                if isinstance(i, int) and n // 2 + 5 * i <= 0:
                    return bank(n)
                pe.wait_ge(proj_evacuated[n % 2], i * 5 + n // 2)
                return bank(n)

            def turn(n, sources, i=0):
                o = begin(n, i)
                for c, a in enumerate(sources):
                    k = a.shape[0]
                    ins = pe.transpose(o[:, c * P:c * P + k], a, ident[0:k, 0:k])
                ins.then_inc(proj_ready, 1)

            def token_major(stage, name, width, first=0, before_norm=None):
                need(name)
                s = slot(name)
                for t in range(NT):
                    o = begin(job(stage, first + t))
                    for k in range(KD):
                        ins = pe.matmul(o[:, 0:width], hT[:, k, t * P:(t + 1) * P], s[:, k * width:(k + 1) * width],
                                        start=(k == 0), stop=(k == KD - 1))
                    ins.then_inc(proj_ready, 1)
                    if before_norm:
                        tail(before_norm, t)

            def feature_major(first, name, some=range(4)):
                need(name)
                s = slot(name)
                for m in some:
                    o = begin(first + m)
                    for k in range(KD):
                        ins = pe.matmul(o[:, :], s[:, k * 512 + m * P:k * 512 + (m + 1) * P], hT[:, k, :],
                                        start=(k == 0), stop=(k == KD - 1))
                    ins.then_inc(proj_ready, 1)

            def norm_tile(n, t):
                pe.wait_ge(normed, NT * n + t + 1)
                for half in range(2):
                    turn(norm_turn(n, t, half), [tok[:, t, (4 * half + k) * P:(4 * half + k + 1) * P] for k in range(4)])

            def logits(t):
                if t == 0:
                    pe.wait_ge(params_loaded, PARAM_LOADS * 16)
                for half in range(2):
                    copied(pe, norm_turn(1, t, half))
                router_w = prm("router_w").rearrange("p (k n) -> p k n", k=KD)
                for k in range(KD):
                    ins = pe.matmul(psS[0][:, t * 36:(t + 1) * 36], hT[:, k, t * P:(t + 1) * P], router_w[:, k, :],
                                    start=(k == 0), stop=(k == KD - 1))
                ins.then_inc(logits_ready, 1)

            def tail(n, t):
                for tile in {2: (0,), 3: (1, 2, 3)}.get(t, ()):
                    norm_tile(n, tile)
                    if n == 1 and tile:
                        logits(tile - 1)

            def norm(n):
                for t in range(NT):
                    norm_tile(n, t)

            def normed_in(n):
                if n in SPLIT_NORMS:
                    pe.wait_ge(normed_lo, 2 * NT * (SPLIT_NORMS.index(n) + 1))
                    pe.wait_ge(normed_hi, 2 * NT * (SPLIT_NORMS.index(n) + 1))
                else:
                    for half in range(2):
                        copied(pe, norm_turn(n, NT - 1, half))

            def attention(first, count, meanwhile=None):
                for i in range(first, first + count + 3):
                    if meanwhile:
                        meanwhile(i - first)
                    if i < first + count:
                        it = items[i]
                        if i >= 2:
                            pe.wait_ge(masked, i - 1)
                        o = psS[i % 2]
                        if it["kind"] == "cmp":
                            for j in range(4):
                                ins = pe.matmul(o[:, j * 64:(j + 1) * 64],
                                                qT2[:, 4 * it["c"] + j, it["t"] * P:(it["t"] + 1) * P], kcBD,
                                                start=True, stop=True)
                        else:
                            for c, (a, b) in enumerate(it["scores"]):
                                ins = pe.matmul(o[:, 0:it["n"]], a, b, start=(c == 0),
                                                stop=(c == len(it["scores"]) - 1))
                        ins.then_inc(scores_ready, 1)
                    k = i - 2
                    if first <= k < first + count:
                        pe.wait_ge(probs_ready, k + 1)
                        if k >= 2:
                            pe.wait_ge(turned_copied, k - 1)
                        for b in range(len(items[k]["blocks"])):
                            ins = pe.transpose(psT[k % 2][:, b * P:(b + 1) * P], PR[k % 3][:, b * P:(b + 1) * P], ident)
                        ins.then_inc(turned, 1)
                    k = i - 3
                    if first <= k < first + count:
                        it = items[k]
                        pe.wait_ge(turned_copied, k + 1)
                        if k >= 2:
                            pe.wait_ge(out_taken[k % 2], k // 2)
                        o, pt = psO[k % 2], PT[k % 2]
                        nb = len(it["blocks"])
                        if it["kind"] == "cmp":
                            for b in range(2):
                                ins = pe.matmul(o[:, b * 256:(b + 1) * 256], pt[:, b * P:(b + 1) * P],
                                                vcBD, start=True, stop=True)
                        else:
                            for b, kb in enumerate(it["blocks"]):
                                ins = pe.matmul(o[:, 0:HD], pt[:, b * P:(b + 1) * P], it["values"][:, kb, :],
                                                start=(b == 0), stop=(b == nb - 1))
                        ins.then_inc(values_ready, 1)

            def attended(count):
                for k in (count - 2, count - 1):
                    pe.wait_ge(out_taken[k % 2], k // 2 + 1)

            def split_product(n, width, terms):
                o = begin(n)[:, 0:width]
                at = 0
                for a_hi, a_lo, b_hi, b_lo in terms:
                    for a, b in ((a_hi, b_hi), (a_hi, b_lo), (a_lo, b_hi)):
                        at += 1
                        ins = pe.matmul(o, a, b, start=(at == 1), stop=(at == 3 * len(terms)))
                ins.then_inc(proj_ready, 1)

            def piece(c):
                pe.wait_ge(weight_lo, c + 1)
                pe.wait_ge(weight_hi, c + 1)
                return part(w_hi, c), part(w_lo, c)

            def split_token_major(stage, chunk, first, low, before_norm=None, high=hT_hi):
                for half in range(2):
                    c = SPLIT_AT[chunk] + half
                    wh, wl = piece(c)
                    for t in range(NT):
                        split_product(job(stage, first + NT * half + t), wh.shape[2],
                                      [(high[:, k, t * P:(t + 1) * P], low[:, k, t * P:(t + 1) * P], wh[:, k, :], wl[:, k, :])
                                       for k in range(KD)])
                        if before_norm and half:
                            tail(before_norm, t)

            def split_feature_major(first, name, high):
                for m in range(4):
                    wh, wl = piece(SPLIT_AT[name] + m)
                    split_product(first + m, T, [(wh[:, k, :], wl[:, k, :], high[:, k, :], hT_lo_early[:, k, :])
                                                 for k in range(KD)])

            def out_projection(n, name):
                for k in range(KD):
                    turn(JOBS[f"turn_o{n}"] + k, [tok[:, t, k * P:(k + 1) * P] for t in range(NT)])
                pe.wait_ge(out_lo, n * KD)
                pe.wait_ge(out_hi, n * KD)
                split_token_major(name, name + "0", 0, hT_lo)
                split_token_major(name, name + "1", 2 * NT, hT_lo, TAIL[name])
                normed_in(TAIL[name])

            def mlp(l):
                stage = f"mlp{l}"
                for kind, e, first in MLP_STEPS:
                    for half in range(2):
                        wh, wl = piece(SPLIT_AT[f"{kind}{l}{e}"] + half)
                        if kind == "up":
                            for f in range(2):
                                split_product(job(stage, first + 2 * half + f), T,
                                              [(wh[:, k, f * P:(f + 1) * P], wl[:, k, f * P:(f + 1) * P],
                                                hT_hi[:, k, :], hT_lo[:, k, :]) for k in range(KD)])
                        else:
                            pe.wait_ge(hidden_lo, l * NF + (e + 1) * UP_JOBS)
                            pe.wait_ge(hidden_hi, l * NF + (e + 1) * UP_JOBS)
                            for t in range(NT):
                                split_product(job(stage, first + NT * half + t), 512,
                                              [(hid_hi[e % 2][:, k, t * P:(t + 1) * P], hid_lo[e % 2][:, k, t * P:(t + 1) * P],
                                                wh[:, k, :], wl[:, k, :]) for k in range(UP_JOBS)])
                                if e == EIGHTHS - 1 and half and stage in TAIL:
                                    tail(TAIL[stage], t)
                if stage in TAIL:
                    normed_in(TAIL[stage])

            pe.wait_ge(const_loaded, CONST_LOADS * 16)
            turn(JOBS["vec"], [vec_rows[:, :]])
            copied(pe, JOBS["vec"])
            norm(0)
            normed_in(0)
            token_major("kv", "kv", 256)
            pe.wait_ge(early_in_hi, KD)
            pe.wait_ge(early_in_lo, KD)
            split_token_major("q", "q", 0, hT_lo_early, high=hT_hi_early)
            for name, stage, first in EARLY[:-2]:
                split_feature_major(JOBS[stage] + first, name, hT_hi_early)
            pe.wait_ge(early_in_moved, KD)
            split_feature_major(JOBS["gc0"], "gc0", hT_hi)
            pe.wait_ge(heads_ready, 1)
            for j in range(5):
                turn(JOBS["turn_q"] + j, [qk[:, t, j * P:(j + 1) * P] for t in range(NT)])
            copied_all(pe, "turn_q", 5)

            def conv_gates(step):
                if step == 2:
                    split_feature_major(JOBS["gc1"], "gc1", hT_hi)

            attention(0, n_band, conv_gates)
            attended(n_band)
            for c in range(4):
                turn(JOBS["turn_o0"] + c, [tok[:, t, c * P:(c + 1) * P] for t in range(NT)])
            copied_all(pe, "turn_o0", 4)
            copied_all(pe, "gc1", 4)
            pe.wait_ge(conv_in_hi, 4)
            pe.wait_ge(conv_in_lo, 4)
            pe.wait_ge(attn_in_hi, 4)
            pe.wait_ge(attn_in_lo, 4)
            for m in range(KD):
                for c, (high, low) in enumerate(((conv_hi, conv_lo), (attn_hi, attn_lo))):
                    wh, wl = piece(SPLIT_AT["cp"] + 2 * (m // 2) + c)
                    cols = slice(m % 2 * P, (m % 2 + 1) * P)
                    split_product(JOBS["merge"] + 2 * m + c, T, [(wh[:, k, cols], wl[:, k, cols], high[:, k, :], low[:, k, :])
                                                                 for k in range(4)])
            pe.wait_ge(merged_in_hi, KD)
            pe.wait_ge(merged_in_lo, KD)
            split_token_major("wo", "wo0", 0, merged_lo, high=merged_hi)
            split_token_major("wo", "wo1", 2 * NT, merged_lo, TAIL["wo"], merged_hi)

            logits(NT - 1)
            n = JOBS["ranks"]
            o = begin(n)
            pe.wait_ge(assigned, 1)
            rank3 = o[:, 0:(NT + 1) * E].rearrange("p (t n) -> p t n", n=E)
            pe.matmul(o[:, 0:P], earlier, asg, start=True, stop=False)
            for s in range(NT - 1):
                pe.matmul(rank3[:, s + 1:NT, :], ones, asg[:, s:s + 1, :].broadcast_to([P, NT - 1 - s, E]), start=False,
                          stop=(s == NT - 2))
            for s in range(NT):
                ins = pe.matmul(rank3[:, NT, :], ones, asg[:, s, :], start=(s == 0), stop=(s == NT - 1))
            ins.then_inc(proj_ready, 1)

            n = JOBS["table"]
            o = begin(n)
            pe.wait_ge(slots_ready, 1)
            for c in range(2 * NT):
                ins = pe.matmul(o[:, 0:NB], hot_row[:, c, :], hot_block[:, c, :], start=(c == 0), stop=(c == 2 * NT - 1))
            ins.then_inc(proj_ready, 1)

            def turn_rows(p, i, n, count):
                pe.wait_ge(gathered[p], count * 16)
                for c in range(2):
                    turn(n + c, [xg[:, p, (4 * c + k) * P:(4 * c + k + 1) * P] for k in range(4)], i)

            def down(p, i, ahead):
                q = (p + ahead) % 2
                hidn, n = moe_product(p, i, "hidden", ahead), moe_product(p, i, "down", ahead)
                copied(pe, hidn, i)
                pe.wait_ge(dn_arrived[q], i * 16 + 16 * ((p + ahead) // 2 + 1))
                for half in range(2):
                    o = begin(n + half, i)
                    for k in range(2):
                        ins = pe.matmul(o[:, :], ehidT[:, q, k * P:(k + 1) * P], dn[q][:, k, half * 512:(half + 1) * 512],
                                        start=(k == 0), stop=(k == 1))
                    ins.then_inc(proj_ready, 1)

            def hidden(p, i, ahead):
                pe.wait_ge(gu_taken, i * 2 + (p + ahead + 1))
                turn(moe_product(p, i, "hidden", ahead), [ehid[:, (p + ahead) % 2, k * P:(k + 1) * P] for k in range(2)], i)

            def expert_block(p, i, last=False):
                turns = moe_product(p, i, "turn")
                if not before(p, i, 1):
                    hidden(p, i, -1)
                pe.wait_ge(gu_arrived[p], i * 32 + 32)
                for m in range(2):
                    copied(pe, turns + m, i)
                if not before(p, i, 2):
                    pe.wait_ge(gu_taken, i * 2 + (p - 1))
                for k in range(KD):
                    if k == KD // 2 and not last:
                        turn_rows(1 - p, i, moe_product(p, i, "turn", 1), i + (1 + p))
                    ins = pe.matmul(psS[p][:, :], xT[:, p, k, :], gu[p][:, k, :], start=(k == 0), stop=(k == KD - 1))
                ins.then_inc(gu_ready, 1)
                if not before(p, i, 1):
                    down(p, i, -1)
                if last:
                    hidden(p, i, 0)
                    down(p, i, 0)

            turn_rows(0, 0, moe_job(0, "turn"), 1)
            moe_pairs(pe, expert_block)

            def spill_block(j):
                pe.wait_ge(spill_gathered, j * 16)
                for c in range(2):
                    for k in range(4):
                        ins = pe.transpose(psT[c][:, k * P:(k + 1) * P], xg[:, 0, (4 * c + k) * P:(4 * c + k + 1) * P], ident)
                ins.then_inc(spill_turned, 1)
                pe.wait_ge(spill_arrived, j * 48)
                pe.wait_ge(spill_scaled, j)
                for k in range(KD):
                    ins = pe.matmul(psS[0][:, :], xT[:, 0, k, :], gu[0][:, k, :], start=(k == 0), stop=(k == KD - 1))
                ins.then_inc(spill_gu, 1)
                pe.wait_ge(spill_hidden, j)
                for k in range(2):
                    ins = pe.transpose(psS[1][:, k * P:(k + 1) * P], ehid[:, 0, k * P:(k + 1) * P], ident)
                ins.then_inc(spill_hidden_turned, 1)
                pe.wait_ge(spill_hidden_copied, j)
                for half in range(2):
                    for k in range(2):
                        ins = pe.matmul(psO[half][:, :], ehidT[:, 0, k * P:(k + 1) * P],
                                        dn[0][:, k, half * 512:(half + 1) * 512], start=(k == 0), stop=(k == 1))
                ins.then_inc(spill_down, 1)
                pe.wait_ge(spill_copied, j)
                pe.nop().then_inc(spill_free, 1)

            with pe.If(spilled(pe) > 0):
                product(pe, moe_job(E - 1, "down") + 1)
                pe.nop().then_inc(spill_free, 1)
                with pe.Fori(1, SPILL + 1) as j:
                    spill_block(j)

            norm(2)
            normed_in(2)
            token_major("ax", "ax", 352)
            pe.wait_ge(second_in_hi, KD)
            pe.wait_ge(second_in_lo, KD)
            for name in ("ai", "aq", "bv"):
                split_token_major(name, name, 0, second_lo, high=second_hi)
            pe.wait_ge(heads_ready, 2)
            turn(JOBS["turn_small"], [kid[:, t, :] for t in range(NT)])
            turn(JOBS["turn_small"] + 1, [krd[:, t, :] for t in range(NT)])
            for m in range(2):
                turn(JOBS["turn_small"] + 2 + m, [ckv[:, t, m * P:(m + 1) * P] for t in range(NT)])
            copied_all(pe, "turn_small", 4)
            pe.wait_ge(latent_weights, 48)
            for j in range(4):
                o = begin(JOBS["kh"] + j)
                for m in range(2):
                    ins = pe.matmul(o[:, :], wuk[:, m, 2 * j:2 * j + 2, :].rearrange("p h d -> p (h d)"), ckvT[:, m, :],
                                    start=(m == 0), stop=(m == 1))
                ins.then_inc(proj_ready, 1)
            for t in range(NT):
                o = begin(JOBS["vh"] + t)
                for m in range(2):
                    ins = pe.matmul(o[:, :], ckvT[:, m, t * P:(t + 1) * P], wuv[:, m, :], start=(m == 0), stop=(m == 1))
                ins.then_inc(proj_ready, 1)
            for j in range(4):
                turn(JOBS["turn_qi"] + j, [tok[:, t, 512 + j * P:512 + (j + 1) * P] for t in range(NT)])
            o = begin(JOBS["forget"])
            for t in range(NT):
                ins = pe.matmul(o[0:8, t * P:T], sp_terms[:, t, :], upto[:, 0:T - t * P], start=(t == 0),
                                stop=(t == NT - 1))
            ins.then_inc(proj_ready, 1)
            copied_all(pe, "turn_qi", 4)
            for t in range(1, NT):
                for h in range(8):
                    n, r = JOBS["index"] + 8 * (t - 1) + h, 64 * (h % 2)
                    pe.matmul(begin(n)[:, 0:(t + 1) * P], qiT[r:r + 64, h // 2, t * P:(t + 1) * P],
                              kiT[r:r + 64, 0:(t + 1) * P], start=True, stop=True).then_inc(proj_ready, 1)
            feature_major(JOBS["bq"], "bq")
            for j in range(4):
                turn(JOBS["turn_aq"] + j, [tok[:, t, j * P:(j + 1) * P] for t in range(NT)])
            feature_major(JOBS["bk"], "bk", range(1))
            copied(pe, JOBS["bk"])

            def further_keys(step):
                if step == 2:
                    feature_major(JOBS["bk"], "bk", range(1, 4))
                    copied_all(pe, "bk", 4)

            attention(first_fox, first_nsa - first_fox, further_keys)
            attended(first_nsa)
            out_projection(1, "ao")
            mlp(0)

            split_token_major("nk", "nk", 0, hT_lo)
            split_token_major("nv", "nv", 0, hT_lo)
            for c in range(2):
                split_token_major("nq", f"nq{c}", 2 * NT * c, hT_lo)
            def turn_twice(n, sources):
                o = begin(n)
                for c, a in enumerate(sources):
                    k = a.shape[0]
                    for half in range(2):
                        ins = pe.matmul(o[HD * half:HD * (half + 1), c * P:c * P + k], a, ident[0:k, 0:k],
                                        start=True, stop=True)
                ins.then_inc(proj_ready, 1)

            pe.wait_ge(heads_ready, 3)
            for c, col in enumerate((256, 512)):
                turn(JOBS["turn_nk"] + c, [kv2[:, t, col:col + P] for t in range(NT)])
            pe.wait_ge(heads_ready, 5)
            for j in range(8):
                turn(JOBS["turn_nq"] + j, [tok[:, t, j * P:(j + 1) * P] for t in range(NT)])
            copied_all(pe, "turn_nk", 2)
            copied_all(pe, "turn_nq", 8)

            def compress(step):
                if step == CMP_TURN:
                    for c in range(4):
                        s, g = c // 2, c % 2
                        turn_twice(JOBS["cmp"] + c, [kv2[:, t, P * s + HD * g:P * s + HD * (g + 1)] for t in range(NT)])
                    pe.wait_ge(params_loaded, PARAM_LOADS * 16)
                    turn_twice(JOBS["cmp"] + 4, [pe_rows[:, HD * s:HD * (s + 1)] for s in range(2)])
                elif step == CMP_FIRST:
                    copied_all(pe, "cmp", 5)
                    for s, kind in enumerate("kv"):
                        need("w1" + kind)
                        w1 = slot("w1" + kind)
                        o = begin(JOBS["cmp"] + 5 + s)
                        for j in range(CMP_LEN // 2):
                            ins = pe.matmul(o[:, 0:3 * N_CMP], w1[:, j * P:(j + 1) * P],
                                            win[:, s, :, 2 * j:2 * j + CMP_STRIDE * (N_CMP - 1) + 1:CMP_STRIDE],
                                            start=(j == 0), stop=(j == CMP_LEN // 2 - 1))
                        ins.then_inc(proj_ready, 1)
                elif step == CMP_SECOND:
                    pe.wait_ge(gelu_out, 1)
                    cmp_w2 = prm("cmp_w2").rearrange("p (s n) -> p s n", s=2)
                    o = begin(JOBS["cmp"] + 7)
                    for g in range(2):
                        ins = pe.matmul(o[64 * g:64 * g + 64, 0:32], cmp_w2[:, 0, :], chid[:, 6, 32 * g:32 * g + 32],
                                        start=True, stop=True)
                    ins.then_inc(proj_ready, 1)
                    o = begin(JOBS["cmp"] + 8)
                    for j in range(4):
                        for g in range(2):
                            ins = pe.matmul(o[32 * j:32 * j + 32, 64 * g:64 * g + 64], chid[:, 7, 32 * g:32 * g + 32],
                                            cmp_w2[:, 1, :], start=True, stop=True)
                    ins.then_inc(proj_ready, 1)
                elif step == first_cmp - first_nsa:
                    copied_all(pe, "cmp", 9)

            attention(first_nsa, n_items - first_nsa, compress)
            attended(n_items)
            pe.wait_ge(cmp_added, NT)
            out_projection(2, "no")
            mlp(1)

        @block.scalar
        def _(act):
            chain = [0]

            def link(ins):
                chain[0] += 1
                ins.then_inc(act_chain, 1)
                act.wait_ge(act_chain, chain[0])

            def A(o, i, f, **kw):
                return nc.scalar.activation(o, i, f, **kw)

            def evac(n, o, width=512, f=ACT.Copy, **kw):
                product(act, n)
                A(o, bank(n)[:, 0:width], f, **kw).then_inc(proj_evacuated[n % 2], 1)

            def norm_tile(n, t):
                c = slice(NT * n + t, NT * n + t + 1)
                nth = NT * n + t + 1
                if n == 0:
                    act.wait_ge(x_loaded[t], 16)
                elif n == 2:
                    act.wait_ge(combined, t + 1)
                else:
                    stage = {1: "wo", 3: "ao", 4: "mlp0", 5: "no", 6: "mlp1"}[n]
                    copied(act, job(stage, WIDTH[stage] + t - (NT if n == 6 else 0)))
                A(tok[:, t, :], x[:, t, :], ACT.Square, accum_out=ss[:, c]).then_inc(sumsq_ready, 1)
                act.wait_ge(mean_ready, nth)
                A(rstd[:, c], ss[:, c], ACT.Sqrt).then_inc(root_ready, 1)
                if n < len(NORMS):
                    act.wait_ge(rstd_ready, nth)
                    A(tok[:, t, :], x[:, t, :], ACT.Copy, scale=rstd[:, c]).then_inc(normed, 1)

            def norm_high(n, t):
                for half in range(2):
                    m = norm_turn(n, t, half)
                    copied(act, m)
                    A(hT_hi[:, 4 * half:4 * half + 4, t * P:(t + 1) * P], turned_whole(t, half), ACT.Copy).then_inc(normed_hi, 1)

            def norm(n):
                for t in range(NT):
                    norm_tile(n, t)
                    if n in SPLIT_NORMS and t >= 2:
                        norm_high(n, t - 2)
                if n in SPLIT_NORMS:
                    for t in (NT - 2, NT - 1):
                        norm_high(n, t)
                if n == 1:
                    act.wait_ge(normed, NT * 2)
                    act.dma_start(rows_dram.rearrange("(t p) d -> p t d", p=P), tok[:, :, :]).then_inc(rows_stored, 16)

            def attention(first, count, meanwhile=None):
                for i in range(first, first + count + 2):
                    if meanwhile:
                        meanwhile(i - first)
                    k = i - 2
                    if first <= k < first + count:
                        act.wait_ge(turned, k + 1)
                        if k >= 2:
                            act.wait_ge(values_ready, k - 1)
                        n = P * len(items[k]["blocks"])
                        A(PT[k % 2][:, 0:n], psT[k % 2][:, 0:n], ACT.Copy).then_inc(turned_copied, 1)
                    if i < first + count:
                        it = items[i]
                        act.wait_ge(masked, i + 1)
                        if i >= 3:
                            act.wait_ge(turned, i - 2)
                            if items[i - 3]["kind"] == "cmp":
                                act.wait_ge(factor_ready, i - 2)
                        if it["kind"] == "cmp":
                            A(PR[i % 3][:, 0:256], S[i % 2][:, 0:256], ACT.Exp).then_inc(probs_ready, 1)
                        else:
                            if it["kind"] == "band":
                                A(esink[:, i:i + 1], prm("sink")[:, it["head"]:it["head"] + 1], ACT.Exp,
                                  bias=negm[:, i:i + 1])
                            A(PR[i % 3][:, 0:it["n"]], S[i % 2][:, 0:it["n"]], ACT.Exp, bias=negm[:, i:i + 1],
                              scale=-1.0, accum_out=sums[:, i:i + 1]).then_inc(probs_ready, 1)

            def split_weight(c):
                name = SPLIT[c][0]
                act.wait_ge(w_arrived[slot_of[name]], arrived_at[name])
                piece_used(act, c)
                A(part(w_hi, c), raw_piece(c), ACT.Copy).then_inc(weight_hi, 1)

            def then_split(c):
                if c + 2 < len(SPLIT) and SPLIT[c + 2][5] == SPLIT[c][5]:
                    split_weight(c + 2)

            def out_projection(n, name):
                first = SPLIT_AT[name + "0"]
                for k in range(KD):
                    m = JOBS[f"turn_o{n}"] + k
                    product(act, m)
                    A(hT_hi[:, k, :], bank(m)[:, :], ACT.Copy).then_inc(out_hi, 1)
                    if k < 2:
                        split_weight(first + k)
                for c in range(3):
                    then_split(first + c)
                    if c == 0:
                        A(small[:, 310:311], ident[:, 0:1], ACT.Sqrt)
                norm(TAIL[name])
                then_split(first + 3)

            def mlp(l):
                for kind, e, first in MLP_STEPS:
                    for half in range(2):
                        if kind == "up":
                            for f in range(2 * half, 2 * half + 2):
                                n, nth = job(f"mlp{l}", first + f), l * NF + e * UP_JOBS + f
                                product(act, n)
                                if nth >= 2:
                                    act.wait_ge(hidden_lo, nth - 1)
                                A(S[f % 2], bank(n)[:, :], ACT.Relu).then_inc(proj_evacuated[n % 2], 1)
                                copied(act, n)
                                A(hid_hi[e % 2][:, f, :], S[f % 2], ACT.Square).then_inc(hidden_hi, 1)
                        elif e == EIGHTHS - 1 and half:
                            norm({0: 4, 1: 6}[l])
                        then_split(SPLIT_AT[f"{kind}{l}{e}"] + half)

            for dst, src in loads:
                act.dma_start(dst, src).then_inc(const_loaded, 16)
            norm_tile(0, 0)
            evac(JOBS["vec"], vec[:, :], 64)
            for t in range(1, NT):
                norm_tile(0, t)
            for dst, src in later_loads:
                act.dma_start(dst, src).then_inc(params_loaded, 16)
            copied(act, JOBS["vec"])
            act.wait_ge(const_loaded, CONST_LOADS * 16)
            for half in range(2):
                copied(act, norm_turn(0, NT - 1, half))
            for k in range(KD):
                A(hT_hi_early[:, k, :], hT[:, k, :], ACT.Copy).then_inc(early_in_hi, 1)
            for t in range(NT):
                if t < 2:
                    split_weight(SPLIT_AT["q"] + t)
                n = JOBS["kv"] + t
                product(act, n)
                A(qk[:, t, 512:640], bank(n)[:, 0:P], ACT.Copy)
                A(v1[:, t, :], bank(n)[:, P:2 * P], ACT.Copy).then_inc(proj_evacuated[n % 2], 1)
            for c in range(2):
                split_weight(SPLIT_AT["cc"] + c)
            act.wait_ge(early_in_hi, KD)
            act.wait_ge(early_in_lo, KD)
            for k in range(KD):
                A(hT_hi[:, k, :], hT_hi_early[:, k, :].bitcast(F32), ACT.Copy).then_inc(early_in_moved, 1)
            for m in range(4):
                evac(JOBS["cc"] + m, u[:, m, 1:T + 1])
                then_split(SPLIT_AT["cc"] + m)
            act.wait_ge(head_mean, 1)
            A(qss[:, 0:40], qss[:, 0:40], ACT.Sqrt).then_inc(head_root, 1)
            for c in range(8):
                then_split(SPLIT_AT["cx"] + c)
            act.wait_ge(early_in_moved, KD)
            for m in range(KD):
                evac(JOBS["ga"] + m, ga[:, m, :], f=ACT.Sigmoid)
                then_split(SPLIT_AT["ga0"] + m)

            def conv_gate(c):
                for m in range(4):
                    evac(JOBS[f"gc{c}"] + m, gc[:, 4 * c + m, :], f=ACT.Sigmoid)
                    then_split(SPLIT_AT[f"gc{c}"] + m)

            product(act, JOBS["ga"] + KD - 1)
            conv_gate(0)
            for j in range(5):
                evac(JOBS["turn_q"] + j, qT1[:, j, :] if j < 4 else kT1)

            act.wait_ge(params_loaded, PARAM_LOADS * 16)
            merge_piece = SPLIT_AT["cp"]

            def gates_and_weights(step):
                if step == 2:
                    conv_gate(1)
                elif step == 8:
                    split_weight(merge_piece)

            attention(0, n_band, gates_and_weights)
            act.wait_ge(values_ready, n_band)
            split_weight(merge_piece + 1)
            for c in range(4):
                product(act, JOBS["turn_o0"] + c)
                A(attn_hi[:, c, :], bank(JOBS["turn_o0"] + c)[:, :], ACT.Copy).then_inc(attn_in_hi, 1)
            first = SPLIT_AT["wo0"]
            for m in range(KD):
                if m % 2 and m < KD - 1:
                    then_split(merge_piece + m - 1)
                    then_split(merge_piece + m)
                elif m == KD - 2:
                    for c in range(2):
                        split_weight(first + c)
                act.wait_ge(merged, m + 1)
                A(merged_hi[:, m, :], merged_whole[:, m, :], ACT.Copy).then_inc(merged_in_hi, 1)
            for c in range(2):
                then_split(first + c)

            norm(1)
            act.wait_ge(logits_shifted, 1)
            A(gexp, gexp, ACT.Exp).then_inc(logits_exp, 1)
            A(pexp, pexp, ACT.Exp).then_inc(logits_exp, 1)

            def hidden_out(p, i, ahead):
                n = moe_product(p, i, "hidden", ahead)
                product(act, n, i)
                A(ehidT[:, (p + ahead) % 2, :], bank(n)[:, 0:F_E], ACT.Copy).then_inc(proj_evacuated[n % 2], 1)

            def outputs(p, i, ahead):
                q, nth = (p + ahead) % 2, (p + ahead) // 2
                n = moe_product(p, i, "down", ahead)
                if not before(p, i, 2 - ahead):
                    act.wait_ge(y_written[q], i * 16 + 16 * nth)
                for half in range(2):
                    product(act, n + half, i)
                    A(ey[:, q, half * 512:(half + 1) * 512], bank(n + half)[:, :], ACT.Copy)\
                        .then_inc(proj_evacuated[(n + half) % 2], 1)

            def store(p, i, ahead):
                q, n = (p + ahead) % 2, moe_product(p, i, "down", ahead)
                for half in range(2):
                    copied(act, n + half, i)
                row = i * (2 * P) + (p + ahead) * P
                act.dma_start(y_dram[bass.ds(row, P), :], ey[:, q, :]).then_inc(y_written[q], 16)

            def expert_block(p, i, last=False):
                if not before(p, i, 1):
                    hidden_out(p, i, -1)
                if not before(p, i, 2):
                    store(p, i, -2)
                act.wait_ge(gu_ready, i * 2 + (p + 1))
                if not before(p, i, 2):
                    act.wait_ge(gu_taken, i * 2 + (p - 1))
                A(sg[:, p, :], psS[p][:, 0:F_E], ACT.Sigmoid).then_inc(silu_ready, 1)
                if not before(p, i, 1):
                    outputs(p, i, -1)
                if last:
                    hidden_out(p, i, 0)
                    store(p, i, -1)
                    outputs(p, i, 0)
                    store(p, i, 0)

            def spill_block(j):
                act.wait_ge(spill_gu, j)
                A(sg[:, 0, :], psS[0][:, 0:F_E], ACT.Sigmoid).then_inc(spill_silu, 1)
                act.wait_ge(spill_hidden_turned, j)
                A(ehidT[:, 0, :], psS[1][:, 0:F_E], ACT.Copy).then_inc(spill_hidden_copied, 1)
                act.wait_ge(spill_down, j)
                A(ey[:, 0, 0:512], psO[0][:, :], ACT.Copy)
                A(ey[:, 0, 512:1024], psO[1][:, :], ACT.Copy).then_inc(spill_copied, 1)
                act.wait_ge(spill_copied, j)
                act.dma_start(y_dram[bass.ds(j * P + (E - 1) * P, P), :], ey[:, 0, :]).then_inc(spill_written, 16)
                act.wait_ge(spill_written, j * 16)

            moe_pairs(act, expert_block)
            with act.If(spilled(act) > 0):
                act.wait_ge(y_written[0], 16 * (E // 2))
                with act.Fori(1, SPILL + 1) as j:
                    spill_block(j)

            norm(2)
            for half in range(2):
                copied(act, norm_turn(2, NT - 1, half))
            for k in range(KD):
                A(second_hi[:, k, :], hT[:, k, :], ACT.Copy).then_inc(second_in_hi, 1)
            first = SPLIT_AT["ai"]
            for t in range(NT):
                n = JOBS["ax"] + t
                product(act, n)
                if t == 0:
                    act.wait_ge(latent_zeroed, 3)
                o = bank(n)
                A(ckv[:, t, :], o[:, 0:256], ACT.Copy)
                A(krd[:, t, 0:2 * ROT], o[:, 256:272], ACT.Copy)
                A(kid[:, t, 0:HD], o[:, 272:336], ACT.Copy)
                A(wb[:, t, :], o[:, 336:352], ACT.Copy).then_inc(proj_evacuated[n % 2], 1)
                if 1 <= t <= 2:
                    split_weight(first + t - 1)

            def index_queries(half, tiles):
                for t in tiles:
                    evac(JOBS["ai"] + NT * half + t, tok[:, t, 512 + 256 * half:768 + 256 * half], 256)

            index_queries(0, range(2))
            act.wait_ge(head_mean, 2)
            A(qss[:, 0:8], qss[:, 0:8], ACT.Sqrt).then_inc(head_root, 1)
            act.wait_ge(forget_z, 1)
            link(A(sp_part(1), sp_part(0), ACT.Abs))
            link(A(sp_part(1), sp_part(1), ACT.Exp, scale=-1.0))
            A(sp_part(1), sp_part(1), ACT.Ln, bias=1.0).then_inc(forget_ln, 1)
            index_queries(0, range(2, NT))
            then_split(first)
            index_queries(1, range(NT))
            for c in range(1, 4):
                then_split(first + c)
            for half in range(2):
                for t in range(NT):
                    evac(JOBS["bv"] + NT * half + t, bv[:, t, 256 * half:256 * (half + 1)], 256)
            evac(JOBS["turn_small"], kiT)
            evac(JOBS["turn_small"] + 1, krT)
            for m in range(2):
                evac(JOBS["turn_small"] + 2 + m, ckvT[:, m, :])
            for t in range(NT):
                evac(JOBS["vh"] + t, vh[:, t, :])
            for j in range(4):
                evac(JOBS["turn_qi"] + j, qiT[:, j, :])
            n = JOBS["forget"]
            product(act, n)
            A(ncum[0:8, :], bank(n)[0:8, :], ACT.Copy).then_inc(proj_evacuated[n % 2], 1)
            for c in range(8 * (NT - 1)):
                if c >= 2:
                    act.wait_ge(relu_used, c - 1)
                n = (c // 8 + 2) * P
                evac(JOBS["index"] + c, S[c % 2][:, 0:n], n, ACT.Relu)
            for m in range(4):
                evac(JOBS["bq"] + m, bqT[:, m, :], scale=SCALE)
            for j in range(4):
                evac(JOBS["turn_aq"] + j, aqT[:, j, :])
            evac(JOBS["bk"], bkT[:, 0, :])

            def further_keys(step):
                for m in range(1, 4) if step == 2 else ():
                    evac(JOBS["bk"] + m, bkT[:, m, :])

            attention(first_fox, first_nsa - first_fox, further_keys)
            out_projection(1, "ao")
            mlp(0)

            for half in range(2):
                for t in range(NT):
                    evac(JOBS["nk"] + NT * half + t, kv2[:, t, 256 * half:256 * (half + 1)], 256)
                then_split(SPLIT_AT["nk"] + half)
            for half in range(2):
                for t in range(NT):
                    n = JOBS["nv"] + NT * half + t
                    if half == 0:
                        evac(n, kv2[:, t, 512:664], 152)
                    else:
                        product(act, n)
                        A(kv2[:, t, 664:768], bank(n)[:, 0:104], ACT.Copy)
                        A(gate2[:, t, :], bank(n)[:, 104:152], ACT.Copy).then_inc(proj_evacuated[n % 2], 1)
                then_split(SPLIT_AT["nv"] + half)
            for c in range(2):
                then_split(SPLIT_AT["nq0"] + c)
            act.wait_ge(gate_ready, 1)
            A(a4["gate"], a4["gate"], ACT.Sigmoid).then_inc(gate_ready, 1)
            for c in range(2):
                evac(JOBS["turn_nk"] + c, kT2[:, c, :])
            for j in range(8):
                evac(JOBS["turn_nq"] + j, qT2[:, j, :])

            def compress(step):
                if step == CMP_TURN:
                    for g in range(2):
                        shifted(JOBS["cmp"] + g, win[:, 0, g, :], lambda o, i: A(o, i, ACT.Copy), act)
                elif step == CMP_TURN + 2:
                    n = JOBS["cmp"] + 4
                    product(act, n)
                    act.wait_ge(cmp_zeroed, 4)
                    for s in range(2):
                        A(win[0:HD, s, 2, 0:CMP_LEN], bank(n)[0:HD, s * P:s * P + CMP_LEN], ACT.Copy)
                        ins = A(win[HD:P, s, 2, 0:CMP_LEN - 1], bank(n)[HD:P, s * P + 1:s * P + CMP_LEN], ACT.Copy)
                    ins.then_inc(proj_evacuated[n % 2], 1)
                elif step == CMP_FIRST + 8:
                    act.wait_ge(gelu_in, 1)
                    A(cpart(2), cpart(1), ACT.Exp, scale=-2 * GELU_C).then_inc(gelu_exp, 1)
                elif step == CMP_SECOND + 2:
                    n = JOBS["cmp"] + 7
                    product(act, n)
                    A(kcBD[0:HD, 0:32], bank(n)[0:HD, 0:32], ACT.Copy)
                    A(kcBD[HD:P, 32:64], bank(n)[HD:P, 0:32], ACT.Copy).then_inc(proj_evacuated[n % 2], 1)

            attention(first_nsa, n_items - first_nsa, compress)
            out_projection(2, "no")
            mlp(1)

        @block.vector
        def _(dve):
            chain = [0]

            def link(ins):
                chain[0] += 1
                ins.then_inc(dve_chain, 1)
                dve.wait_ge(dve_chain, chain[0])

            def tt(o, a, b, op):
                return nc.vector.tensor_tensor(o, a, b, op)

            def ts(o, a, s1, s2=None, op0=ALU.mult, op1=None):
                if op1 is None:
                    return nc.vector.tensor_scalar(o, a, s1, None, op0)
                return nc.vector.tensor_scalar(o, a, s1, s2, op0, op1)

            def evac_to(n):
                product(dve, n)
                return bank(n)

            def norm_scale(n, t):
                c, nth = slice(NT * n + t, NT * n + t + 1), NT * n + t + 1
                dve.wait_ge(sumsq_ready, nth)
                ts(ss[:, c], ss[:, c], 1.0 / D, EPS, ALU.mult, ALU.add).then_inc(mean_ready, 1)
                dve.wait_ge(root_ready, nth)
                nc.vector.reciprocal(rstd[:, c], rstd[:, c]).then_inc(rstd_ready, 1)

            def norm_whole(n, t):
                g = GAINS[NORMS[n]]
                for half in range(2):
                    m = norm_turn(n, t, half)
                    if n in SPLIT_NORMS and 2 * t + half >= 6:
                        dve.wait_ge(normed_lo, 2 * NT * SPLIT_NORMS.index(n) + 2 * t + half - 5)
                    dst = turned_whole(t, half) if n in SPLIT_NORMS else hT[:, 4 * half:4 * half + 4, t * P:(t + 1) * P]
                    gain = vec[:, g + 4 * half:g + 4 * half + 4].unsqueeze(2).broadcast_to([P, 4, P])
                    tt(dst, evac_to(m).rearrange("p (k n) -> p k n", k=4), gain, ALU.mult).then_inc(proj_evacuated[m % 2], 1)

            def norm_low(n, t):
                for half in range(2):
                    dve.wait_ge(normed_hi, 2 * NT * SPLIT_NORMS.index(n) + 2 * t + half + 1)
                    to = (slice(None), slice(4 * half, 4 * half + 4), slice(t * P, (t + 1) * P))
                    tt(hT_lo[to], turned_whole(t, half), hT_hi[to].bitcast(F32), ALU.subtract).then_inc(normed_lo, 1)

            def norm(n, add=None):
                for t in range(NT):
                    if add:
                        add(t)
                    if t >= 2 and n < len(NORMS):
                        norm_whole(n, t - 2)
                    norm_scale(n, t)
                    if n == len(NORMS):
                        dve.wait_ge(rstd_ready, NT * n + t + 1)
                        nc.vector.scalar_tensor_tensor(out=tok[:, t, :], in0=x[:, t, :], scalar=rstd[:, NT * n + t:NT * n + t + 1],
                                                       in1=prm("final"), op0=ALU.mult, op1=ALU.mult).then_inc(final_ready, 1)
                if n < len(NORMS):
                    for t in (NT - 2, NT - 1):
                        norm_whole(n, t)
                        if n in SPLIT_NORMS:
                            norm_low(n, t - 2)
                    if n in SPLIT_NORMS:
                        for t in (NT - 2, NT - 1):
                            norm_low(n, t)

            def add_to_x(stage, i, t, c0, c1):
                n = job(stage, i)
                xs = x[:, t, c0:c1]
                tt(xs, evac_to(n)[:, 0:c1 - c0], xs, ALU.add).then_inc(proj_evacuated[n % 2], 1)

            def rope(view, heads, temps, signal=None):
                x1, x2 = view[:, :, :, 0:ROT], view[:, :, :, ROT:2 * ROT]
                shape = [P, NT, heads, ROT]
                n = NT * heads * ROT
                t1, t2, t3, t4 = (temps[:, k * n:(k + 1) * n].rearrange("p (t h c) -> p t h c", t=NT, h=heads)
                                  for k in range(4))
                c, s = cos4.unsqueeze(2).broadcast_to(shape), sin4.unsqueeze(2).broadcast_to(shape)
                tt(t1, x1, c, ALU.mult)
                tt(t2, x2, s, ALU.mult)
                tt(t3, x2, c, ALU.mult)
                link(tt(t4, x1, s, ALU.mult))
                tt(x1, t1, t2, ALU.subtract)
                if signal is None:
                    link(tt(x2, t3, t4, ALU.add))
                else:
                    tt(x2, t3, t4, ALU.add).then_inc(signal, 1)

            def attention(first, count, meanwhile=None):
                for i in range(first, first + count + 3):
                    if i < first + count:
                        it = items[i]
                        dve.wait_ge(scores_ready, i + 1)
                        if i >= 2:
                            dve.wait_ge(probs_ready, i - 1)
                        if it["kind"] == "cmp":
                            s3 = S[i % 2][:, 0:256].rearrange("p (j n) -> p j n", j=8)
                            st = cmpst[:, it["index"], :]
                            link(tt(s3, psS[i % 2][:, 0:256].rearrange("p (j n) -> p j n", j=8),
                                    cmpmask[:, it["t"], :].unsqueeze(1).broadcast_to([P, 8, 32]), ALU.add))
                            link(nc.vector.tensor_reduce(st, s3, X, ALU.max))
                            tt(s3, s3, st.unsqueeze(2).broadcast_to([P, 8, 32]), ALU.subtract).then_inc(masked, 1)
                        else:
                            floor = negsink[:, it["head"]:it["head"] + 1] if it["kind"] == "band" else 3e38
                            nc.vector.tensor_tensor_reduce(
                                out=S[i % 2][:, 0:it["n"]], in0=psS[i % 2][:, 0:it["n"]], in1=it["mask"], scale=-1.0,
                                scalar=floor, op0=ALU.add, op1=ALU.min, accum_out=negm[:, i:i + 1]).then_inc(masked, 1)
                    k = i - 2
                    if first <= k < first + count:
                        factor(k)
                    k = i - 3
                    if first <= k < first + count:
                        finish(k)
                    k = i - 2
                    if first <= k < first + count and items[k]["kind"] == "pair":
                        gate_factor(k)
                    if meanwhile:
                        meanwhile(i - first)

            def factor(k):
                it, t = items[k], items[k]["t"]
                f, total = fac[:, k:k + 1], sums[:, k:k + 1]
                dve.wait_ge(probs_ready, k + 1)
                if it["kind"] == "cmp":
                    st = cmpst[:, it["index"], :]
                    link(nc.vector.tensor_reduce(st, PR[k % 3][:, 0:256].rearrange("p (j n) -> p j n", j=8), X, ALU.add))
                    link(nc.vector.reciprocal(st, st))
                    nc.vector.scalar_tensor_tensor(
                        out=st.rearrange("p (j g) -> p j g", g=2), in0=st.rearrange("p (j g) -> p j g", g=2),
                        scalar=cmpok[:, t:t + 1],
                        in1=gate2[:, t, :].rearrange("p (g j r) -> p j g r", g=2, r=3)[:, 4 * it["c"]:4 * it["c"] + 4, :, 0],
                        op0=ALU.mult, op1=ALU.mult).then_inc(factor_ready, 1)
                elif it["kind"] == "pair":
                    nc.vector.reciprocal(f, total).then_inc(inverted, 1)
                else:
                    if it["kind"] == "band":
                        link(tt(total, total, esink[:, k:k + 1], ALU.add))
                    nc.vector.reciprocal(f, total).then_inc(factor_ready, 1)

            def gate_factor(k):
                f = fac[:, k:k + 1]
                dve.wait_ge(inverted, items[k]["nth"])
                tt(f, f, items[k]["gate"], ALU.mult).then_inc(factor_ready, 1)

            def taken(k):
                dve.wait_ge(out_taken[k % 2], k // 2 + 1)

            def finish(k):
                it, t = items[k], items[k]["t"]
                f, o = fac[:, k:k + 1], psO[k % 2]
                dve.wait_ge(values_ready, k + 1)
                dve.wait_ge(factor_ready, k + 1)
                if it["kind"] == "cmp":
                    st = cmpst[:, it["index"], :]
                    heads = tok[:, t, :].rearrange("p (g j d) -> p j g d", g=2, d=HD)[:, 4 * it["c"]:4 * it["c"] + 4, :, :]
                    scale = st.unsqueeze(2).broadcast_to([P, 8, HD])
                    if it["c"]:
                        tt(heads, o[:, :].rearrange("p (j g d) -> p j g d", j=4, g=2),
                           scale.rearrange("p (j g) d -> p j g d", g=2), ALU.mult).then_inc(out_taken[k % 2], 1)
                        return
                    if it["index"] > NT:
                        dve.wait_ge(cmp_added, it["index"] - NT)
                    tt(cmpout.rearrange("p (j d) -> p j d", d=HD), o[:, :].rearrange("p (j d) -> p j d", d=HD),
                       scale, ALU.mult).then_inc(out_taken[k % 2], 1)
                    for h in range(8):
                        taken(pair_at[8 * (h // 4) + h % 4, 1, t])
                    taken(k)
                    tt(heads, heads, cmpout.rearrange("p (j g d) -> p j g d", j=4, g=2), ALU.add).then_inc(cmp_added, 1)
                    return
                dst = tok[:, t, it["head"] * HD:(it["head"] + 1) * HD]
                h = it["head"]
                if it["kind"] == "pair" and (it["branch"] or h % 8 >= 4):
                    taken(pair_at[h, 0, t] if it["branch"] else cmp_items[t])
                    nc.vector.scalar_tensor_tensor(out=dst, in0=o[:, 0:HD], scalar=f, in1=dst, op0=ALU.mult,
                                                   op1=ALU.add).then_inc(out_taken[k % 2], 1)
                else:
                    ts(dst, o[:, 0:HD], f).then_inc(out_taken[k % 2], 1)

            def out_projection(n, name):
                for k in range(KD):
                    m = JOBS[f"turn_o{n}"] + k
                    dve.wait_ge(out_hi, (n - 1) * KD + k + 1)
                    tt(hT_lo[:, k, :], evac_to(m)[:, :], hT_hi[:, k, :].bitcast(F32), ALU.subtract).then_inc(out_lo, 1)
                    dve.wait_ge(out_lo, (n - 1) * KD + k + 1)
                    nc.vector.nop().then_inc(proj_evacuated[m % 2], 1)
                for c in range(3):
                    for t in range(NT):
                        add_to_x(name, NT * c + t, t, 256 * c, 256 * (c + 1))
                norm(TAIL[name], lambda t: add_to_x(name, 3 * NT + t, t, 768, 1024))

            def mlp(l):
                for kind, e, first in MLP_STEPS:
                    for half in range(2):
                        if kind == "up":
                            for f in range(2 * half, 2 * half + 2):
                                nth = l * NF + e * UP_JOBS + f
                                dve.wait_ge(hidden_hi, nth + 1)
                                tt(PR[f % 2], S[f % 2], S[f % 2], ALU.mult).then_inc(squared, 1)
                                dve.wait_ge(squared, nth + 1)
                                tt(hid_lo[e % 2][:, f, :], PR[f % 2], hid_hi[e % 2][:, f, :].bitcast(F32), ALU.subtract)\
                                    .then_inc(hidden_lo, 1)
                        elif e == EIGHTHS - 1 and half:
                            norm({0: 4, 1: 6}[l], lambda t: add_to_x(f"mlp{l}", first + NT + t, t, 512, 1024))
                        else:
                            for t in range(NT):
                                add_to_x(f"mlp{l}", first + NT * half + t, t, 512 * half, 512 * (half + 1))

            nc.vector.memset(u[:, :, 0:T + 2:T + 1], 0.0)

            def gains(t):
                if t == 2:
                    dve.wait_ge(const_loaded, CONST_LOADS * 16)
                    copied(dve, JOBS["vec"])

            norm(0, gains)
            for half in range(2):
                copied(dve, norm_turn(0, NT - 1, half))
            for k in range(KD):
                dve.wait_ge(early_in_hi, k + 1)
                tt(hT_lo_early[:, k, :], hT[:, k, :], hT_hi_early[:, k, :].bitcast(F32), ALU.subtract).then_inc(early_in_lo, 1)
            for g in range(2):
                for t in range(NT):
                    n = JOBS["q"] + NT * g + t
                    nc.vector.tensor_copy(qk[:, t, 0:512].rearrange("p (j g d) -> p j g d", j=4, g=2)[:, :, g, :],
                                          evac_to(n)[:, 0:256].rearrange("p (j d) -> p j d", j=4))\
                        .then_inc(proj_evacuated[n % 2], 1)
            copied_all(dve, "q", 2 * NT)
            copied_all(dve, "kv", NT)
            qk4 = qk.rearrange("p t (h d) -> p (t h) d", d=HD)
            squares = a1["ga"][:, 0:NT * 640].rearrange("p (t n) -> p t n", t=NT)
            sq4 = squares.rearrange("p t (h d) -> p t h d", d=HD)
            qss3 = qss[:, 0:40].rearrange("p (t h) -> p t h", t=NT)
            for t in range(NT):
                last = tt(squares[:, t, :], qk[:, t, :], qk[:, t, :], ALU.mult)
            link(last)
            link(nc.vector.tensor_reduce(qss3, sq4, X, ALU.add))
            ts(qss[:, 0:40], qss[:, 0:40], 1.0 / HD, EPS, ALU.mult, ALU.add).then_inc(head_mean, 1)
            for m in range(4):
                n = JOBS["cx"] + m
                o = evac_to(n)
                copied(dve, JOBS["cc"] + m)
                tt(u[:, m, 1:T + 1], o[:, :], u[:, m, 1:T + 1], ALU.mult).then_inc(proj_evacuated[n % 2], 1)
            copied_all(dve, "cx", 4)
            for m in range(4):
                cw = [vec[:, CONVW + 4 * j + m:CONVW + 4 * j + m + 1] for j in range(3)]
                cb = vec[:, CONVB + m:CONVB + m + 1]
                link(ts(conv[:, m, :], u[:, m, 0:T], cw[0], cb, ALU.mult, ALU.add))
                for j in (1, 2):
                    link(nc.vector.scalar_tensor_tensor(out=conv[:, m, :], in0=u[:, m, j:j + T], scalar=cw[j],
                                                        in1=conv[:, m, :], op0=ALU.mult, op1=ALU.add))
                n = JOBS["cb"] + m
                o = evac_to(n)
                tt(conv[:, m, :], o[:, :], conv[:, m, :], ALU.mult).then_inc(proj_evacuated[n % 2], 1)
            dve.wait_ge(head_root, 1)
            link(nc.vector.reciprocal(qss[:, 0:40], qss[:, 0:40]))
            link(ts(qss3[:, :, 0:8], qss3[:, :, 0:8], SCALE))
            link(tt(qk4, qk4, qss[:, 0:40].unsqueeze(2).broadcast_to([P, 40, HD]), ALU.mult))
            dve.wait_ge(params_loaded, PARAM_LOADS * 16)
            link(ts(negsink, prm("sink"), -1.0))
            link(tt(qk, qk, prm("qk_gain").unsqueeze(1).broadcast_to([P, NT, 640]), ALU.mult))
            rope(qk.rearrange("p t (h d) -> p t h d", d=HD), 10, scr.rearrange("p a n -> p (a n)"),
                 heads_ready)
            attention(0, n_band)
            for c in range(4):
                n = JOBS["turn_o0"] + c
                dve.wait_ge(attn_in_hi, c + 1)
                tt(attn_lo[:, c, :], evac_to(n)[:, :], attn_hi[:, c, :].bitcast(F32), ALU.subtract).then_inc(attn_in_lo, 1)
                dve.wait_ge(attn_in_lo, c + 1)
                nc.vector.nop().then_inc(proj_evacuated[n % 2], 1)

            def merged_low(m):
                dve.wait_ge(merged_in_hi, m + 1)
                tt(merged_lo[:, m, :], merged_whole[:, m, :], merged_hi[:, m, :].bitcast(F32), ALU.subtract).then_inc(merged_in_lo, 1)

            for m in range(KD):
                for c, gate in enumerate((gc, ga)):
                    n = JOBS["merge"] + 2 * m + c
                    o = evac_to(n)
                    tt(gate[:, m, :], o[:, :], gate[:, m, :], ALU.mult).then_inc(proj_evacuated[n % 2], 1)
                for c in range(2):
                    copied(dve, JOBS["merge"] + 2 * m + c)
                tt(merged_whole[:, m, :], ga[:, m, :], gc[:, m, :], ALU.add).then_inc(merged, 1)
                if m:
                    merged_low(m - 1)
            merged_low(KD - 1)
            for c in range(3):
                for t in range(NT):
                    add_to_x("wo", NT * c + t, t, 256 * c, 256 * (c + 1))

            norm(1, lambda t: add_to_x("wo", 3 * NT + t, t, 768, 1024))
            logit = a2["logit"].rearrange("p (t n) -> p t n", t=NT)
            dve.wait_ge(logits_ready, NT)
            link(tt(logit, psS[0][:, 0:NT * 36].rearrange("p (t n) -> p t n", t=NT),
                    prm("router_b").unsqueeze(1).broadcast_to([P, NT, 36]), ALU.add))
            gl, el = logit[:, :, 0:G], logit[:, :, G:36]

            def bc(a, shape):
                return a.unsqueeze(2).broadcast_to(shape)

            def first_max(values, width, best, work, hot):
                shape = [P, NT, width]
                link(nc.vector.tensor_reduce(best, values, X, ALU.max))
                link(tt(work, values, bc(best, shape), ALU.is_equal))
                link(tt(work, work, iota[:, 0:width].unsqueeze(1).broadcast_to(shape), ALU.mult))
                link(nc.vector.tensor_reduce(where, work, X, ALU.min))
                link(tt(hot, iota[:, 0:width].unsqueeze(1).broadcast_to(shape), bc(where, shape), ALU.is_equal))

            def s4(k):
                return a2["s"][:, 4 * k:4 * k + 4]

            where, gbest, best1, best2, den, pick = (s4(k) for k in range(6))
            g16 = a2["w1"][:, 0:16].rearrange("p (t n) -> p t n", t=NT)
            hot_g = a2["w1"][:, 16:32].rearrange("p (t n) -> p t n", t=NT)
            work = a2["w2"][:, 0:128].rearrange("p (t n) -> p t n", t=NT)
            inside = a2["w3"][:, 0:128].rearrange("p (t n) -> p t n", t=NT)
            oh = [a2[k].rearrange("p (t n) -> p t n", t=NT) for k in ("oh1", "oh2")]
            first_max(gl, G, gbest, g16, hot_g)
            link(tt(gexp.rearrange("p (t n) -> p t n", t=NT), gl, bc(gbest, [P, NT, G]), ALU.subtract))
            link(ts(g16, hot_g, -1.0, -NEG, ALU.add, ALU.mult))
            link(tt(inside.rearrange("p t (g e) -> p t g e", g=G), el.rearrange("p t (g e) -> p t g e", g=G),
                    g16.unsqueeze(3).broadcast_to([P, NT, G, EG]), ALU.add))
            first_max(inside, E, best1, work, oh[0])
            link(ts(work, oh[0], NEG))
            link(tt(inside, inside, work, ALU.add))
            first_max(inside, E, best2, work, oh[1])
            tt(asg, oh[0], oh[1], ALU.add).then_inc(assigned, 1)
            tt(pexp, best2, best1, ALU.subtract).then_inc(logits_shifted, 1)
            dve.wait_ge(logits_exp, 2)
            link(nc.vector.tensor_reduce(den, gexp.rearrange("p (t n) -> p t n", t=NT), X, ALU.add))
            link(ts(pick, pexp, 1.0, None, ALU.add))
            link(tt(den, den, pick, ALU.mult))
            link(nc.vector.reciprocal(g12[:, 0, :], den))
            link(tt(g12[:, 1, :], g12[:, 0, :], pexp, ALU.mult))
            n = JOBS["ranks"]
            o = evac_to(n)
            rank = a2["rank"].rearrange("p (t n) -> p t n", t=NT)
            cnt, spill, incl, obase = a2["cnt"], a2["spill"], a2["incl"], a2["obase"]
            nc.vector.tensor_copy(a2["rank"], o[:, 0:P])
            nc.vector.tensor_copy(cnt, o[:, P:P + E]).then_inc(proj_evacuated[n % 2], 1)
            copied(dve, n)

            def over(dst, src, tmp, strict):
                op = ALU.is_gt if strict else ALU.is_ge
                link(ts(dst, src, float(P), None, op))
                for k in (2, 3):
                    link(ts(tmp, src, float(k * P), None, op))
                    link(tt(dst, dst, tmp, ALU.add))

            w2_32 = a2["w2"][:, 128:160]
            over(spill, cnt, w2_32, True)
            link(nc.vector.memset(a2["w2"][:, 160:192], 1.0))
            link(nc.vector.tensor_tensor_scan(incl, a2["w2"][:, 160:192], spill, 0.0, ALU.mult, ALU.add))
            link(tt(obase, incl, spill, ALU.subtract))
            link(ts(obase, obase, float(E - 1), None, ALU.add))
            rk, ek, ob, q, tmp, blk, row = (a2["s"][:, 32 + 8 * j:40 + 8 * j] for j in range(7))
            shape = [P, 2, NT, E]
            both = big[:, at_oh:at_oh + 2 * NT * E].rearrange("p (k t n) -> p k t n", k=2, t=NT)
            work4 = a2["w3"][:, 0:256].rearrange("p (k t n) -> p k t n", k=2, t=NT)
            work8 = a2["w3"][:, 0:256].rearrange("p (c n) -> p c n", n=E)

            def each(a):
                return a[:, 0:E].unsqueeze(1).unsqueeze(1).broadcast_to(shape)

            link(tt(work4, both, rank.unsqueeze(1).broadcast_to(shape), ALU.mult))
            link(nc.vector.tensor_reduce(rk, work8, X, ALU.add))
            link(tt(work4, both, each(iota), ALU.mult))
            link(nc.vector.tensor_reduce(ek, work8, X, ALU.add))
            link(tt(work4, both, each(obase), ALU.mult))
            link(nc.vector.tensor_reduce(ob, work8, X, ALU.add))
            link(ts(ek, ek, 64.0, None, ALU.add))
            over(q, rk, tmp, False)
            link(tt(blk, ob, q, ALU.add))
            link(tt(blk, blk, ek, ALU.subtract))
            link(ts(tmp, q, 0.0, None, ALU.is_gt))
            link(tt(blk, blk, tmp, ALU.mult))
            link(tt(blk, blk, ek, ALU.add))
            link(nc.vector.scalar_tensor_tensor(out=row, in0=q, scalar=-float(P), in1=rk, op0=ALU.mult, op1=ALU.add))
            link(ts(tmp, row, -64.0, None, ALU.add))
            tt(hot_row, iota.unsqueeze(1).broadcast_to([P, 2 * NT, P]), bc(tmp, [P, 2 * NT, P]), ALU.is_equal)
            link(ts(ob, blk, -64.0, None, ALU.add))
            link(tt(hot_block, iota[:, 0:NB].unsqueeze(1).broadcast_to([P, 2 * NT, NB]), bc(ob, [P, 2 * NT, NB]), ALU.is_equal))
            token = cst("token").unsqueeze(1).unsqueeze(3).broadcast_to([P, 2, NT, NB])
            hot_block4 = hot_block.rearrange("p (k t) n -> p k t n", k=2)
            tt(hot_block4, hot_block4, token, ALU.mult).then_inc(slots_ready, 1)
            link(nc.vector.scalar_tensor_tensor(out=tmp, in0=blk, scalar=float(P), in1=row, op0=ALU.mult, op1=ALU.add))
            nc.vector.tensor_copy(yrow, tmp)
            n = JOBS["table"]
            o = evac_to(n)
            nc.vector.tensor_copy(slot_token, o[:, 0:NB]).then_inc(proj_evacuated[n % 2], 1)
            which, number = a2["s"][:, 88:88 + SPILL], a2["s"][:, 96:96 + SPILL]
            reach = a2["w1"][:, 64:64 + SPILL * E].rearrange("p (j n) -> p j n", j=SPILL)
            link(ts(number, iota[:, 0:SPILL], 64.0, None, ALU.add))
            link(tt(reach, incl.unsqueeze(1).broadcast_to([P, SPILL, E]),
                    number.unsqueeze(2).broadcast_to([P, SPILL, E]), ALU.is_le))
            link(nc.vector.tensor_reduce(which, reach, X, ALU.add))
            link(ts(which, which, float(E - 1), None, ALU.min))
            nc.vector.tensor_copy(spill_expert[:, 1:1 + SPILL], which)
            nc.vector.tensor_copy(spill_expert[:, 0:1], incl[:, E - 1:E]).then_inc(slots_ready, 1)

            gain2 = vec[:, GAINS["norm2_g"]:GAINS["norm2_g"] + KD]

            def turned_rows(p, n, i):
                for half in range(2):
                    o = bank(n + half)
                    product(dve, n + half, i)
                    tt(xT[:, p, 4 * half:4 * half + 4, :], o[:, :].rearrange("p (k n) -> p k n", k=4),
                       gain2[:, 4 * half:4 * half + 4].unsqueeze(2).broadcast_to([P, 4, P]), ALU.mult)\
                        .then_inc(proj_evacuated[(n + half) % 2], 1)

            def expert_block(p, i, last=False):
                if not last:
                    turned_rows(1 - p, moe_product(p, i, "turn", 1), i)
                o = psS[p]
                nth = i * 2 + (p + 1)
                dve.wait_ge(silu_ready, nth)
                tt(ehid[:, p, :], o[:, 0:F_E], sg[:, p, :], ALU.mult).then_inc(hidden_part, 1)
                dve.wait_ge(hidden_part, nth)
                tt(ehid[:, p, :], o[:, F_E:2 * F_E], ehid[:, p, :], ALU.mult).then_inc(gu_taken, 1)

            turned_rows(0, moe_job(0, "turn"), 0)
            moe_pairs(dve, expert_block)

            def spill_block(j):
                dve.wait_ge(spill_turned, j)
                for half in range(2):
                    ins = tt(xT[:, 0, 4 * half:4 * half + 4, :], psT[half][:, :].rearrange("p (k n) -> p k n", k=4),
                             gain2[:, 4 * half:4 * half + 4].unsqueeze(2).broadcast_to([P, 4, P]), ALU.mult)
                ins.then_inc(spill_scaled, 1)
                dve.wait_ge(spill_silu, j)
                tt(ehid[:, 0, :], psS[0][:, 0:F_E], sg[:, 0, :], ALU.mult).then_inc(spill_part, 1)
                dve.wait_ge(spill_part, j)
                tt(ehid[:, 0, :], psS[0][:, F_E:2 * F_E], ehid[:, 0, :], ALU.mult).then_inc(spill_hidden, 1)

            with dve.If(spilled(dve) > 0):
                with dve.Fori(1, SPILL + 1) as j:
                    spill_block(j)

            def combine(t):
                dve.wait_ge(picked[t], 32)
                for k in range(2):
                    ins = nc.vector.scalar_tensor_tensor(out=x[:, t, :], in0=rows_of[k][:, t, :], scalar=g12[:, k, t:t + 1],
                                                         in1=x[:, t, :], op0=ALU.mult, op1=ALU.add)
                    if k == 0:
                        link(ins)
                ins.then_inc(combined, 1)

            norm(2, combine)
            for k in range(KD):
                dve.wait_ge(second_in_hi, k + 1)
                tt(second_lo[:, k, :], hT[:, k, :], second_hi[:, k, :].bitcast(F32), ALU.subtract).then_inc(second_in_lo, 1)
            copied_all(dve, "ax", NT)
            sq = scr[:, 4:6, :].rearrange("p a n -> p (a n)")
            temps = scr.rearrange("p a n -> p (a n)")[:, 0:1024]
            link(tt(sq, a3["sel"][:, 0:1024], a3["sel"][:, 0:1024], ALU.mult))
            link(nc.vector.tensor_reduce(qss[:, 0:4], sq.rearrange("p (t n) -> p t n", t=NT), X, ALU.add))
            link(ts(qss[:, 0:4], qss[:, 0:4], 1.0 / 256, EPS, ALU.mult, ALU.add))
            kid1 = kid[:, :, 0:HD]
            sq1 = sq[:, 0:256].rearrange("p (t n) -> p t n", t=NT)
            link(tt(sq1, kid1, kid1, ALU.mult))
            link(nc.vector.tensor_reduce(qss[:, 4:8], sq1, X, ALU.add))
            ts(qss[:, 4:8], qss[:, 4:8], 1.0 / HD, EPS, ALU.mult, ALU.add).then_inc(head_mean, 1)
            tt(sp_part(0).rearrange("p (t n) -> p t n", t=NT), wb[:, :, 8:16],
               prm("forget_b").unsqueeze(1).broadcast_to([P, NT, 8]), ALU.add).then_inc(forget_z, 1)
            link(ts(wb[:, :, 0:8], wb[:, :, 0:8], 8 ** -0.5 * 64 ** -0.5))
            dve.wait_ge(head_root, 2)
            link(nc.vector.reciprocal(qss[:, 0:8], qss[:, 0:8]))
            link(tt(ckv, ckv, qss[:, 0:4].unsqueeze(2).broadcast_to([P, NT, 256]), ALU.mult))
            link(tt(ckv, ckv, prm("ckv_gain").unsqueeze(1).broadcast_to([P, NT, 256]), ALU.mult))
            link(tt(kid1, kid1, qss[:, 4:8].unsqueeze(2).broadcast_to([P, NT, HD]), ALU.mult))
            link(tt(kid1, kid1, prm("kidx_gain").unsqueeze(1).broadcast_to([P, NT, HD]), ALU.mult))
            rope(kid1.unsqueeze(2), 1, temps)
            rope(krd[:, :, 0:HD].unsqueeze(2), 1, temps)
            nc.vector.tensor_copy(kid[:, :, HD:P], kid1)
            nc.vector.tensor_copy(krd[:, :, HD:HD + 2 * ROT], krd[:, :, 0:2 * ROT])
            for half in range(2):
                for t in range(NT):
                    n = JOBS["aq"] + NT * half + t
                    ts(tok[:, t, 256 * half:256 * (half + 1)], evac_to(n)[:, 0:256], SCALE).then_inc(proj_evacuated[n % 2], 1)
            copied_all(dve, "ai", 2 * NT)
            rope(tok[:, :, 512:1024].rearrange("p t (h d) -> p t h d", d=HD), 8, temps)
            copied_all(dve, "aq", 2 * NT)
            rope(tok[:, :, 0:512].rearrange("p t (h d) -> p t h d", d=HD), 8, temps)
            dve.wait_ge(forget_ln, 1)
            link(ts(sp_part(0), sp_part(0), -1.0, 0.0, ALU.mult, ALU.max))
            tt(sp_part(2), sp_part(0), sp_part(1), ALU.add).then_inc(heads_ready, 1)
            for j in range(4):
                n = JOBS["kh"] + j
                tt(khT[:, j, :], evac_to(n)[:, :], krT, ALU.add).then_inc(proj_evacuated[n % 2], 1)
            for c in range(8 * (NT - 1)):
                t, h = c // 8 + 1, c % 8
                copied(dve, JOBS["index"] + c)
                if c >= 1:
                    dve.wait_ge(relu_used, c)
                nc.vector.scalar_tensor_tensor(out=sel[t], in0=S[c % 2][:, 0:(t + 1) * P], scalar=wb[:, t, h:h + 1],
                                               in1=cmask(t) if h == 0 else sel[t], op0=ALU.mult, op1=ALU.add)\
                    .then_inc(relu_used, 1)
            dve.wait_ge(relu_used, 8 * (NT - 1))
            top8 = small[:, 288:296]

            def take(t, n):
                if n % 2 == 0:
                    link(nc.vector.max(top8, sel[t]))
                else:
                    link(nc.vector.match_replace(sel[t], top8, sel[t], TAKEN))
                if n == KEEP // 4 - 1:
                    link(ts(sel[t], sel[t], 0.7 * TAKEN, NEG, ALU.is_gt, ALU.mult))

            for t in range(1, NT - 1):
                for n in range(KEEP // 4):
                    take(t, n)
            attention(first_fox, first_nsa - first_fox,
                      lambda i: take(NT - 1, i) if i < KEEP // 4 else None)
            out_projection(1, "ao")
            mlp(0)

            copied_all(dve, "nv", 2 * NT)
            tt(gate2, gate2, prm("gate_b").unsqueeze(1).broadcast_to([P, NT, 48]), ALU.add).then_inc(gate_ready, 1)
            temps = scr.rearrange("p a n -> p (a n)")
            copied_all(dve, "nk", 2 * NT)
            for col in (0, 256, 512):
                rope(kv2[:, :, col:col + P].rearrange("p t (h d) -> p t h d", d=HD), 2, temps,
                     heads_ready if col == 512 else None)
            for c in range(4):
                for t in range(NT):
                    n = JOBS["nq"] + NT * c + t
                    ts(tok[:, t, :].rearrange("p (j g d) -> p j g d", g=2, d=HD)[:, 4 * (c % 2):4 * (c % 2) + 4, c // 2, :],
                       evac_to(n)[:, 0:256].rearrange("p (j d) -> p j d", d=HD), SCALE).then_inc(proj_evacuated[n % 2], 1)
                if c % 2 == 1:
                    copied_all(dve, "nq", NT * (c + 1))
                    dve.wait_ge(heads_ready, 3 + c // 2)
                    rope(tok.rearrange("p t (j g d) -> p t j g d", g=2, d=HD)[:, :, :, c // 2, :], 8, temps, heads_ready)

            def compress(step):
                if step == CMP_TURN - 1:
                    for g in range(2):
                        shifted(JOBS["cmp"] + 2 + g, win[:, 1, g, :], nc.vector.tensor_copy, dve)
                elif step == CMP_FIRST + 3:
                    dve.wait_ge(cmp_zeroed, 4)
                    for s in range(2):
                        n = JOBS["cmp"] + 5 + s
                        o = evac_to(n)
                        nc.vector.tensor_copy(small[:, 304 + s:305 + s], o[:, 2 * N_CMP:2 * N_CMP + 1])
                        nc.vector.tensor_copy(chid[:, s, :].rearrange("p (g n) -> p g n", g=2)[:, :, 0:N_CMP],
                                              o[:, 0:2 * N_CMP].rearrange("p (g n) -> p g n", g=2))\
                            .then_inc(proj_evacuated[n % 2], 1)
                elif step == CMP_FIRST + 5:
                    copied_all(dve, "cmp", 7)
                    for s in range(2):
                        windows = chid[:, s, :].rearrange("p (g n) -> p g n", g=2)[:, :, 0:N_CMP]
                        link(ts(windows, windows, small[:, 304 + s:305 + s], None, ALU.add))
                elif step == CMP_FIRST + 7:
                    link(tt(cpart(1), cpart(0), cpart(0), ALU.mult))
                    link(ts(cpart(1), cpart(1), 0.044715, 1.0, ALU.mult, ALU.add))
                    link(tt(cpart(1), cpart(1), cpart(0), ALU.mult))
                    ts(cpart(1), cpart(1), -40 / GELU_C, None, ALU.max).then_inc(gelu_in, 1)
                elif step == CMP_FIRST + 10:
                    dve.wait_ge(gelu_exp, 1)
                    link(ts(cpart(2), cpart(2), 1.0, None, ALU.add))
                    link(nc.vector.reciprocal(cpart(2), cpart(2)))
                    tt(cpart(3), cpart(2), cpart(0), ALU.mult).then_inc(gelu_out, 1)
                elif step == CMP_SECOND + 2:
                    n = JOBS["cmp"] + 8
                    o = evac_to(n)
                    for q in range(4):
                        last = nc.vector.tensor_copy(vcBD[32 * q:32 * q + 32, HD * q:HD * q + HD],
                                                     o[32 * q:32 * q + 32, HD * (q % 2):HD * (q % 2) + HD])
                    last.then_inc(proj_evacuated[n % 2], 1)

            dve.wait_ge(gate_ready, 2)
            attention(first_nsa, n_items - first_nsa, compress)
            out_projection(2, "no")
            mlp(1)


_INS = ["x", "norm1_g", "w_in", "q_norm_g", "k_norm_g", "attn_sink", "conv_w", "conv_b", "w_attn_proj", "w_conv_proj",
        "w_out", "norm2_g", "w_router_group", "b_router_group", "w_router_expert", "b_router_expert", "w_gate_e",
        "w_up_e", "w_down_e", "attn_norm_2", "mlp_norm_2", "mlp_w1_2", "mlp_w2_2", "ab_w_in_2", "ab_b_forget_2",
        "a_kv_norm_2", "a_w_uk_2", "a_w_uv_2", "a_kidx_norm_2", "ab_w_out_2", "c_w_in_2", "c_b_gate_2", "c_pe_k_2",
        "c_pe_v_2", "c_cmp_k_w1_2", "c_cmp_k_w2_2", "c_cmp_v_w1_2", "c_cmp_v_w2_2", "c_w_out_2", "final_norm_2"]


def kernel(**inputs):
    import numpy as _np
    import concourse.bacc as _bacc
    from concourse import mybir as _mybir
    from concourse.bass_utils import run_bass_kernel_spmd as _run

    nc = _bacc.Bacc("TRN2", target_bir_lowering=False, num_devices=1)
    arrays, w = {}, {}
    for name in _INS:
        a = _np.ascontiguousarray(inputs[name])
        arrays[f"in_{name}"] = a
        w[name] = nc.dram_tensor(f"in_{name}", a.shape, _mybir.dt.float32, kind="ExternalInput").ap()
    arrays["in_constants"] = constants()
    w["constants"] = nc.dram_tensor("in_constants", (P, NCONST), _mybir.dt.float32, kind="ExternalInput").ap()
    out = nc.dram_tensor("out_x", (1, T, D), _mybir.dt.float32, kind="ExternalOutput").ap()
    build(nc, w, out)
    r = _run(nc, [arrays], core_ids=[0])
    return r.results[0]["out_x"]
```
